# Optimizing a Trainium2 kernel written in Bass

```python
import math
import jax, jax.numpy as jnp
from jax import lax
import numpy as np

D_MODEL = 2048
BATCH = 1
SEQ = 256
DEPTH = 2

N_EVEN = (DEPTH + 1) // 2
N_ODD = DEPTH // 2

H_A = 8
DA = 64
W_A_QK = H_A * 2 * DA
W_A_V = H_A * 2 * DA
Q_BLOCK = 128

H_B = 8
DK_B = 128
DV_B = 128
W_B = H_B * DK_B
CHUNK = 64

AB_SIZES = (W_A_QK, W_A_QK, W_A_V, W_B, H_B * DV_B, H_B * DV_B, W_B, W_B)
AB_IN = sum(AB_SIZES)
AB_MIX = W_A_V + H_B * DV_B

CONV_W = 3

D_FF = 4 * D_MODEL

EPS = 1e-6

kernel_name = "hybrid_diffattn_hgrn2_shortconv_encoder"

def rms_norm(x, g):
    xf = x.astype(jnp.float32)
    y = xf * lax.rsqrt(jnp.mean(xf * xf, axis=-1, keepdims=True) + EPS)
    return (y * g.astype(jnp.float32)).astype(x.dtype)

def alibi_slopes(n_heads):
    return 2.0 ** (-8.0 * jnp.arange(1, n_heads + 1, dtype=jnp.float32) / n_heads)

def diff_attention(q, k, v, lam, slopes):
    B, H, _, T, d = q.shape
    nb = T // Q_BLOCK
    q_blocks = jnp.moveaxis(q.reshape(B, H, 2, nb, Q_BLOCK, d), 3, 0)
    starts = jnp.arange(nb, dtype=jnp.int32) * Q_BLOCK
    k_pos = jnp.arange(T, dtype=jnp.int32)
    scale = d ** -0.5

    def block(args):
        q_blk, start = args
        s = jnp.einsum('bhmqd,bhmkd->bhmqk', q_blk, k).astype(jnp.float32) * scale
        q_pos = start + jnp.arange(Q_BLOCK, dtype=jnp.int32)
        dist = jnp.abs(q_pos[:, None] - k_pos[None, :]).astype(jnp.float32)
        s = s - slopes[None, :, None, None, None] * dist
        p = jax.nn.softmax(s, axis=-1)
        a = p[:, :, 0] - lam.astype(jnp.float32) * p[:, :, 1]
        return jnp.einsum('bhqk,bhkv->bhqv', a.astype(v.dtype), v)

    o = lax.map(block, (q_blocks, starts))
    return jnp.moveaxis(o, 0, 2).reshape(B, H, T, v.shape[-1])

def hgrn2_scan(q, k, v, log_f):
    B, H, T, dk = q.shape
    dv = v.shape[-1]
    n = T // CHUNK

    def to_chunks(a):
        return jnp.moveaxis(a.reshape(B, H, n, CHUNK, a.shape[-1]), 2, 0)

    mask = jnp.tril(jnp.ones((CHUNK, CHUNK), dtype=bool))[:, :, None]

    def step(S, inp):
        qc, kc, vc, gc = inp
        b = jnp.cumsum(gc, axis=2)
        inter = jnp.einsum('bhtk,bhkv->bhtv', qc * jnp.exp(b), S)
        rel = b[:, :, :, None, :] - b[:, :, None, :, :]
        decay = jnp.where(mask, jnp.exp(jnp.where(mask, rel, 0.0)), 0.0)
        att = jnp.einsum('bhtk,bhtsk,bhsk->bhts', qc, decay, kc)
        intra = jnp.einsum('bhts,bhsv->bhtv', att, vc)
        b_last = b[:, :, -1:, :]
        S_new = jnp.exp(b_last[:, :, 0, :, None]) * S + jnp.einsum(
            'bhsk,bhsv->bhkv', kc * jnp.exp(b_last - b), vc)
        return S_new, inter + intra

    S0 = jnp.zeros((B, H, dk, dv), jnp.float32)
    _, o = lax.scan(step, S0, (to_chunks(q), to_chunks(k), to_chunks(v), to_chunks(log_f)))
    return jnp.moveaxis(o, 0, 2).reshape(B, H, T, dv)

def diff_hgrn_mixer(xn, w_in, w_out, lam_p, subln_g, lb_table, hgrn_g, layer):
    B, T, _ = xn.shape
    proj = xn @ w_in
    idx = np.cumsum(AB_SIZES)[:-1].tolist()
    q, k, v, hq, hi, hg, hf_fwd, hf_bwd = jnp.split(proj, idx, axis=-1)

    qa = q.reshape(B, T, H_A, 2, DA).transpose(0, 2, 3, 1, 4)
    ka = k.reshape(B, T, H_A, 2, DA).transpose(0, 2, 3, 1, 4)
    va = v.reshape(B, T, H_A, 2 * DA).transpose(0, 2, 1, 3)
    lam_init = 0.8 - 0.6 * math.exp(-0.3 * layer)
    lp = lam_p.astype(jnp.float32)
    lam = jnp.exp(jnp.sum(lp[0] * lp[1])) - jnp.exp(jnp.sum(lp[2] * lp[3])) + lam_init
    oa = diff_attention(qa, ka, va, lam, alibi_slopes(H_A))
    oa = rms_norm(oa, subln_g) * (1.0 - lam_init)
    oa = oa.transpose(0, 2, 1, 3).reshape(B, T, W_A_V)

    lb = jnp.cumsum(jax.nn.softmax(lb_table.astype(jnp.float32), axis=1), axis=1)[:, layer]

    def heads(a):
        return a.astype(jnp.float32).reshape(B, T, H_B, -1).transpose(0, 2, 1, 3)

    def gates(z, lb_d):
        zf = z.astype(jnp.float32)
        f = lb_d + (1.0 - lb_d) * jax.nn.sigmoid(zf)
        k_in = (1.0 - lb_d) * jax.nn.sigmoid(-zf)
        return heads(k_in), heads(jnp.log(f))

    qh, vh = heads(hq), heads(hi)
    k_f, g_f = gates(hf_fwd, lb[0])
    k_b, g_b = gates(hf_bwd, lb[1])
    flip = lambda a: jnp.flip(a, axis=2)
    ob = hgrn2_scan(qh, k_f, vh, g_f) + flip(hgrn2_scan(flip(qh), flip(k_b), flip(vh), flip(g_b)))
    ob = rms_norm(ob, hgrn_g.reshape(H_B, 1, DV_B))
    ob = ob.transpose(0, 2, 1, 3).reshape(B, T, H_B * DV_B).astype(xn.dtype)
    ob = ob * jax.nn.silu(hg)

    return jnp.concatenate([oa, ob], axis=-1) @ w_out

def short_conv_mixer(xn, w_in, conv_w, w_out):
    b_gate, c_gate, h = jnp.split(xn @ w_in, 3, axis=-1)
    u = c_gate * h
    conv = lax.conv_general_dilated(
        u, conv_w[:, None, :], window_strides=(1,), padding=[(1, 1)],
        dimension_numbers=('NWC', 'WIO', 'NWC'), feature_group_count=u.shape[-1])
    return (b_gate * conv) @ w_out

def sq_relu_mlp(xn, w_up, w_down):
    return jnp.square(jax.nn.relu(xn @ w_up)) @ w_down

def setup_inputs(seed: int = 0) -> dict:
    key = jax.random.key(seed)
    ks = jax.random.split(key, 16)
    nrm = lambda k, shape, scale: jax.random.normal(k, shape, jnp.float32) * scale
    return {
        "x": nrm(ks[0], (BATCH, SEQ, D_MODEL), 1.0),
        "mix_norm_g": 1.0 + nrm(ks[1], (DEPTH, D_MODEL), 0.02),
        "mlp_norm_g": 1.0 + nrm(ks[2], (DEPTH, D_MODEL), 0.02),
        "final_norm_g": 1.0 + nrm(ks[3], (D_MODEL,), 0.02),
        "ab_w_in": nrm(ks[4], (N_EVEN, D_MODEL, AB_IN), D_MODEL ** -0.5),
        "ab_w_out": nrm(ks[5], (N_EVEN, AB_MIX, D_MODEL), AB_MIX ** -0.5),
        "diff_lambda": nrm(ks[6], (N_EVEN, 4, DA), 0.1),
        "diff_subln_g": 1.0 + nrm(ks[7], (N_EVEN, 2 * DA), 0.02),
        "hgrn_lb": nrm(ks[8], (2, DEPTH + 1, W_B), 0.1),
        "hgrn_norm_g": 1.0 + nrm(ks[9], (N_EVEN, H_B * DV_B), 0.02),
        "conv_w_in": nrm(ks[10], (N_ODD, D_MODEL, 3 * D_MODEL), D_MODEL ** -0.5),
        "conv_w": nrm(ks[11], (N_ODD, CONV_W, D_MODEL), CONV_W ** -0.5),
        "conv_w_out": nrm(ks[12], (N_ODD, D_MODEL, D_MODEL), D_MODEL ** -0.5),
        "mlp_w_up": nrm(ks[13], (DEPTH, D_MODEL, D_FF), D_MODEL ** -0.5),
        "mlp_w_down": nrm(ks[14], (DEPTH, D_FF, D_MODEL), D_FF ** -0.5),
    }

def reference(x, mix_norm_g, mlp_norm_g, final_norm_g, ab_w_in, ab_w_out, diff_lambda,
              diff_subln_g, hgrn_lb, hgrn_norm_g, conv_w_in, conv_w, conv_w_out,
              mlp_w_up, mlp_w_down):
    h = x
    for l in range(DEPTH):
        j = l // 2
        hn = rms_norm(h, mix_norm_g[l])
        if l % 2 == 0:
            h = h + diff_hgrn_mixer(hn, ab_w_in[j], ab_w_out[j], diff_lambda[j],
                                    diff_subln_g[j], hgrn_lb, hgrn_norm_g[j], l)
        else:
            h = h + short_conv_mixer(hn, conv_w_in[j], conv_w[j], conv_w_out[j])
        hn = rms_norm(h, mlp_norm_g[l])
        h = h + sq_relu_mlp(hn, mlp_w_up[l], mlp_w_down[l])
    return rms_norm(h, final_norm_g)


_drawn_inputs = setup_inputs


def setup_inputs(seed=0):
    import zlib

    import numpy as np

    out = dict(_drawn_inputs(seed))
    spreads = {}
    factors = {}
    for name, (base, spread) in spreads.items():
        noise = np.random.default_rng([zlib.crc32(name.encode()), seed]).standard_normal(out[name].shape)
        drawn = base * np.exp(spread * noise) if base else spread * noise
        out[name] = __import__('jax').numpy.asarray(drawn.astype(out[name].dtype))
    for name, factor in factors.items():
        out[name] = (out[name] * factor).astype(out[name].dtype)
    return out
```

```python
from contextlib import ExitStack

import concourse.bass as bass
import numpy as np
from concourse import mybir

F32 = mybir.dt.float32
F32R = mybir.dt.float32r
U32 = mybir.dt.uint32
ALU = mybir.AluOpType
ACT = mybir.ActivationFunctionType
AX_X = mybir.AxisListType.X

P = 128
T = 256
NT = T // P
D = 2048
KT = D // P
CB = D // 512
FF = 4 * D
HEADS = 8
DA = 64
EPS = 1e-6
LAM_INIT = 0.8 - 0.6 * 1.0
RAW = 4
HALVES = 4
LEVELS = [1, 2, 4, 8, 16, 32, 64, 128]

PROJ_AT = 0
OUT_AT = PROJ_AT + HEADS * 8
MLP_SLOTS = (FF // 512) * 8
MLP0_AT = OUT_AT + 16
CONV_AT = MLP0_AT + MLP_SLOTS
CONV_SLOTS = CB * 16
MLP1_AT = CONV_AT + CONV_SLOTS
TOTAL = MLP1_AT + MLP_SLOTS

PAIR_L0 = HEADS + CB // 2
PAIR_MLP0 = PAIR_L0 + (FF // 512) * CB // 2
PAIR_CONV = PAIR_MLP0 + CB * (1 + CB // 2)
PAIR_MLP1 = PAIR_CONV + (FF // 512) * CB // 2

CONV_STEPS = 4
CONST_ALL = 11 + 2 * 2 * 7
PAR_LB = 11
ROWS_DMAS = 6

G_MIX, G_MLP, G_CONV, G_HGRN, G_SUB = 0, 32, 64, 112, 120

OUT_ORDER = [(0, 0), (0, 1), (0, 2), (1, 0), (1, 1), (1, 2), (0, 3), (1, 3)] + [
    (cb, j) for cb in (2, 3) for j in range(4)]


class Steps:

    def __init__(self, sem, names):
        self.sem, self.names = sem, names

    def at(self, name, n):
        return n * len(self.names) + (self.names.index(name) + 1)


def build(nc, x, mix_norm_g, mlp_norm_g, final_norm_g, ab_w_in, ab_w_out, diff_lambda, diff_subln_g,
          hgrn_lb, hgrn_norm_g, conv_w_in, conv_w, conv_w_out, mlp_w_up, mlp_w_down, out):
    with ExitStack() as ctx:
        def sb(name, shape, dt=F32):
            return ctx.enter_context(nc.sbuf_tensor(name, shape, dt))

        def pb(name, shape, dt=F32):
            return ctx.enter_context(nc.psum_tensor(name, shape, dt))

        def sem(name):
            return ctx.enter_context(nc.semaphore(name))

        raw = sb("raw", [P, RAW, 4, 512])
        w_hi = sb("w_hi", [P, HALVES, 2, 512], F32R)
        w_lo = sb("w_lo", [P, HALVES, 2, 512], F32R)
        h = sb("h", [P, NT, D])
        xT_hi = sb("xT_hi", [P, KT, T], F32R)
        xT_lo = sb("xT_lo", [P, KT, T], F32R)
        yT_hi = sb("yT_hi", [P, KT, T], F32R)
        yT_lo = sb("yT_lo", [P, KT, T], F32R)
        ident = sb("ident", [P, P])
        rows_a = sb("rows_a", [P, P])
        rows_b = sb("rows_b", [48, P])
        gains = sb("gains", [P, P])
        lbt = sb("lbt", [P, 2, 3, HEADS])
        lbm = sb("lbm", [P, 2, HEADS])
        lbs = sb("lbs", [P, 2, HEADS])
        lb = sb("lb", [P, HEADS, 2])
        one_lb = sb("one_lb", [P, HEADS, 2])
        lam4 = sb("lam4", [P, 4, DA])
        lam_sum = sb("lam_sum", [P, 2])
        neg_lam = sb("neg_lam", [P, 1])
        sumsq = sb("sumsq", [P, NT, CB])
        meansq = sb("meansq", [P, NT])
        rstd = sb("rstd", [P, 5, NT])
        minus_half = sb("minus_half", [P, 4])
        mask = sb("mask", [P, 2, 7, 64])
        bias = sb("bias", [P, NT, T])
        proj_a = sb("proj_a", [P, NT, 4, P])
        proj_b = sb("proj_b", [P, NT, 4, P])
        qkT = sb("qkT", [P, 2, T])
        hqT = sb("hqT", [P, T])
        gate = sb("gate", [P, 2, T])
        kin = sb("kin", [P, 2, T])
        kin_sum = sb("kin_sum", [P, T])
        silu = sb("silu", [P, NT, P])
        even = sb("even", [P, 2, 512])
        odd = sb("odd", [P, 2, 512])
        lq = sb("lq", [P, 8, T])
        lk = sb("lk", [P, 7, T])
        sm = sb("sm", [P, NT, 2, T])
        aT = sb("aT", [P, NT, T])
        att = sb("att", [P, NT, 2, P])
        on = sb("on", [P, 4, P])
        mx = sb("mx", [P, 4])
        neg_mx = sb("neg_mx", [P, 4])
        rowsum = sb("rowsum", [P, 4])
        rinv = sb("rinv", [P, 4])
        neg_lr = sb("neg_lr", [P, NT])
        osq = sb("osq", [P, 4])
        orstd = sb("orstd", [P, 4])
        act = sm[:, :, :, :].rearrange("p a b c -> p a (b c)")
        junk = lq[:, 0:2, :].rearrange("p a b -> p (a b)")
        cg = proj_a[:, :, :, :].rearrange("p a b c -> p a (b c)")
        bg = proj_b[:, :, :, :].rearrange("p a b c -> p a (b c)")
        uT = lk[:, 0:4, :]
        cT = lq[:, 4:8, :]

        pair = [pb(f"pair{i}", [P, NT, 512]) for i in range(2)]
        m01 = pb("m01", [P, 2, 512])
        m23 = pb("m23", [P, 2, 512])
        M = [m01[:, 0], m01[:, 1], m23[:, 0], m23[:, 1]]

        landed = [sem(f"landed{i}") for i in range(RAW)]
        hi_ready = sem("hi_ready")
        lo_ready = sem("lo_ready")
        w_used = sem("w_used")
        x_in = [sem(f"x_in{i}") for i in range(CB)]
        rows_in = sem("rows_in")
        lam_in = sem("lam_in")
        const_pool = sem("const_pool")
        rows_T = sem("rows_T")
        par_dve = sem("par_dve")
        par_act = sem("par_act")
        pair_read = [sem(f"pair_read{i}") for i in range(2)]
        norm_T = [sem(f"norm_T{i}") for i in range(4)]
        norm_hi = [sem(f"norm_hi{i}") for i in range(4)]
        norm_lo = [sem(f"norm_lo{i}") for i in range(4)]
        sq_done = sem("sq_done")
        sq_sum = sem("sq_sum")
        rstd_step = sem("rstd_step")
        up_relu = [sem(f"up_relu{i}") for i in range(2)]
        up_sq = [sem(f"up_sq{i}") for i in range(2)]
        hT_done = [sem(f"hT_done{i}") for i in range(2)]
        hT_hi = [sem(f"hT_hi{i}") for i in range(2)]
        hT_lo = [sem(f"hT_lo{i}") for i in range(2)]
        waited = sem("waited")
        picked = sem("picked")
        b_read = sem("b_read")
        uT_done, uT_read = sem("uT_done"), sem("uT_read")
        bT_done = sem("bT_done")
        cv_step = sem("cv_step")
        cv_hi, cv_lo = sem("cv_hi"), sem("cv_lo")
        fin_rows = sem("fin_rows")
        fin_ready = sem("fin_ready")
        stored = sem("stored")

        mix_pe = Steps(sem("mix_pe"), ["qkT", "hqT", "gateT", "S0", "S1", "diag", "F0", "F1", "B0",
                                       "aT", "B1", "oAB", "oT"])
        mix_act = Steps(sem("mix_act"), ["qkT", "hqT", "exp_neg", "exp_pos", "exp_hg", "exp_s",
                                         "aT", "osq", "hi_a", "hi_b"])
        mix_dve = Steps(sem("mix_dve"), ["f_inv", "k_inv", "f", "silu_inv", "s", "max"]
                        + [f"QF{m}" for m in LEVELS[:4]]
                        + ["diag", "r_inv", "neg_lr", "a1", "a", "PF0"]
                        + [f"QF{m}" for m in LEVELS[4:]]
                        + ["PF1"] + [f"QB{m}" for m in LEVELS[:4]]
                        + ["PB0"] + [f"QB{m}" for m in LEVELS[4:]]
                        + ["PB1", "on", "lo"])
        mix_pool = Steps(sem("mix_pool"), ["f_add", "k_add", "silu_add", "kin", "kin_sum"]
                         + [f"tree{m}" for m in LEVELS[:7]] + [f"KF{m}" for m in LEVELS[1:4]]
                         + ["neg_mx", "silu"] + [f"KF{m}" for m in LEVELS[4:]]
                         + [f"KB{m}" for m in LEVELS[1:]] + ["bias", "o_ms", "o_rstd"])

        def flat(tile, d, lv):
            at = 512 - (512 >> lv)
            return tile[:, d, at:at + (256 >> lv)]

        def row(tile, at):
            return tile[:, at] if isinstance(at, int) else tile[:, bass.ds(at, 1), :].rearrange(
                "p a b -> p (a b)")

        def out_gain(g, n):
            if g == 0:
                return gains[:, G_SUB:G_SUB + 1]
            return gains[:, G_HGRN + n:G_HGRN + n + 1] if isinstance(n, int) else \
                gains[:, bass.ds(n + G_HGRN, 1)]

        def lb_col(tile, n, d):
            return tile[:, n, d:d + 1] if isinstance(n, int) else \
                tile[:, bass.ds(n, 1), d:d + 1].rearrange("p a b -> p (a b)")

        ab_in = ab_w_in[0].rearrange("(kt p) (g h n) -> p kt g h n", p=P, g=8, h=HEADS)
        ab_out = ab_w_out[0].rearrange("(g h p) n -> p h g n", g=2, p=P)
        up_src = [mlp_w_up[i].rearrange("(kt p) n -> p kt n", p=P) for i in range(2)]
        down_src = [mlp_w_down[i].rearrange("(kt p) n -> p kt n", p=P) for i in range(2)]
        cin = conv_w_in[0].rearrange("(kt p) n -> p kt n", p=P)
        cout = conv_w_out[0].rearrange("(kt p) n -> p kt n", p=P)

        def count(scale, const, base, step, i):
            if isinstance(i, int):
                return scale * (base + step * i) + const
            return i * (scale * step) + (scale * base + const)

        def stand_alone(eng, n):
            if not isinstance(n, int):
                eng.sem_inc(waited, 1)

        def load(sp, base, step, i, src, pieces=1):
            slot = base % RAW
            if base >= RAW:
                sp.wait_ge(lo_ready, count(2, 2 - 2 * RAW, base, step, i))
            if pieces == 1:
                sp.dma_start(raw[:, slot], src).then_inc(landed[slot], 16)
                return
            for q in range(pieces):
                sp.dma_start(raw[:, slot, q], src(q)).then_inc(landed[slot], 16)

        def landed_at(base, step, i):
            each, before = (64, 0) if base < MLP0_AT else (16, 48 * (MLP0_AT // RAW))
            uses = base // RAW + 1
            return i * (each * step // RAW) + (each * uses + before)

        def split_hi(eng, base, step, i):
            if base >= TOTAL:
                return
            slot = base % RAW
            eng.wait_ge(landed[slot], landed_at(base, step, i))
            for k in range(2):
                ring = (2 * base + k) % HALVES
                if 2 * base + k >= HALVES:
                    eng.wait_ge(w_used, count(2, k + 1 - HALVES, base, step, i))
                nc.scalar.activation(w_hi[:, ring], raw[:, slot, 2 * k:2 * k + 2], ACT.Copy
                                     ).then_inc(hi_ready, 1)

        def split_lo(eng, base, step, i):
            if base >= TOTAL:
                return
            slot = base % RAW
            for k in range(2):
                ring = (2 * base + k) % HALVES
                eng.wait_ge(hi_ready, count(2, k + 1, base, step, i))
                nc.vector.tensor_tensor(w_lo[:, ring], raw[:, slot, 2 * k:2 * k + 2],
                                        w_hi[:, ring].bitcast(F32), ALU.subtract
                                        ).then_inc(lo_ready, 1)

        def multiply(eng, base, step, i, hi, lo, kt0, dst, first, last):
            for k in range(2):
                ring = (2 * base + k) % HALVES
                eng.wait_ge(lo_ready, count(2, k + 1, base, step, i))
                for q in range(2):
                    kt = kt0 + 2 * k + q
                    begin, end = first and k == 0 and q == 0, last and k == 1 and q == 1
                    for tt in range(NT):
                        cols = slice(tt * P, (tt + 1) * P)
                        nc.tensor.matmul(dst[:, tt], hi[:, kt, cols], w_hi[:, ring, q],
                                         start=begin, stop=False)
                        nc.tensor.matmul(dst[:, tt], hi[:, kt, cols], w_lo[:, ring, q],
                                         start=False, stop=False)
                        mm = nc.tensor.matmul(dst[:, tt], lo[:, kt, cols], w_hi[:, ring, q],
                                              start=False, stop=end)
                mm.then_inc(w_used, 1)

        def wait_product(eng, base, step, i):
            eng.wait_ge(w_used, count(2, 2, base, step, i))

        block = ctx.enter_context(nc.Block())

        @block.sync
        def _(sp):
            def head_columns(c, j, at):
                return lambda q: ab_in[:, 4 * j + q, 4 * c:4 * c + 4, at, :]

            for p in range(8):
                load(sp, p, 0, 0, head_columns(p // 4, p % 4, 0), 4)
            with sp.Fori(0, HEADS - 1) as i:
                for p in range(8):
                    load(sp, 8 + p, 8, i,
                         lambda q: head_columns(p // 4, p % 4, bass.ds(i + 1, 1))(q)
                         .rearrange("p a b n -> p (a b) n"), 4)
            for n, (cb, j) in enumerate(OUT_ORDER):
                load(sp, OUT_AT + n, 0, 0,
                     lambda q: ab_out[:, 2 * j + q // 2, q % 2, cb * 512:(cb + 1) * 512], 4)

            def mlp(at, layer):
                for j in range(4):
                    load(sp, at + j, 0, 0, up_src[layer][:, 4 * j:4 * j + 4, 0:512])
                with sp.Fori(0, FF // 512 - 1) as i:
                    for j in range(4):
                        load(sp, at + 4 + j, 8, i,
                             up_src[layer][:, 4 * j:4 * j + 4, bass.ds(i * 512 + 512, 512)])
                    for cb in range(CB):
                        load(sp, at + 8 + cb, 8, i,
                             down_src[layer][:, bass.ds(i * 4, 4), cb * 512:(cb + 1) * 512])
                for cb in range(CB):
                    load(sp, at + MLP_SLOTS - 4 + cb, 0, 0,
                         down_src[layer][:, FF // P - 4:FF // P, cb * 512:(cb + 1) * 512])

            mlp(MLP0_AT, 0)
            for u, g in enumerate((1, 2, 0)):
                for j in range(4):
                    load(sp, CONV_AT + 4 * u + j, 0, 0,
                         cin[:, 4 * j:4 * j + 4, g * D:g * D + 512])
            with sp.Fori(0, CB - 1) as i:
                for u, g in ((0, 1), (1, 2)):
                    for j in range(4):
                        load(sp, CONV_AT + 12 + 4 * u + j, 16, i,
                             cin[:, 4 * j:4 * j + 4, bass.ds(i * 512 + (g * D + 512), 512)])
                for cb in range(CB):
                    load(sp, CONV_AT + 20 + cb, 16, i,
                         cout[:, bass.ds(i * 4, 4), cb * 512:(cb + 1) * 512])
                for j in range(4):
                    load(sp, CONV_AT + 24 + j, 16, i,
                         cin[:, 4 * j:4 * j + 4, bass.ds(i * 512 + 512, 512)])
            for cb in range(CB):
                load(sp, CONV_AT + CONV_SLOTS - 4 + cb, 0, 0,
                     cout[:, KT - 4:KT, cb * 512:(cb + 1) * 512])
            mlp(MLP1_AT, 1)
            sp.wait_ge(lo_ready, 2 * (TOTAL - 4) + 2)
            sp.dma_start(raw[:, 0], final_norm_g.rearrange("(a c n) -> a c n", a=1, n=512)
                         .broadcast_to([P, 4, 512])).then_inc(fin_rows, 16)
            for cb in range(CB):
                for tt in range(NT):
                    sp.wait_ge(fin_ready, cb * NT + tt + 1)
                    sp.dma_start(out[0, tt * P:(tt + 1) * P, cb * 512:(cb + 1) * 512],
                                 h[:, tt, cb * 512:(cb + 1) * 512]).then_inc(stored, 16)
            sp.wait_ge(stored, 16 * CB * NT)

        @block.gpsimd
        def _(pool):
            nc.gpsimd.memset(ident[:], 1.0).then_inc(const_pool, 1)
            pool.wait_ge(const_pool, 1)
            nc.gpsimd.affine_select(out=ident[:], in_=ident[:], compare_op=ALU.is_equal, fill=0.0,
                                    base=0, pattern=[[-1, P]], channel_multiplier=1
                                    ).then_inc(const_pool, 1)
            nc.gpsimd.memset(minus_half[:], -0.5).then_inc(const_pool, 1)
            nc.gpsimd.iota(sm[:, :, 0, :], pattern=[[P, NT], [-1, T]], base=0, channel_multiplier=1,
                           allow_small_or_imprecise_dtypes=True).then_inc(const_pool, 1)
            pool.wait_ge(const_pool, 4)
            nc.gpsimd.tensor_scalar(sm[:, :, 1, :], sm[:, :, 0, :], 0.0, None, ALU.max
                                    ).then_inc(const_pool, 1)
            nc.gpsimd.tensor_scalar(bias[:], sm[:, :, 0, :], 0.0, None, ALU.min
                                    ).then_inc(const_pool, 1)
            pool.wait_ge(const_pool, 6)
            nc.gpsimd.tensor_tensor(bias[:], bias[:], sm[:, :, 1, :], ALU.subtract
                                    ).then_inc(const_pool, 1)
            pool.wait_ge(const_pool, 7)
            nc.gpsimd.tensor_scalar(bias[:], bias[:], 0.5, None, ALU.mult).then_inc(const_pool, 1)
            nc.gpsimd.memset(even[:], 1.0).then_inc(const_pool, 1)
            nc.gpsimd.memset(odd[:], 1.0).then_inc(const_pool, 1)
            nc.gpsimd.memset(mask[:], 1.0).then_inc(const_pool, 1)
            done = 11
            pool.wait_ge(const_pool, done)

            def rstd_of(n):
                pool.wait_ge(sq_sum, n + 1)
                nc.gpsimd.tensor_scalar(meansq[:], meansq[:], 1.0 / D, EPS, ALU.mult, ALU.add
                                        ).then_inc(rstd_step, 1)
                pool.wait_ge(rstd_step, 2 * n + 1)
                nc.gpsimd.tensor_tensor(rstd[:, n], meansq[:], minus_half[:, 0:NT], ALU.pow
                                        ).then_inc(rstd_step, 1)

            rstd_of(0)
            for d in range(2):
                for lv in range(7):
                    m = LEVELS[lv]
                    part = mask[:, d, lv].rearrange("p (a b) -> p a b", b=m)
                    lo = m * d
                    nc.gpsimd.affine_select(out=part, in_=part, compare_op=ALU.is_ge, fill=0.0,
                                            base=-lo, pattern=[[-2 * m, 64 // m], [0, m]],
                                            channel_multiplier=1).then_inc(const_pool, 1)
                    done += 1
                    pool.wait_ge(const_pool, done)
                    nc.gpsimd.affine_select(out=part, in_=part, compare_op=ALU.is_ge, fill=0.0,
                                            base=lo + m - 1, pattern=[[2 * m, 64 // m], [0, m]],
                                            channel_multiplier=-1).then_inc(const_pool, 1)
                    done += 1

            def both(tile, lv):
                at = 512 - (512 >> lv)
                return tile[:, :, at:at + (256 >> lv)].rearrange("p d (a b) -> p d a b", b=2)

            assert done == CONST_ALL

            def mix(n):
                def mark(ins, name):
                    assert mix_pool.names[marks[0]] == name
                    marks[0] += 1
                    ins.then_inc(mix_pool.sem, 1)

                marks = [0]

                def own(name):
                    pool.wait_ge(mix_pool.sem, mix_pool.at(name, n))

                pool.wait_ge(mix_act.sem, mix_act.at("exp_neg", n))
                stand_alone(pool, n)
                mark(nc.gpsimd.tensor_scalar(gate[:], gate[:], 1.0, None, ALU.add), "f_add")
                pool.wait_ge(mix_act.sem, mix_act.at("exp_pos", n))
                stand_alone(pool, n)
                mark(nc.gpsimd.tensor_scalar(kin[:], kin[:], 1.0, None, ALU.add), "k_add")
                pool.wait_ge(mix_act.sem, mix_act.at("exp_hg", n))
                stand_alone(pool, n)
                mark(nc.gpsimd.tensor_scalar(silu[:], silu[:], 1.0, None, ALU.add), "silu_add")
                pool.wait_ge(mix_dve.sem, mix_dve.at("k_inv", n))
                scale = (one_lb[:, n] if isinstance(n, int) else
                         one_lb[:, bass.ds(n, 1), :].rearrange("p a b -> p (a b)"))
                mark(nc.gpsimd.tensor_tensor(kin[:], kin[:],
                                             scale.unsqueeze(2).broadcast_to([P, 2, T]), ALU.mult),
                     "kin")
                own("kin")
                mark(nc.gpsimd.tensor_tensor(kin_sum[:], kin[:, 0], kin[:, 1], ALU.add), "kin_sum")
                f_pairs = gate[:, :, :].rearrange("p d (a b) -> p d a b", b=2)
                pool.wait_ge(mix_dve.sem, mix_dve.at("f", n))
                stand_alone(pool, n)
                nc.gpsimd.tensor_copy(both(even, 0)[:, :, :, 1], f_pairs[:, :, :, 0])
                mark(nc.gpsimd.tensor_copy(both(odd, 0)[:, :, :, 0], f_pairs[:, :, :, 1]), "tree1")
                for lv in range(1, 7):
                    own(f"tree{LEVELS[lv - 1]}")
                    first, second = both(even, lv - 1)[:, :, :, 1], both(odd, lv - 1)[:, :, :, 0]
                    nc.gpsimd.tensor_tensor(both(even, lv)[:, :, :, 1], first[:, :, 0::2],
                                            second[:, :, 0::2], ALU.mult)
                    mark(nc.gpsimd.tensor_tensor(both(odd, lv)[:, :, :, 0], first[:, :, 1::2],
                                                 second[:, :, 1::2], ALU.mult), f"tree{LEVELS[lv]}")

                def k_level(d, lv):
                    m = LEVELS[lv - 1]
                    src = kin[:, d] if lv == 1 else lk[:, lv - 2]
                    factor = flat(odd if d == 0 else even, d, lv - 1)
                    mark(nc.gpsimd.tensor_tensor(
                        lk[:, lv - 1].rearrange("p (a b) -> p a b", b=m),
                        src.rearrange("p (a b) -> p a b", b=m),
                        factor.unsqueeze(2).broadcast_to([P, T // m, m]), ALU.mult),
                        f"K{'FB'[d]}{LEVELS[lv]}")

                for lv in range(1, 8):
                    if lv == 4:
                        pool.wait_ge(mix_dve.sem, mix_dve.at("max", n))
                        stand_alone(pool, n)
                        mark(nc.gpsimd.tensor_scalar(neg_mx[:], mx[:], -1.0, None, ALU.mult),
                             "neg_mx")
                        pool.wait_ge(mix_dve.sem, mix_dve.at("silu_inv", n))
                        mark(nc.gpsimd.tensor_tensor(silu[:], silu[:], proj_b[:, :, 1], ALU.mult),
                             "silu")
                    own("tree64" if lv == 1 else f"KF{LEVELS[lv - 1]}")
                    k_level(0, lv)
                for lv in range(1, 8):
                    if lv > 1:
                        own(f"KB{LEVELS[lv - 1]}")
                    pool.wait_ge(mix_pe.sem, mix_pe.at("F0" if lv < 4 else "F1", n))
                    k_level(1, lv)
                pool.wait_ge(mix_dve.sem, mix_dve.at("s", n))
                stand_alone(pool, n)
                mark(nc.gpsimd.tensor_scalar(bias[:], bias[:], 0.5, None, ALU.mult), "bias")
                pool.wait_ge(mix_act.sem, mix_act.at("osq", n))
                stand_alone(pool, n)
                mark(nc.gpsimd.tensor_scalar(osq[:], osq[:], 1.0 / P, EPS, ALU.mult, ALU.add),
                     "o_ms")
                own("o_ms")
                mark(nc.gpsimd.tensor_tensor(orstd[:], osq[:], minus_half[:], ALU.pow), "o_rstd")
                assert marks[0] == len(mix_pool.names)

            pool.wait_ge(const_pool, CONST_ALL)
            pool.wait_ge(par_dve, PAR_LB)
            with pool.Fori(0, HEADS - 1) as i:
                mix(i)
            mix(HEADS - 1)
            for n in range(1, 5):
                rstd_of(n)

        def gain_transpose_pe(n):
            for cb in range(CB):
                if n == 0:
                    nc.tensor.wait_ge(x_in[cb], 16)
                else:
                    last = {1: PAIR_L0, 2: PAIR_MLP0, 3: PAIR_CONV}[n]
                    nc.tensor.wait_ge(pair_read[cb % 2], last - 1 + cb // 2)
                for b in range(2):
                    bank = 2 * (cb % 2) + b
                    if cb >= 2:
                        nc.tensor.wait_ge(norm_lo[n], 2 * (cb - 2) + b + 1)
                    for q in range(2):
                        kt = 4 * cb + 2 * b + q
                        for tt in range(NT):
                            ins = nc.tensor.transpose(
                                M[bank][:, q * T + tt * P:q * T + (tt + 1) * P],
                                h[:, tt, kt * P:(kt + 1) * P], ident[:])
                    ins.then_inc(norm_T[n], 1)

        @block.tensor
        def _(pe):
            pe.wait_ge(const_pool, 2)
            pe.wait_ge(rows_in, 16 * ROWS_DMAS)
            nc.tensor.transpose(M[3][:, 0:121], rows_a[0:121, :], ident[0:121, 0:121])
            nc.tensor.transpose(M[3][:, 128:176], rows_b[:, :], ident[0:48, 0:48]
                                ).then_inc(rows_T, 1)
            pe.wait_ge(par_act, 1)
            gain_transpose_pe(0)

            def head_product(c, j, base, step, i, n):
                if j == 0 and not isinstance(n, int):
                    pe.wait_ge(pair_read[c], n)
                multiply(pe, base, step, i, xT_hi, xT_lo, 4 * j, pair[c], j == 0, j == 3)

            def hook(k, n):
                def mark(ins, name):
                    assert name in mix_pe.names
                    ins.then_inc(mix_pe.sem, 1)

                def levels(d, group):
                    bank = M[3] if group == 0 else M[2]
                    for g in range(4):
                        lv = 4 * group + g
                        m = LEVELS[lv]
                        keys = kin[:, d] if lv == 0 else lk[:, lv - 1]
                        if m == 128:
                            s_at, t_at = (0, P) if d == 0 else (P, 0)
                            ins = nc.tensor.matmul(bank[:, g * P:(g + 1) * P], keys[:, s_at:s_at + P],
                                                   lq[:, lv, t_at:t_at + P], start=True, stop=True)
                            continue
                        for tile in range(NT):
                            t_half = lq[:, lv, tile * P:(tile + 1) * P].rearrange(
                                "p (a b c) -> p a b c", b=2, c=m)[:, :, 1 - d]
                            ins = nc.tensor.matmul(
                                bank[:, g * P + tile * 64:g * P + (tile + 1) * 64]
                                .rearrange("p (a c) -> p a c", c=m),
                                keys[:, tile * P:(tile + 1) * P], t_half, start=True, stop=True)
                    return ins

                if k == 1:
                    pe.wait_ge(pair_read[0], n + 1)
                    pe.wait_ge(pair_read[1], n + 1)
                    for g in range(2):
                        for tt in range(NT):
                            ins = nc.tensor.transpose(M[0][:, g * T + tt * P:g * T + (tt + 1) * P],
                                                      proj_a[:, tt, g], ident[:])
                    mark(ins, "qkT")
                    for tt in range(NT):
                        ins = nc.tensor.transpose(M[2][:, tt * P:(tt + 1) * P], proj_a[:, tt, 3],
                                                  ident[:])
                    mark(ins, "hqT")
                    for g in range(2):
                        for tt in range(NT):
                            ins = nc.tensor.transpose(M[1][:, g * T + tt * P:g * T + (tt + 1) * P],
                                                      proj_b[:, tt, 2 + g], ident[:])
                    mark(ins, "gateT")
                if k == 2:
                    pe.wait_ge(mix_act.sem, mix_act.at("exp_pos", n))
                    for mp in range(2):
                        part = slice(mp * DA, (mp + 1) * DA)
                        for tt in range(NT):
                            ins = nc.tensor.matmul(M[mp][:, tt * T:(tt + 1) * T],
                                                   qkT[part, 0, tt * P:(tt + 1) * P], qkT[part, 1],
                                                   start=True, stop=True)
                        mark(ins, f"S{mp}")
                if k == 3:
                    pe.wait_ge(mix_pool.sem, mix_pool.at("kin_sum", n))
                    for tile in range(NT):
                        cols = slice(tile * P, (tile + 1) * P)
                        ins = nc.tensor.matmul(M[2][:, cols], kin_sum[:, cols], hqT[:, cols],
                                               start=True, stop=True)
                    mark(ins, "diag")
                    pe.wait_ge(mix_pool.sem, mix_pool.at("KF8", n))
                    pe.wait_ge(mix_dve.sem, mix_dve.at("QF8", n))
                    mark(levels(0, 0), "F0")
                if k == 4:
                    pe.wait_ge(mix_pool.sem, mix_pool.at("KF128", n))
                    pe.wait_ge(mix_dve.sem, mix_dve.at("QF128", n))
                    mark(levels(0, 1), "F1")
                if k == 5:
                    pe.wait_ge(mix_pool.sem, mix_pool.at("KB8", n))
                    pe.wait_ge(mix_dve.sem, mix_dve.at("QB8", n))
                    mark(levels(1, 0), "B0")
                    for st in range(NT):
                        for tt in range(NT):
                            ins = nc.tensor.transpose(M[0][:, st * T + tt * P:st * T + (tt + 1) * P],
                                                      sm[:, tt, 0, st * P:(st + 1) * P], ident[:])
                    mark(ins, "aT")
                if k == 6:
                    pe.wait_ge(mix_pool.sem, mix_pool.at("KB128", n))
                    pe.wait_ge(mix_dve.sem, mix_dve.at("QB128", n))
                    mark(levels(1, 1), "B1")
                if k == 7:
                    pe.wait_ge(mix_act.sem, mix_act.at("aT", n))
                    pe.wait_ge(mix_dve.sem, mix_dve.at("PB1", n))
                    for g, rhs in enumerate((proj_a[:, :, 2], proj_b[:, :, 0])):
                        for tt in range(NT):
                            for st in range(NT):
                                lhs = (aT[:, st, tt * P:(tt + 1) * P] if g == 0 else
                                       att[:, st, int(st != tt)])
                                ins = nc.tensor.matmul(
                                    M[0][:, (2 * g + tt) * P:(2 * g + tt + 1) * P], lhs, rhs[:, st],
                                    start=st == 0, stop=st == NT - 1)
                    mark(ins, "oAB")
                if k == 8:
                    pe.wait_ge(mix_dve.sem, mix_dve.at("on", n))
                    for g in range(4):
                        ins = nc.tensor.transpose(M[3][:, g * P:(g + 1) * P], on[:, g], ident[:])
                    mark(ins, "oT")

            for c in range(2):
                for j in range(4):
                    if c == 0:
                        pe.wait_ge(norm_lo[0], 2 * j + 2)
                    head_product(c, j, 4 * c + j, 0, 0, 0)
            with pe.Fori(0, HEADS - 1) as i:
                for p in range(8):
                    if p:
                        hook(p, i)
                    head_product(p // 4, p % 4, 8 + p, 8, i, i + 1)
                hook(8, i)
            for p, (cb, j) in enumerate(OUT_ORDER):
                if 1 <= p <= 6:
                    hook(p, HEADS - 1)
                if p == 6:
                    hook(7, HEADS - 1)
                    hook(8, HEADS - 1)
                    pe.wait_ge(mix_dve.sem, mix_dve.at("lo", HEADS - 1))
                if p == 0:
                    pe.wait_ge(mix_dve.sem, mix_dve.at("lo", HEADS - 2))
                if j == 0:
                    pe.wait_ge(pair_read[cb % 2], HEADS + cb // 2)
                multiply(pe, OUT_AT + p, 0, 0, yT_hi, yT_lo, 4 * j, pair[cb % 2], j == 0, j == 3)

            def mlp(at, layer, norm):
                gain_transpose_pe(norm)
                before = [PAIR_L0, PAIR_CONV][layer]

                def up(p, base, step, i, n, first=False):
                    if first:
                        pe.wait_ge(norm_lo[norm], 8 if p == 0 else 2 * p + 2)
                    elif p == 0:
                        pe.wait_ge(up_relu[layer], n * NT)
                    multiply(pe, base, step, i, xT_hi, xT_lo, 4 * p, m23, p == 0, p == 3)

                def hidden_T(n):
                    pe.wait_ge(up_sq[layer], n * NT + NT)
                    for b in range(2):
                        for q in range(2):
                            for tt in range(NT):
                                ins = nc.tensor.transpose(
                                    M[b][:, q * T + tt * P:q * T + (tt + 1) * P],
                                    act[:, tt, (2 * b + q) * P:(2 * b + q + 1) * P], ident[:])
                        ins.then_inc(hT_done[layer], 1)

                def down(cb, base, step, i, n):
                    if cb == 0:
                        pe.wait_ge(hT_lo[layer], n * 2 + 2)
                    pe.wait_ge(pair_read[cb % 2], n * 2 + (before + cb // 2))
                    multiply(pe, base, step, i, yT_hi, yT_lo, 0, pair[cb % 2], True, True)

                for p in range(4):
                    up(p, at + p, 0, 0, 0, first=True)
                blocks_n = FF // 512
                with pe.Fori(0, blocks_n - 1) as i:
                    for p in range(8):
                        if p == 2:
                            hidden_T(i)
                        if p < 4:
                            up(p, at + 4 + p, 8, i, i + 1)
                        else:
                            down(p - 4, at + 4 + p, 8, i, i)
                hidden_T(blocks_n - 1)
                for cb in range(CB):
                    down(cb, at + MLP_SLOTS - 4 + cb, 0, 0, blocks_n - 1)

            mlp(MLP0_AT, 0, 1)

            gain_transpose_pe(2)

            def conv_in(which, j, base, step, i, n, first=False):
                if first and which == "c":
                    pe.wait_ge(norm_lo[2], 2 * j + 2)
                if j == 0:
                    if which == "b":
                        if not first:
                            pe.wait_ge(b_read, n)
                    else:
                        pe.wait_ge(pair_read["ch".index(which)],
                                   PAIR_MLP0 if first else n * 3 + (PAIR_MLP0 - 2))
                dst = {"c": pair[0], "h": pair[1], "b": m23}[which]
                multiply(pe, base, step, i, xT_hi, xT_lo, 4 * j, dst, j == 0, j == 3)

            def conv_T(src, done):
                for b in range(2):
                    for q in range(2):
                        for tt in range(NT):
                            ins = nc.tensor.transpose(
                                M[b][:, q * T + tt * P:q * T + (tt + 1) * P],
                                src[:, tt, (2 * b + q) * P:(2 * b + q + 1) * P], ident[:])
                    ins.then_inc(done, 1)

            def u_T(n):
                pe.wait_ge(pair_read[1], n * 3 + (PAIR_MLP0 + 1))
                conv_T(cg, uT_done)

            def b_T(n):
                pe.wait_ge(b_read, n + 1)
                pe.wait_ge(uT_read, n * 2 + 2)
                conv_T(bg, bT_done)

            def conv_out(cb, base, step, i, n):
                if cb == 0:
                    pe.wait_ge(cv_lo, n + 1)
                more = 0 if isinstance(n, int) else 1
                pe.wait_ge(pair_read[cb % 2], n * 3 + (PAIR_MLP0 + 1 + more + cb // 2))
                multiply(pe, base, step, i, yT_hi, yT_lo, 0, pair[cb % 2], True, True)

            for u, which in enumerate("chb"):
                for j in range(4):
                    conv_in(which, j, CONV_AT + 4 * u + j, 0, 0, 0, first=True)
            with pe.Fori(0, CB - 1) as i:
                for p in range(16):
                    if p == 1:
                        u_T(i)
                    if p == 2:
                        b_T(i)
                    at = CONV_AT + 12 + p
                    if p < 4:
                        conv_in("c", p, at, 16, i, i + 1)
                    elif p < 8:
                        conv_in("h", p - 4, at, 16, i, i + 1)
                    elif p < 12:
                        conv_out(p - 8, at, 16, i, i)
                    else:
                        conv_in("b", p - 12, at, 16, i, i + 1)
            u_T(CB - 1)
            b_T(CB - 1)
            for cb in range(CB):
                conv_out(cb, CONV_AT + CONV_SLOTS - 4 + cb, 0, 0, CB - 1)

            mlp(MLP1_AT, 1, 3)

        @block.scalar
        def _(eng):
            for cb in range(CB):
                eng.dma_start(h[:, :, cb * 512:(cb + 1) * 512],
                              x[0].rearrange("(t p) n -> p t n", p=P)[:, :, cb * 512:(cb + 1) * 512]
                              ).then_inc(x_in[cb], 16)
            for at, n, src in ((G_MIX, 32, mix_norm_g.rearrange("a (k p) -> (a k) p", p=P)),
                               (G_MLP, 32, mlp_norm_g.rearrange("a (k p) -> (a k) p", p=P)),
                               (G_CONV, 48, conv_w[0].rearrange("a (k p) -> (a k) p", p=P)),
                               (G_HGRN, 8, hgrn_norm_g[0].rearrange("(k p) -> k p", p=P)),
                               (G_SUB, 1, diff_subln_g)):
                eng.dma_start(rows_a[at:at + n, :], src).then_inc(rows_in, 16)
            eng.dma_start(rows_b[:, :], hgrn_lb.rearrange("a b (k p) -> (a b k) p", p=P)
                          ).then_inc(rows_in, 16)
            eng.dma_start(lam4[:].rearrange("p a b -> p (a b)"),
                          diff_lambda[0].rearrange("(o a) b -> o (a b)", o=1).broadcast_to([P, 4 * DA])
                          ).then_inc(lam_in, 16)

            def norm_hi_of(n, gain):
                for cb in range(CB):
                    for b in range(2):
                        eng.wait_ge(norm_T[n], 2 * cb + b + 1)
                        for q in range(2):
                            kt = 4 * cb + 2 * b + q
                            ins = nc.scalar.activation(
                                xT_hi[:, kt], M[2 * (cb % 2) + b][:, q * T:(q + 1) * T], ACT.Copy,
                                scale=gains[:, gain + kt:gain + kt + 1])
                        ins.then_inc(norm_hi[n], 1)

            def squares(n, cbs):
                for cb in cbs:
                    for tt in range(NT):
                        if (cb, tt) != (0, 0) or n:
                            eng.wait_ge(sq_done, (n * CB + cb) * NT + tt)
                        ins = nc.scalar.activation(junk, h[:, tt, cb * 512:(cb + 1) * 512],
                                                   ACT.Square, accum_out=sumsq[:, tt, cb:cb + 1])
                        ins.then_inc(sq_done, 1)

            def copy_product(c, n):
                wait_product(eng, PROJ_AT + 4 * c + 3, 8, n)
                for tt in range(NT):
                    ins = nc.scalar.activation([proj_a, proj_b][c][:, tt],
                                               pair[c][:, tt].rearrange("p (g n) -> p g n", g=4),
                                               ACT.Copy, scale=rstd[:, 0, tt:tt + 1])
                ins.then_inc(pair_read[c], 1)

            def hook(k, n):
                def mark(ins, name):
                    assert name in mix_act.names
                    ins.then_inc(mix_act.sem, 1)

                if k == 1:
                    eng.wait_ge(mix_pe.sem, mix_pe.at("qkT", n))
                    mark(nc.scalar.activation(qkT[:], M[0].rearrange("p (a b) -> p a b", a=2),
                                              ACT.Copy), "qkT")
                    eng.wait_ge(mix_pe.sem, mix_pe.at("hqT", n))
                    mark(nc.scalar.activation(hqT[:], M[2][:, 0:T], ACT.Copy), "hqT")
                    eng.wait_ge(mix_pe.sem, mix_pe.at("gateT", n))
                    z = M[1].rearrange("p (a b) -> p a b", a=2)
                    mark(nc.scalar.activation(gate[:], z, ACT.Exp, scale=-1.0), "exp_neg")
                    mark(nc.scalar.activation(kin[:], z, ACT.Exp), "exp_pos")
                    mark(nc.scalar.activation(silu[:], proj_b[:, :, 1], ACT.Exp, scale=-1.0), "exp_hg")
                if k == 2:
                    eng.wait_ge(mix_pool.sem, mix_pool.at("neg_mx", n))
                    for tt in range(NT):
                        for mp in range(2):
                            c = 2 * tt + mp
                            ins = nc.scalar.activation(sm[:, tt, mp], sm[:, tt, mp], ACT.Exp,
                                                       bias=neg_mx[:, c:c + 1],
                                                       accum_out=rowsum[:, c:c + 1])
                    mark(ins, "exp_s")
                if k == 5:
                    eng.wait_ge(mix_pe.sem, mix_pe.at("aT", n))
                    mark(nc.scalar.activation(aT[:], M[0].rearrange("p (a b) -> p a b", a=NT),
                                              ACT.Copy), "aT")
                if k == 7:
                    eng.wait_ge(mix_pe.sem, mix_pe.at("oAB", n))
                    for g in range(4):
                        ins = nc.scalar.activation(on[:, g], M[0][:, g * P:(g + 1) * P], ACT.Square,
                                                   accum_out=osq[:, g:g + 1])
                    mark(ins, "osq")
                if k == 8:
                    eng.wait_ge(mix_pe.sem, mix_pe.at("oT", n))
                    for g, name in enumerate(("hi_a", "hi_b")):
                        mark(nc.scalar.activation(row(yT_hi, n * 2 + g), M[3][:, g * T:(g + 1) * T],
                                                  ACT.Copy, scale=out_gain(g, n)), name)

            eng.wait_ge(rows_T, 1)
            nc.scalar.activation(gains[:, 0:121], M[3][:, 0:121], ACT.Copy)
            nc.scalar.activation(lbt[:].rearrange("p a b c -> p (a b c)"), M[3][:, 128:176], ACT.Copy
                                 ).then_inc(par_act, 1)
            eng.wait_ge(par_act, 1)
            norm_hi_of(0, G_MIX)
            for n in range(2):
                split_hi(eng, n, 0, 0)
            eng.wait_ge(par_dve, 4)
            nc.scalar.activation(lbt[:], lbt[:], ACT.Exp).then_inc(par_act, 1)
            nc.scalar.activation(lam_sum[:], lam_sum[:], ACT.Exp).then_inc(par_act, 1)
            for p in range(8):
                if p in (1, 2):
                    squares(0, (2 * p - 2, 2 * p - 1))
                if p == 5:
                    eng.wait_ge(rstd_step, 2)
                    copy_product(0, 0)
                split_hi(eng, p + 2, 0, 0)
            with eng.Fori(0, HEADS - 1) as i:
                copy_product(1, i)
                for p in range(8):
                    if p:
                        hook(p, i)
                    if p == 7:
                        copy_product(0, i + 1)
                    split_hi(eng, 8 + p + 2, 8, i)
                hook(8, i)
            copy_product(1, HEADS - 1)
            for p in range(16):
                if 1 <= p <= 6:
                    hook(p, HEADS - 1)
                if p == 6:
                    hook(7, HEADS - 1)
                    hook(8, HEADS - 1)
                split_hi(eng, OUT_AT + p + 2, 0, 0)

            def mlp(at, layer, norm, gain):
                norm_hi_of(norm, gain)
                rows = rstd[:, norm]

                def rectify(n, *position):
                    wait_product(eng, *position)
                    for tt in range(NT):
                        nc.scalar.activation(act[:, tt], m23[:, tt], ACT.Relu,
                                             scale=rows[:, tt:tt + 1]).then_inc(up_relu[layer], 1)
                    for tt in range(NT):
                        eng.wait_ge(up_relu[layer], n * NT + (tt + 1))
                        nc.scalar.activation(act[:, tt], act[:, tt], ACT.Square
                                             ).then_inc(up_sq[layer], 1)

                def hidden_hi(n):
                    for b in range(2):
                        eng.wait_ge(hT_done[layer], n * 2 + (b + 1))
                        nc.scalar.activation(yT_hi[:, 2 * b:2 * b + 2],
                                             M[b].rearrange("p (a b) -> p a b", a=2), ACT.Copy
                                             ).then_inc(hT_hi[layer], 1)

                for p in range(4):
                    if p in (1, 2):
                        squares(norm, (2 * p - 2, 2 * p - 1))
                    split_hi(eng, at + p + 2, 0, 0)
                eng.wait_ge(rstd_step, 2 * norm + 2)
                rectify(0, at + 3, 0, 0)
                with eng.Fori(0, FF // 512 - 1) as i:
                    for p in range(8):
                        if p == 2:
                            hidden_hi(i)
                        if p == 4:
                            rectify(i + 1, at + 7, 8, i)
                        split_hi(eng, at + 4 + p + 2, 8, i)
                hidden_hi(FF // 512 - 1)
                for cb in range(CB):
                    split_hi(eng, at + MLP_SLOTS - 4 + cb + 2, 0, 0)

            mlp(MLP0_AT, 0, 1, G_MLP)

            norm_hi_of(2, G_MIX + KT)

            def copy_gate(read, dst, src, position):
                wait_product(eng, *position)
                for tt in range(NT):
                    ins = nc.scalar.activation(dst[:, tt], src[:, tt], ACT.Copy,
                                               scale=rstd[:, 2, tt:tt + 1])
                ins.then_inc(read, 1)

            def c_gate(*position):
                copy_gate(pair_read[0], cg, pair[0], position)

            def b_gate(*position):
                copy_gate(b_read, bg, m23, position)

            def copy_uT(n):
                for b in range(2):
                    eng.wait_ge(uT_done, n * 2 + (b + 1))
                    nc.scalar.activation(uT[:, 2 * b:2 * b + 2],
                                         M[b].rearrange("p (a b) -> p a b", a=2), ACT.Copy
                                         ).then_inc(uT_read, 1)

            def conv_hi(n):
                eng.wait_ge(cv_step, n * CONV_STEPS + CONV_STEPS)
                nc.scalar.activation(yT_hi[:, 0:4], cT, ACT.Copy).then_inc(cv_hi, 1)

            for p in range(12):
                if p in (1, 2):
                    squares(2, (2 * p - 2, 2 * p - 1))
                if p == 5:
                    eng.wait_ge(rstd_step, 6)
                    c_gate(CONV_AT + 3, 0, 0)
                split_hi(eng, CONV_AT + p + 2, 0, 0)
            b_gate(CONV_AT + 11, 0, 0)
            with eng.Fori(0, CB - 1) as i:
                for p in range(16):
                    if p == 2:
                        copy_uT(i)
                    if p == 4:
                        c_gate(CONV_AT + 15, 16, i)
                    if p == 6:
                        conv_hi(i)
                    split_hi(eng, CONV_AT + 12 + p + 2, 16, i)
                b_gate(CONV_AT + 27, 16, i)
            copy_uT(CB - 1)
            conv_hi(CB - 1)
            for cb in range(CB):
                split_hi(eng, CONV_AT + CONV_SLOTS - 4 + cb + 2, 0, 0)

            mlp(MLP1_AT, 1, 3, G_MLP + KT)
            for cb in range(CB):
                eng.wait_ge(pair_read[cb % 2], PAIR_MLP1 - 1 + cb // 2)
                squares(4, (cb,))

        @block.vector
        def _(dve):
            def norm_lo_of(n, gain):
                for cb in range(CB):
                    for b in range(2):
                        dve.wait_ge(norm_hi[n], 2 * cb + b + 1)
                        for q in range(2):
                            kt = 4 * cb + 2 * b + q
                            ins = nc.vector.scalar_tensor_tensor(
                                out=xT_lo[:, kt], in0=M[2 * (cb % 2) + b][:, q * T:(q + 1) * T],
                                scalar=gains[:, gain + kt:gain + kt + 1],
                                in1=xT_hi[:, kt].bitcast(F32), op0=ALU.mult, op1=ALU.subtract)
                        ins.then_inc(norm_lo[n], 1)

            def sum_squares(n):
                dve.wait_ge(sq_done, (n + 1) * NT * CB)
                if n:
                    dve.wait_ge(rstd_step, 2 * n)
                nc.vector.tensor_reduce(meansq[:], sumsq[:], AX_X, ALU.add).then_inc(sq_sum, 1)

            def add_block(cb, *position):
                wait_product(dve, *position)
                cols = slice(cb * 512, (cb + 1) * 512)
                for tt in range(NT):
                    ins = nc.vector.tensor_tensor(h[:, tt, cols], pair[cb % 2][:, tt], h[:, tt, cols],
                                                  ALU.add)
                ins.then_inc(pair_read[cb % 2], 1)

            def hook(k, n):
                def mark(ins, name):
                    assert name in mix_dve.names
                    order.append(name)
                    ins.then_inc(mix_dve.sem, 1)

                def own(name):
                    dve.wait_ge(mix_dve.sem, mix_dve.at(name, n))

                def q_level(d, lv):
                    if lv == 0:
                        mark(nc.vector.tensor_tensor(lq[:, 0], hqT[:], gate[:, d], ALU.mult),
                             f"Q{'FB'[d]}1")
                        return
                    m = LEVELS[lv - 1]
                    own(f"Q{'FB'[d]}{m}")
                    factor = flat(even if d == 0 else odd, d, lv - 1)
                    mark(nc.vector.tensor_tensor(
                        lq[:, lv].rearrange("p (a b) -> p a b", b=m),
                        lq[:, lv - 1].rearrange("p (a b) -> p a b", b=m),
                        factor.unsqueeze(2).broadcast_to([P, T // m, m]), ALU.mult),
                        f"Q{'FB'[d]}{2 * m}")

                def pick(d, group):
                    bank = M[3] if group == 0 else M[2]
                    for g in range(4):
                        lv = 4 * group + g
                        m = LEVELS[lv]
                        if m == 128:
                            ins = nc.vector.tensor_copy(att[:, d, 1], bank[:, g * P:(g + 1) * P])
                            continue
                        stand_alone(dve, n)
                        dst = att[:, :, 0].rearrange("p t (a b c) -> p t a b c", b=2, c=m)[
                            :, :, :, 1 - d]
                        ins = nc.vector.copy_predicated(
                            dst, mask[:, d, lv].bitcast(U32).rearrange("p (a c) -> p a c", c=m)
                            .unsqueeze(1).broadcast_to([P, NT, 64 // m, m]),
                            bank[:, g * P:(g + 1) * P].rearrange("p (t a c) -> p t a c", t=NT, c=m))
                        if g < 3:
                            ins.then_inc(picked, 1)
                            dve.wait_ge(picked, n * 12 + ((2 * d + group) * 3 + g + 1))
                    mark(ins, f"P{'FB'[d]}{group}")

                if k == 1:
                    dve.wait_ge(mix_pool.sem, mix_pool.at("f_add", n))
                    mark(nc.vector.reciprocal(gate[:], gate[:]), "f_inv")
                    dve.wait_ge(mix_pool.sem, mix_pool.at("k_add", n))
                    mark(nc.vector.reciprocal(kin[:], kin[:]), "k_inv")
                    own("f_inv")
                    for d in range(2):
                        ins = nc.vector.tensor_scalar(gate[:, d], gate[:, d], lb_col(one_lb, n, d),
                                                      lb_col(lb, n, d), ALU.mult, ALU.add)
                    mark(ins, "f")
                    dve.wait_ge(mix_pool.sem, mix_pool.at("silu_add", n))
                    mark(nc.vector.reciprocal(silu[:], silu[:]), "silu_inv")
                if k == 2:
                    for mp in range(2):
                        dve.wait_ge(mix_pe.sem, mix_pe.at(f"S{mp}", n))
                        if mp == 0:
                            dve.wait_ge(mix_pool.sem, mix_pool.at("kin_sum", n))
                        ins = nc.vector.scalar_tensor_tensor(
                            out=sm[:, :, mp], in0=M[mp].rearrange("p (a b) -> p a b", a=2),
                            scalar=DA ** -0.5, in1=bias[:], op0=ALU.mult, op1=ALU.add)
                    mark(ins, "s")
                    own("s")
                    mark(nc.vector.tensor_reduce(mx[:], sm[:].rearrange("p a b c -> p (a b) c"),
                                                 AX_X, ALU.max), "max")
                    dve.wait_ge(mix_act.sem, mix_act.at("hqT", n))
                    for lv in range(4):
                        if lv == 1:
                            dve.wait_ge(mix_pool.sem, mix_pool.at("tree4", n))
                        q_level(0, lv)
                if k == 3:
                    dve.wait_ge(const_pool, CONST_ALL)
                    dve.wait_ge(mix_pe.sem, mix_pe.at("diag", n))
                    mark(nc.vector.tensor_copy(att[:, :, 0], M[2][:, 0:T].rearrange(
                        "p (a b) -> p a b", a=NT)), "diag")
                    dve.wait_ge(mix_act.sem, mix_act.at("exp_s", n))
                    mark(nc.vector.reciprocal(rinv[:], rowsum[:]), "r_inv")
                    own("r_inv")
                    mark(nc.vector.tensor_scalar(neg_lr[:], rinv[:].rearrange(
                        "p (a b) -> p a b", b=2)[:, :, 1], neg_lam[:, 0:1], None, ALU.mult), "neg_lr")
                    own("neg_lr")
                    for tt in range(NT):
                        ins = nc.vector.tensor_scalar(sm[:, tt, 1], sm[:, tt, 1], neg_lr[:, tt:tt + 1],
                                                      None, ALU.mult)
                    mark(ins, "a1")
                    own("a1")
                    for tt in range(NT):
                        ins = nc.vector.scalar_tensor_tensor(
                            out=sm[:, tt, 0], in0=sm[:, tt, 0], scalar=rinv[:, 2 * tt:2 * tt + 1],
                            in1=sm[:, tt, 1], op0=ALU.mult, op1=ALU.add)
                    mark(ins, "a")
                    dve.wait_ge(mix_pe.sem, mix_pe.at("F0", n))
                    own("diag")
                    pick(0, 0)
                    dve.wait_ge(mix_pool.sem, mix_pool.at("tree64", n))
                    for lv in range(4, 8):
                        q_level(0, lv)
                if k == 4:
                    dve.wait_ge(mix_pe.sem, mix_pe.at("F1", n))
                    own("PF0")
                    pick(0, 1)
                    for lv in range(4):
                        q_level(1, lv)
                if k == 5:
                    dve.wait_ge(mix_pe.sem, mix_pe.at("B0", n))
                    own("PF1")
                    pick(1, 0)
                    for lv in range(4, 8):
                        q_level(1, lv)
                if k == 6:
                    dve.wait_ge(mix_pe.sem, mix_pe.at("B1", n))
                    own("PB0")
                    pick(1, 1)
                if k == 7:
                    dve.wait_ge(mix_pool.sem, mix_pool.at("o_rstd", n))
                    for tt in range(NT):
                        nc.vector.tensor_scalar(on[:, tt], M[0][:, tt * P:(tt + 1) * P],
                                                orstd[:, tt:tt + 1], None, ALU.mult)
                    for tt in range(NT):
                        ins = nc.vector.scalar_tensor_tensor(
                            out=on[:, 2 + tt], in0=M[0][:, (2 + tt) * P:(3 + tt) * P],
                            scalar=orstd[:, 2 + tt:3 + tt], in1=silu[:, tt], op0=ALU.mult,
                            op1=ALU.mult)
                    mark(ins, "on")
                if k == 8:
                    dve.wait_ge(mix_act.sem, mix_act.at("hi_b", n))
                    for g in range(2):
                        ins = nc.vector.scalar_tensor_tensor(
                            out=row(yT_lo, n * 2 + g), in0=M[3][:, g * T:(g + 1) * T],
                            scalar=out_gain(g, n), in1=row(yT_hi, n * 2 + g).bitcast(F32),
                            op0=ALU.mult, op1=ALU.subtract)
                    mark(ins, "lo")
                    assert order == mix_dve.names, (order, mix_dve.names)
                    order.clear()

            order = []
            step = [0]

            def par(ins):
                step[0] += 1
                ins.then_inc(par_dve, 1)
                dve.wait_ge(par_dve, step[0])

            dve.wait_ge(lam_in, 16)
            par(nc.vector.tensor_tensor(lam4[:, 0::2], lam4[:, 0::2], lam4[:, 1::2], ALU.mult))
            par(nc.vector.tensor_reduce(lam_sum[:], lam4[:, 0::2], AX_X, ALU.add))
            dve.wait_ge(par_act, 1)
            par(nc.vector.tensor_reduce(lbm[:], lbt[:].rearrange("p a b c -> p a c b"), AX_X, ALU.max))
            par(nc.vector.tensor_tensor(lbt[:], lbt[:], lbm[:].unsqueeze(2).broadcast_to(
                [P, 2, 3, HEADS]), ALU.subtract))
            norm_lo_of(0, G_MIX)
            for n in range(2):
                split_lo(dve, n, 0, 0)
            dve.wait_ge(par_act, 3)
            par(nc.vector.tensor_tensor(neg_lam[:], lam_sum[:, 1:2], lam_sum[:, 0:1], ALU.subtract))
            par(nc.vector.tensor_scalar(neg_lam[:], neg_lam[:], -LAM_INIT, None, ALU.add))
            par(nc.vector.tensor_reduce(lbs[:], lbt[:].rearrange("p a b c -> p a c b"), AX_X, ALU.add))
            par(nc.vector.reciprocal(lbs[:], lbs[:]))
            lb_v = lb[:].rearrange("p h d -> p d h")
            one_v = one_lb[:].rearrange("p h d -> p d h")
            par(nc.vector.tensor_tensor(lb_v, lbt[:, :, 0], lbs[:], ALU.mult))
            par(nc.vector.tensor_scalar(one_v, lb_v, -1.0, 1.0, ALU.mult, ALU.add))
            par(nc.vector.tensor_scalar(gains[:, G_SUB:G_SUB + 1], gains[:, G_SUB:G_SUB + 1],
                                        1.0 - LAM_INIT, None, ALU.mult))
            assert step[0] == PAR_LB
            for p in range(8):
                if p == 3:
                    sum_squares(0)
                split_lo(dve, p + 2, 0, 0)
            with dve.Fori(0, HEADS - 1) as i:
                for p in range(8):
                    if p:
                        hook(p, i)
                    split_lo(dve, 8 + p + 2, 8, i)
                hook(8, i)
            for p, (cb, j) in enumerate(OUT_ORDER):
                if 1 <= p <= 6:
                    hook(p, HEADS - 1)
                if p == 6:
                    hook(7, HEADS - 1)
                    hook(8, HEADS - 1)
                split_lo(dve, OUT_AT + p + 2, 0, 0)
                if j == 3:
                    add_block(cb, OUT_AT + p, 0, 0)

            def mlp(at, layer, norm, gain):
                norm_lo_of(norm, gain)

                def hidden_lo(n):
                    for b in range(2):
                        dve.wait_ge(hT_hi[layer], n * 2 + (b + 1))
                        nc.vector.tensor_tensor(yT_lo[:, 2 * b:2 * b + 2],
                                                M[b].rearrange("p (a b) -> p a b", a=2),
                                                yT_hi[:, 2 * b:2 * b + 2].bitcast(F32), ALU.subtract
                                                ).then_inc(hT_lo[layer], 1)

                for p in range(4):
                    if p == 3:
                        sum_squares(norm)
                    split_lo(dve, at + p + 2, 0, 0)
                with dve.Fori(0, FF // 512 - 1) as i:
                    for p in range(8):
                        if p == 2:
                            hidden_lo(i)
                        split_lo(dve, at + 4 + p + 2, 8, i)
                        if p >= 4:
                            add_block(p - 4, at + 4 + p, 8, i)
                hidden_lo(FF // 512 - 1)
                for cb in range(CB):
                    split_lo(dve, at + MLP_SLOTS - 4 + cb + 2, 0, 0)
                    add_block(cb, at + MLP_SLOTS - 4 + cb, 0, 0)

            mlp(MLP0_AT, 0, 1, G_MLP)

            norm_lo_of(2, G_MIX + KT)

            def make_u(n, *position):
                wait_product(dve, *position)
                dve.wait_ge(pair_read[0], PAIR_MLP0 + 1 if isinstance(n, int) else
                            n * 3 + (PAIR_MLP0 - 1))
                for tt in range(NT):
                    ins = nc.vector.scalar_tensor_tensor(
                        out=cg[:, tt], in0=pair[1][:, tt], scalar=rstd[:, 2, tt:tt + 1],
                        in1=cg[:, tt], op0=ALU.mult, op1=ALU.mult)
                ins.then_inc(pair_read[1], 1)

            def convolve(n):
                def tap(w, q):
                    at = G_CONV + w * KT + q
                    if isinstance(n, int):
                        return gains[:, at + 4 * n:at + 4 * n + 1]
                    return gains[:, bass.ds(n * 4 + at, 1)]

                dve.wait_ge(uT_read, n * 2 + 2)
                for q in range(4):
                    ins = nc.vector.tensor_scalar(cT[:, q], uT[:, q], tap(1, q), None, ALU.mult)
                ins.then_inc(cv_step, 1)
                dve.wait_ge(cv_step, n * CONV_STEPS + 1)
                for q in range(4):
                    ins = nc.vector.scalar_tensor_tensor(
                        out=cT[:, q, 1:T], in0=uT[:, q, 0:T - 1], scalar=tap(0, q),
                        in1=cT[:, q, 1:T], op0=ALU.mult, op1=ALU.add)
                ins.then_inc(cv_step, 1)
                dve.wait_ge(cv_step, n * CONV_STEPS + 2)
                for q in range(4):
                    ins = nc.vector.scalar_tensor_tensor(
                        out=cT[:, q, 0:T - 1], in0=uT[:, q, 1:T], scalar=tap(2, q),
                        in1=cT[:, q, 0:T - 1], op0=ALU.mult, op1=ALU.add)
                ins.then_inc(cv_step, 1)
                dve.wait_ge(cv_step, n * CONV_STEPS + 3)
                for b in range(2):
                    dve.wait_ge(bT_done, n * 2 + (b + 1))
                    ins = nc.vector.tensor_tensor(cT[:, 2 * b:2 * b + 2],
                                                  M[b].rearrange("p (a b) -> p a b", a=2),
                                                  cT[:, 2 * b:2 * b + 2], ALU.mult)
                ins.then_inc(cv_step, 1)

            def conv_lo(n):
                dve.wait_ge(cv_hi, n + 1)
                nc.vector.tensor_tensor(yT_lo[:, 0:4], cT, yT_hi[:, 0:4].bitcast(F32), ALU.subtract
                                        ).then_inc(cv_lo, 1)

            for p in range(12):
                if p == 3:
                    sum_squares(2)
                if p == 9:
                    dve.wait_ge(rstd_step, 6)
                    make_u(0, CONV_AT + 7, 0, 0)
                split_lo(dve, CONV_AT + p + 2, 0, 0)
            with dve.Fori(0, CB - 1) as i:
                for p in range(16):
                    if p == 4:
                        convolve(i)
                    if p == 7:
                        conv_lo(i)
                    if p == 8:
                        make_u(i + 1, CONV_AT + 19, 16, i)
                    split_lo(dve, CONV_AT + 12 + p + 2, 16, i)
                    if 8 <= p < 12:
                        add_block(p - 8, CONV_AT + 12 + p, 16, i)
            convolve(CB - 1)
            conv_lo(CB - 1)
            for cb in range(CB):
                split_lo(dve, CONV_AT + CONV_SLOTS - 4 + cb + 2, 0, 0)
                add_block(cb, CONV_AT + CONV_SLOTS - 4 + cb, 0, 0)

            mlp(MLP1_AT, 1, 3, G_MLP + KT)

            sum_squares(4)
            dve.wait_ge(rstd_step, 10)
            dve.wait_ge(fin_rows, 16)
            for cb in range(CB):
                cols = slice(cb * 512, (cb + 1) * 512)
                for tt in range(NT):
                    nc.vector.scalar_tensor_tensor(
                        out=h[:, tt, cols], in0=h[:, tt, cols], scalar=rstd[:, 4, tt:tt + 1],
                        in1=raw[:, 0, cb], op0=ALU.mult, op1=ALU.mult).then_inc(fin_ready, 1)


_INS = ["x", "mix_norm_g", "mlp_norm_g", "final_norm_g", "ab_w_in", "ab_w_out", "diff_lambda",
        "diff_subln_g", "hgrn_lb", "hgrn_norm_g", "conv_w_in", "conv_w", "conv_w_out", "mlp_w_up",
        "mlp_w_down"]


def kernel(**inputs):
    import concourse.bacc as _bacc
    from concourse.bass_utils import run_bass_kernel_spmd as _run

    nc = _bacc.Bacc("TRN2", target_bir_lowering=False, num_devices=1)
    arrays, args = {}, []
    for name in _INS:
        a = np.ascontiguousarray(inputs[name])
        arrays[f"in_{name}"] = a
        args.append(nc.dram_tensor(f"in_{name}", a.shape, mybir.dt.from_np(a.dtype),
                                   kind="ExternalInput").ap())
    out = nc.dram_tensor("out_dram", (1, T, D), F32, kind="ExternalOutput").ap()
    build(nc, *args, out)
    r = _run(nc, [arrays], core_ids=[0])
    return r.results[0]["out_dram"]
```

```python
from contextlib import ExitStack

import concourse.bass as bass
import numpy as np
from concourse import mybir

F32 = mybir.dt.float32
F32R = mybir.dt.float32r
U32 = mybir.dt.uint32
ALU = mybir.AluOpType
ACT = mybir.ActivationFunctionType
AX_X = mybir.AxisListType.X

P = 128
T = 256
NT = T // P
D = 2048
KT = D // P
CB = D // 512
FF = 4 * D
HEADS = 8
DA = 64
EPS = 1e-6
LAM_INIT = 0.8 - 0.6 * 1.0
RAW = 4
HALVES = 4
LEVELS = [1, 2, 4, 8, 16, 32, 64, 128]

PROJ_AT = 0
OUT_AT = PROJ_AT + HEADS * 8
MLP_SLOTS = (FF // 512) * 8
MLP0_AT = OUT_AT + 16
CONV_AT = MLP0_AT + MLP_SLOTS
CONV_SLOTS = CB * 16
MLP1_AT = CONV_AT + CONV_SLOTS
TOTAL = MLP1_AT + MLP_SLOTS

PAIR_L0 = HEADS + CB // 2
PAIR_MLP0 = PAIR_L0 + (FF // 512) * CB // 2
PAIR_CONV = PAIR_MLP0 + CB * (1 + CB // 2)
PAIR_MLP1 = PAIR_CONV + (FF // 512) * CB // 2

CONV_STEPS = 4
CONST_ALL = 11 + 2 * 2 * 7
PAR_LB = 11
ROWS_DMAS = 6

G_MIX, G_MLP, G_CONV, G_HGRN, G_SUB = 0, 32, 64, 112, 120
GAIN_OF = [G_MIX, G_MLP, G_MIX + KT, G_MLP + KT]

OUT_ORDER = [(0, 0), (0, 1), (0, 2), (1, 0), (1, 1), (1, 2), (0, 3), (1, 3)] + [
    (cb, j) for cb in (2, 3) for j in range(4)]


MIX_AT = {1: 1, 3: 2, 6: 3, 8: 4, 10: 5, 12: 6, 14: 7, 16: 8}
LAST_MIX_AT = {1: 1, 3: 2, 5: 3, 7: 4, 8: 5, 9: 6, 11: 7, 12: 8}


class Steps:

    def __init__(self, sem, names):
        self.sem, self.names = sem, names

    def at(self, name, n):
        return n * len(self.names) + (self.names.index(name) + 1)


def build(nc, x, mix_norm_g, mlp_norm_g, final_norm_g, ab_w_in, ab_w_out, diff_lambda, diff_subln_g,
          hgrn_lb, hgrn_norm_g, conv_w_in, conv_w, conv_w_out, mlp_w_up, mlp_w_down, out):
    with ExitStack() as ctx:
        def sb(name, shape, dt=F32):
            return ctx.enter_context(nc.sbuf_tensor(name, shape, dt))

        def pb(name, shape, dt=F32):
            return ctx.enter_context(nc.psum_tensor(name, shape, dt))

        def sem(name):
            return ctx.enter_context(nc.semaphore(name))

        raw = sb("raw", [P, RAW, 4, 512])
        w_hi = sb("w_hi", [P, HALVES, 2, 512], F32R)
        w_lo = sb("w_lo", [P, HALVES, 2, 512], F32R)
        h = sb("h", [P, NT, D])
        xT_hi = sb("xT_hi", [P, KT, T], F32R)
        xT_lo = sb("xT_lo", [P, KT, T], F32R)
        yT_hi = sb("yT_hi", [P, KT, T], F32R)
        yT_lo = sb("yT_lo", [P, KT, T], F32R)
        ident = sb("ident", [P, P])
        rows_a = sb("rows_a", [P, P])
        rows_b = sb("rows_b", [48, P])
        gains = sb("gains", [P, P])
        lbt = sb("lbt", [P, 2, 3, HEADS])
        lbm = sb("lbm", [P, 2, HEADS])
        lbs = sb("lbs", [P, 2, HEADS])
        lb = sb("lb", [P, HEADS, 2])
        one_lb = sb("one_lb", [P, HEADS, 2])
        lam4 = sb("lam4", [P, 4, DA])
        lam_sum = sb("lam_sum", [P, 2])
        neg_lam = sb("neg_lam", [P, 1])
        sumsq = sb("sumsq", [P, NT, CB])
        meansq = sb("meansq", [P, NT])
        rstd = sb("rstd", [P, 5, NT])
        minus_half = sb("minus_half", [P, 4])
        mask = sb("mask", [P, 2, 7, 64])
        bias = sb("bias", [P, NT, T])
        proj_a = sb("proj_a", [P, NT, 4, P])
        proj_b = sb("proj_b", [P, NT, 4, P])
        qkT = sb("qkT", [P, 2, T])
        hqT = sb("hqT", [P, T])
        gate = sb("gate", [P, 2, T])
        kin = sb("kin", [P, 2, T])
        kin_sum = sb("kin_sum", [P, T])
        silu = sb("silu", [P, NT, P])
        even = sb("even", [P, 2, 512])
        odd = sb("odd", [P, 2, 512])
        lq = sb("lq", [P, 8, T])
        lk = sb("lk", [P, 7, T])
        sm = sb("sm", [P, NT, 2, T])
        aT = sb("aT", [P, NT, T])
        att = sb("att", [P, NT, 2, P])
        on = sb("on", [P, 4, P])
        mx = sb("mx", [P, 4])
        neg_mx = sb("neg_mx", [P, 4])
        rowsum = sb("rowsum", [P, 4])
        rinv = sb("rinv", [P, 4])
        neg_lr = sb("neg_lr", [P, NT])
        osq = sb("osq", [P, 4])
        orstd = sb("orstd", [P, 4])
        act = sm[:, :, :, :].rearrange("p a b c -> p a (b c)")
        junk = lq[:, 0:2, :].rearrange("p a b -> p (a b)")
        cg = proj_a[:, :, :, :].rearrange("p a b c -> p a (b c)")
        bg = proj_b[:, :, :, :].rearrange("p a b c -> p a (b c)")
        uT = lk[:, 0:4, :]
        cT = lq[:, 4:8, :]

        pair = [pb(f"pair{i}", [P, NT, 512]) for i in range(2)]
        m01 = pb("m01", [P, 2, 512])
        m23 = pb("m23", [P, 2, 512])
        M = [m01[:, 0], m01[:, 1], m23[:, 0], m23[:, 1]]

        landed = [sem(f"landed{i}") for i in range(RAW)]
        hi_ready = sem("hi_ready")
        lo_ready = sem("lo_ready")
        w_used = sem("w_used")
        x_in = [sem(f"x_in{i}") for i in range(CB)]
        rows_in = sem("rows_in")
        lam_in = sem("lam_in")
        const_pool = sem("const_pool")
        rows_T = sem("rows_T")
        par_dve = sem("par_dve")
        par_act = sem("par_act")
        pair_read = [sem(f"pair_read{i}") for i in range(2)]
        norm_T = [sem(f"norm_T{i}") for i in range(4)]
        norm_hi = [sem(f"norm_hi{i}") for i in range(4)]
        norm_lo = [sem(f"norm_lo{i}") for i in range(4)]
        sq_done = sem("sq_done")
        sq_sum = sem("sq_sum")
        rstd_step = sem("rstd_step")
        up_relu = [sem(f"up_relu{i}") for i in range(2)]
        up_sq = [sem(f"up_sq{i}") for i in range(2)]
        hT_done = [sem(f"hT_done{i}") for i in range(2)]
        hT_hi = [sem(f"hT_hi{i}") for i in range(2)]
        hT_lo = [sem(f"hT_lo{i}") for i in range(2)]
        waited = sem("waited")
        picked = sem("picked")
        b_read = sem("b_read")
        uT_done, uT_read = sem("uT_done"), sem("uT_read")
        bT_done = sem("bT_done")
        cv_step = sem("cv_step")
        cv_hi, cv_lo = sem("cv_hi"), sem("cv_lo")
        fin_rows = sem("fin_rows")
        fin_ready = sem("fin_ready")
        stored = sem("stored")

        mix_pe = Steps(sem("mix_pe"), ["gateT", "qkT", "hqT", "S0", "S1", "diag", "F0", "F1", "B0",
                                       "aT", "B1", "oAB", "oT"])
        mix_act = Steps(sem("mix_act"), ["sig_hg", "sig_neg", "sig_pos", "qkT", "hqT", "exp_s",
                                         "aT", "osq", "hi_a", "hi_b"])
        mix_dve = Steps(sem("mix_dve"), ["kin", "f", "tree1", "s", "max"]
                        + [f"QF{m}" for m in LEVELS[:4]]
                        + ["diag", "r_inv", "neg_lr", "a1", "a", "PF0"]
                        + [f"QF{m}" for m in LEVELS[4:]]
                        + ["PF1"] + [f"QB{m}" for m in LEVELS[:4]]
                        + ["PB0"] + [f"QB{m}" for m in LEVELS[4:]]
                        + ["PB1", "on", "lo"])
        mix_pool = Steps(sem("mix_pool"), ["silu", "kin_sum", "tree2", "tree4"]
                         + [f"KF{m}" for m in LEVELS[1:4]] + ["neg_mx"]
                         + [f"tree{m}" for m in LEVELS[3:7]] + [f"KF{m}" for m in LEVELS[4:]]
                         + [f"KB{m}" for m in LEVELS[1:]] + ["bias", "o_ms", "o_rstd"])

        def flat(tile, d, lv):
            at = 512 - (512 >> lv)
            return tile[:, d, at:at + (256 >> lv)]

        def both(tile, lv):
            at = 512 - (512 >> lv)
            return tile[:, :, at:at + (256 >> lv)].rearrange("p d (a b) -> p d a b", b=2)


        def row(tile, at):
            return tile[:, at] if isinstance(at, int) else tile[:, bass.ds(at, 1), :].rearrange(
                "p a b -> p (a b)")

        def out_gain(g, n):
            if g == 0:
                return gains[:, G_SUB:G_SUB + 1]
            return gains[:, G_HGRN + n:G_HGRN + n + 1] if isinstance(n, int) else \
                gains[:, bass.ds(n + G_HGRN, 1)]

        def lb_col(tile, n, d):
            return tile[:, n, d:d + 1] if isinstance(n, int) else \
                tile[:, bass.ds(n, 1), d:d + 1].rearrange("p a b -> p (a b)")

        ab_in = ab_w_in[0].rearrange("(kt p) (g h n) -> p kt g h n", p=P, g=8, h=HEADS)
        ab_out = ab_w_out[0].rearrange("(g h p) n -> p h g n", g=2, p=P)
        up_src = [mlp_w_up[i].rearrange("(kt p) n -> p kt n", p=P) for i in range(2)]
        down_src = [mlp_w_down[i].rearrange("(kt p) n -> p kt n", p=P) for i in range(2)]
        cin = conv_w_in[0].rearrange("(kt p) n -> p kt n", p=P)
        cout = conv_w_out[0].rearrange("(kt p) n -> p kt n", p=P)

        def count(scale, const, base, step, i):
            if isinstance(i, int):
                return scale * (base + step * i) + const
            return i * (scale * step) + (scale * base + const)

        def stand_alone(eng, n):
            if not isinstance(n, int):
                eng.sem_inc(waited, 1)

        def load(sp, base, step, i, src, pieces=1):
            slot = base % RAW
            if base >= RAW:
                sp.wait_ge(lo_ready, count(2, 2 - 2 * RAW, base, step, i))
            if pieces == 1:
                sp.dma_start(raw[:, slot], src).then_inc(landed[slot], 16)
                return
            for q in range(pieces):
                sp.dma_start(raw[:, slot, q], src(q)).then_inc(landed[slot], 16)

        def landed_at(base, step, i):
            each, before = (64, 0) if base < MLP0_AT else (16, 48 * (MLP0_AT // RAW))
            uses = base // RAW + 1
            return i * (each * step // RAW) + (each * uses + before)

        def split_hi(eng, base, step, i, ks=(0, 1)):
            if base >= TOTAL:
                return
            slot = base % RAW
            if 0 in ks:
                eng.wait_ge(landed[slot], landed_at(base, step, i))
            for k in ks:
                ring = (2 * base + k) % HALVES
                if 2 * base + k >= HALVES:
                    eng.wait_ge(w_used, count(2, k + 1 - HALVES, base, step, i))
                nc.scalar.activation(w_hi[:, ring], raw[:, slot, 2 * k:2 * k + 2], ACT.Copy
                                     ).then_inc(hi_ready, 1)

        def split_lo(eng, base, step, i, ks=(0, 1)):
            if base >= TOTAL:
                return
            slot = base % RAW
            for k in ks:
                ring = (2 * base + k) % HALVES
                eng.wait_ge(hi_ready, count(2, k + 1, base, step, i))
                nc.vector.tensor_tensor(w_lo[:, ring], raw[:, slot, 2 * k:2 * k + 2],
                                        w_hi[:, ring].bitcast(F32), ALU.subtract
                                        ).then_inc(lo_ready, 1)

        def multiply(eng, base, step, i, hi, lo, kt0, dst, first, last, ks=(0, 1)):
            for k in ks:
                ring = (2 * base + k) % HALVES
                eng.wait_ge(lo_ready, count(2, k + 1, base, step, i))
                for q in range(2):
                    kt = kt0 + 2 * k + q
                    begin, end = first and k == 0 and q == 0, last and k == 1 and q == 1
                    for tt in range(NT):
                        cols = slice(tt * P, (tt + 1) * P)
                        nc.tensor.matmul(dst[:, tt], hi[:, kt, cols], w_hi[:, ring, q],
                                         start=begin, stop=False)
                        nc.tensor.matmul(dst[:, tt], hi[:, kt, cols], w_lo[:, ring, q],
                                         start=False, stop=False)
                        mm = nc.tensor.matmul(dst[:, tt], lo[:, kt, cols], w_hi[:, ring, q],
                                              start=False, stop=end)
                mm.then_inc(w_used, 1)

        def wait_product(eng, base, step, i):
            eng.wait_ge(w_used, count(2, 2, base, step, i))

        block = ctx.enter_context(nc.Block())

        @block.sync
        def _(sp):
            def head_columns(c, j, at):
                return lambda q: ab_in[:, 4 * j + q, 4 * c:4 * c + 4, at, :]

            for p in range(8):
                if p < CB:
                    sp.dma_start(h[:, :, p * 512:(p + 1) * 512],
                                 x[0].rearrange("(t p) n -> p t n", p=P)[:, :, p * 512:(p + 1) * 512]
                                 ).then_inc(x_in[p], 16)
                load(sp, p, 0, 0, head_columns(p // 4, p % 4, 0), 4)
            with sp.Fori(0, HEADS - 1) as i:
                for p in range(8):
                    load(sp, 8 + p, 8, i,
                         lambda q: head_columns(p // 4, p % 4, bass.ds(i + 1, 1))(q)
                         .rearrange("p a b n -> p (a b) n"), 4)
            for n, (cb, j) in enumerate(OUT_ORDER):
                load(sp, OUT_AT + n, 0, 0,
                     lambda q: ab_out[:, 2 * j + q // 2, q % 2, cb * 512:(cb + 1) * 512], 4)

            def mlp(at, layer):
                for j in range(4):
                    load(sp, at + j, 0, 0, up_src[layer][:, 4 * j:4 * j + 4, 0:512])
                with sp.Fori(0, FF // 512 - 1) as i:
                    for j in range(4):
                        load(sp, at + 4 + j, 8, i,
                             up_src[layer][:, 4 * j:4 * j + 4, bass.ds(i * 512 + 512, 512)])
                    for cb in range(CB):
                        load(sp, at + 8 + cb, 8, i,
                             down_src[layer][:, bass.ds(i * 4, 4), cb * 512:(cb + 1) * 512])
                for cb in range(CB):
                    load(sp, at + MLP_SLOTS - 4 + cb, 0, 0,
                         down_src[layer][:, FF // P - 4:FF // P, cb * 512:(cb + 1) * 512])

            mlp(MLP0_AT, 0)
            for u, g in enumerate((1, 2, 0)):
                for j in range(4):
                    load(sp, CONV_AT + 4 * u + j, 0, 0,
                         cin[:, 4 * j:4 * j + 4, g * D:g * D + 512])
            with sp.Fori(0, CB - 1) as i:
                for u, g in ((0, 1), (1, 2)):
                    for j in range(4):
                        load(sp, CONV_AT + 12 + 4 * u + j, 16, i,
                             cin[:, 4 * j:4 * j + 4, bass.ds(i * 512 + (g * D + 512), 512)])
                for cb in range(CB):
                    load(sp, CONV_AT + 20 + cb, 16, i,
                         cout[:, bass.ds(i * 4, 4), cb * 512:(cb + 1) * 512])
                for j in range(4):
                    load(sp, CONV_AT + 24 + j, 16, i,
                         cin[:, 4 * j:4 * j + 4, bass.ds(i * 512 + 512, 512)])
            for cb in range(CB):
                load(sp, CONV_AT + CONV_SLOTS - 4 + cb, 0, 0,
                     cout[:, KT - 4:KT, cb * 512:(cb + 1) * 512])
            mlp(MLP1_AT, 1)
            sp.wait_ge(lo_ready, 2 * (TOTAL - 4) + 2)
            sp.dma_start(raw[:, 0], final_norm_g.rearrange("(a c n) -> a c n", a=1, n=512)
                         .broadcast_to([P, 4, 512])).then_inc(fin_rows, 16)
            for cb in range(CB):
                for tt in range(NT):
                    sp.wait_ge(fin_ready, cb * NT + tt + 1)
                    sp.dma_start(out[0, tt * P:(tt + 1) * P, cb * 512:(cb + 1) * 512],
                                 h[:, tt, cb * 512:(cb + 1) * 512]).then_inc(stored, 16)
            sp.wait_ge(stored, 16 * CB * NT)

        @block.gpsimd
        def _(pool):
            nc.gpsimd.memset(ident[:], 1.0).then_inc(const_pool, 1)
            pool.wait_ge(const_pool, 1)
            nc.gpsimd.affine_select(out=ident[:], in_=ident[:], compare_op=ALU.is_equal, fill=0.0,
                                    base=0, pattern=[[-1, P]], channel_multiplier=1
                                    ).then_inc(const_pool, 1)
            nc.gpsimd.memset(minus_half[:], -0.5).then_inc(const_pool, 1)
            nc.gpsimd.iota(sm[:, :, 0, :], pattern=[[P, NT], [-1, T]], base=0, channel_multiplier=1,
                           allow_small_or_imprecise_dtypes=True).then_inc(const_pool, 1)
            pool.wait_ge(const_pool, 4)
            nc.gpsimd.tensor_scalar(sm[:, :, 1, :], sm[:, :, 0, :], 0.0, None, ALU.max
                                    ).then_inc(const_pool, 1)
            nc.gpsimd.tensor_scalar(bias[:], sm[:, :, 0, :], 0.0, None, ALU.min
                                    ).then_inc(const_pool, 1)
            pool.wait_ge(const_pool, 6)
            nc.gpsimd.tensor_tensor(bias[:], bias[:], sm[:, :, 1, :], ALU.subtract
                                    ).then_inc(const_pool, 1)
            pool.wait_ge(const_pool, 7)
            nc.gpsimd.tensor_scalar(bias[:], bias[:], 0.5, None, ALU.mult).then_inc(const_pool, 1)
            nc.gpsimd.memset(even[:], 1.0).then_inc(const_pool, 1)
            nc.gpsimd.memset(odd[:], 1.0).then_inc(const_pool, 1)
            nc.gpsimd.memset(mask[:], 1.0).then_inc(const_pool, 1)
            done = 11
            pool.wait_ge(const_pool, done)

            def rstd_of(n):
                pool.wait_ge(sq_sum, n + 1)
                nc.gpsimd.tensor_scalar(meansq[:], meansq[:], 1.0 / D, EPS, ALU.mult, ALU.add
                                        ).then_inc(rstd_step, 1)
                pool.wait_ge(rstd_step, 2 * n + 1)
                nc.gpsimd.tensor_tensor(rstd[:, n], meansq[:], minus_half[:, 0:NT], ALU.pow
                                        ).then_inc(rstd_step, 1)

            rstd_of(0)
            for d in range(2):
                for lv in range(7):
                    m = LEVELS[lv]
                    part = mask[:, d, lv].rearrange("p (a b) -> p a b", b=m)
                    lo = m * d
                    nc.gpsimd.affine_select(out=part, in_=part, compare_op=ALU.is_ge, fill=0.0,
                                            base=-lo, pattern=[[-2 * m, 64 // m], [0, m]],
                                            channel_multiplier=1).then_inc(const_pool, 1)
                    done += 1
                    pool.wait_ge(const_pool, done)
                    nc.gpsimd.affine_select(out=part, in_=part, compare_op=ALU.is_ge, fill=0.0,
                                            base=lo + m - 1, pattern=[[2 * m, 64 // m], [0, m]],
                                            channel_multiplier=-1).then_inc(const_pool, 1)
                    done += 1

            assert done == CONST_ALL

            def mix(n):
                def mark(ins, name):
                    assert mix_pool.names[marks[0]] == name
                    marks[0] += 1
                    ins.then_inc(mix_pool.sem, 1)

                marks = [0]

                def own(name):
                    pool.wait_ge(mix_pool.sem, mix_pool.at(name, n))

                pool.wait_ge(mix_act.sem, mix_act.at("sig_hg", n))
                mark(nc.gpsimd.tensor_tensor(silu[:], silu[:], proj_b[:, :, 1], ALU.mult), "silu")
                pool.wait_ge(mix_dve.sem, mix_dve.at("kin", n))
                mark(nc.gpsimd.tensor_tensor(kin_sum[:], kin[:, 0], kin[:, 1], ALU.add), "kin_sum")

                def tree(lv):
                    first, second = both(even, lv - 1)[:, :, :, 1], both(odd, lv - 1)[:, :, :, 0]
                    nc.gpsimd.tensor_tensor(both(even, lv)[:, :, :, 1], first[:, :, 0::2],
                                            second[:, :, 0::2], ALU.mult)
                    mark(nc.gpsimd.tensor_tensor(both(odd, lv)[:, :, :, 0], first[:, :, 1::2],
                                                 second[:, :, 1::2], ALU.mult), f"tree{LEVELS[lv]}")

                def k_level(d, lv):
                    m = LEVELS[lv - 1]
                    src = kin[:, d] if lv == 1 else lk[:, lv - 2]
                    factor = flat(odd if d == 0 else even, d, lv - 1)
                    mark(nc.gpsimd.tensor_tensor(
                        lk[:, lv - 1].rearrange("p (a b) -> p a b", b=m),
                        src.rearrange("p (a b) -> p a b", b=m),
                        factor.unsqueeze(2).broadcast_to([P, T // m, m]), ALU.mult),
                        f"K{'FB'[d]}{LEVELS[lv]}")

                pool.wait_ge(mix_dve.sem, mix_dve.at("tree1", n))
                tree(1)
                own("tree2")
                tree(2)
                for lv in range(1, 4):
                    own("tree4" if lv == 1 else f"KF{LEVELS[lv - 1]}")
                    k_level(0, lv)
                pool.wait_ge(mix_dve.sem, mix_dve.at("max", n))
                stand_alone(pool, n)
                mark(nc.gpsimd.tensor_scalar(neg_mx[:], mx[:], -1.0, None, ALU.mult), "neg_mx")
                for lv in range(3, 7):
                    own(f"tree{LEVELS[lv - 1]}")
                    tree(lv)
                for lv in range(4, 8):
                    own("tree64" if lv == 4 else f"KF{LEVELS[lv - 1]}")
                    k_level(0, lv)
                for lv in range(1, 8):
                    if lv > 1:
                        own(f"KB{LEVELS[lv - 1]}")
                    pool.wait_ge(mix_pe.sem, mix_pe.at("F0" if lv < 4 else "F1", n))
                    k_level(1, lv)
                pool.wait_ge(mix_dve.sem, mix_dve.at("s", n))
                stand_alone(pool, n)
                mark(nc.gpsimd.tensor_scalar(bias[:], bias[:], 0.5, None, ALU.mult), "bias")
                pool.wait_ge(mix_act.sem, mix_act.at("osq", n))
                stand_alone(pool, n)
                mark(nc.gpsimd.tensor_scalar(osq[:], osq[:], 1.0 / P, EPS, ALU.mult, ALU.add),
                     "o_ms")
                own("o_ms")
                mark(nc.gpsimd.tensor_tensor(orstd[:], osq[:], minus_half[:], ALU.pow), "o_rstd")
                assert marks[0] == len(mix_pool.names)

            pool.wait_ge(const_pool, CONST_ALL)
            pool.wait_ge(par_dve, PAR_LB)
            with pool.Fori(0, HEADS - 1) as i:
                mix(i)
            mix(HEADS - 1)
            for n in range(1, 5):
                rstd_of(n)

        def gain_transpose_pe(n, cb):
            if n == 0:
                nc.tensor.wait_ge(x_in[cb], 16)
            else:
                last = {1: PAIR_L0, 2: PAIR_MLP0, 3: PAIR_CONV}[n]
                nc.tensor.wait_ge(pair_read[cb % 2], last - 1 + cb // 2)
            for b in range(2):
                if cb:
                    nc.tensor.wait_ge(norm_lo[n], 2 * (cb - 1) + b + 1)
                for q in range(2):
                    kt = 4 * cb + 2 * b + q
                    for tt in range(NT):
                        ins = nc.tensor.transpose(M[b][:, q * T + tt * P:q * T + (tt + 1) * P],
                                                  h[:, tt, kt * P:(kt + 1) * P], ident[:])
                ins.then_inc(norm_T[n], 1)

        def before_slot(n, j):
            if n == 0 and j == 0:
                gain_transpose_pe(0, 0)
                gain_transpose_pe(0, 1)
            if j:
                if j < 3:
                    gain_transpose_pe(n, j + 1)
            nc.tensor.wait_ge(norm_lo[n], 2 * j + 2)

        @block.tensor
        def _(pe):
            pe.wait_ge(const_pool, 2)
            pe.wait_ge(rows_in, 16 * ROWS_DMAS)
            nc.tensor.transpose(M[3][:, 0:121], rows_a[0:121, :], ident[0:121, 0:121])
            nc.tensor.transpose(M[3][:, 128:176], rows_b[:, :], ident[0:48, 0:48]
                                ).then_inc(rows_T, 1)
            pe.wait_ge(par_act, 1)
            def head_product(c, j, base, step, i, n, ks=(0, 1)):
                if j == 0 and 0 in ks and not isinstance(n, int):
                    pe.wait_ge(pair_read[c], n)
                multiply(pe, base, step, i, xT_hi, xT_lo, 4 * j, pair[c], j == 0, j == 3, ks)

            def hook(k, n):
                def mark(ins, name):
                    assert name in mix_pe.names
                    ins.then_inc(mix_pe.sem, 1)

                def levels(d, group):
                    bank = M[3] if group == 0 else M[2]
                    for g in range(4):
                        lv = 4 * group + g
                        m = LEVELS[lv]
                        keys = kin[:, d] if lv == 0 else lk[:, lv - 1]
                        if m == 128:
                            s_at, t_at = (0, P) if d == 0 else (P, 0)
                            ins = nc.tensor.matmul(bank[:, g * P:(g + 1) * P], keys[:, s_at:s_at + P],
                                                   lq[:, lv, t_at:t_at + P], start=True, stop=True)
                            continue
                        for tile in range(NT):
                            t_half = lq[:, lv, tile * P:(tile + 1) * P].rearrange(
                                "p (a b c) -> p a b c", b=2, c=m)[:, :, 1 - d]
                            ins = nc.tensor.matmul(
                                bank[:, g * P + tile * 64:g * P + (tile + 1) * 64]
                                .rearrange("p (a c) -> p a c", c=m),
                                keys[:, tile * P:(tile + 1) * P], t_half, start=True, stop=True)
                    return ins

                if k == 1:
                    pe.wait_ge(pair_read[0], n + 1)
                    pe.wait_ge(pair_read[1], n + 1)
                    for bank, src, gs, name in ((M[1], proj_b, (2, 3), "gateT"),
                                                (M[0], proj_a, (0, 1), "qkT"),
                                                (M[2], proj_a, (3,), "hqT")):
                        for at, g in enumerate(gs):
                            for tt in range(NT):
                                ins = nc.tensor.transpose(
                                    bank[:, at * T + tt * P:at * T + (tt + 1) * P], src[:, tt, g],
                                    ident[:])
                        mark(ins, name)
                if k == 2:
                    pe.wait_ge(mix_act.sem, mix_act.at("qkT", n))
                    for mp in range(2):
                        part = slice(mp * DA, (mp + 1) * DA)
                        for tt in range(NT):
                            ins = nc.tensor.matmul(M[mp][:, tt * T:(tt + 1) * T],
                                                   qkT[part, 0, tt * P:(tt + 1) * P], qkT[part, 1],
                                                   start=True, stop=True)
                        mark(ins, f"S{mp}")
                if k == 3:
                    pe.wait_ge(mix_act.sem, mix_act.at("hqT", n))
                    pe.wait_ge(mix_pool.sem, mix_pool.at("kin_sum", n))
                    for tile in range(NT):
                        cols = slice(tile * P, (tile + 1) * P)
                        ins = nc.tensor.matmul(M[2][:, cols], kin_sum[:, cols], hqT[:, cols],
                                               start=True, stop=True)
                    mark(ins, "diag")
                    pe.wait_ge(mix_pool.sem, mix_pool.at("KF8", n))
                    pe.wait_ge(mix_dve.sem, mix_dve.at("QF8", n))
                    mark(levels(0, 0), "F0")
                if k == 4:
                    pe.wait_ge(mix_pool.sem, mix_pool.at("KF128", n))
                    pe.wait_ge(mix_dve.sem, mix_dve.at("QF128", n))
                    mark(levels(0, 1), "F1")
                if k == 5:
                    pe.wait_ge(mix_pool.sem, mix_pool.at("KB8", n))
                    pe.wait_ge(mix_dve.sem, mix_dve.at("QB8", n))
                    mark(levels(1, 0), "B0")
                    for st in range(NT):
                        for tt in range(NT):
                            ins = nc.tensor.transpose(M[0][:, st * T + tt * P:st * T + (tt + 1) * P],
                                                      sm[:, tt, 0, st * P:(st + 1) * P], ident[:])
                    mark(ins, "aT")
                if k == 6:
                    pe.wait_ge(mix_pool.sem, mix_pool.at("KB128", n))
                    pe.wait_ge(mix_dve.sem, mix_dve.at("QB128", n))
                    mark(levels(1, 1), "B1")
                if k == 7:
                    pe.wait_ge(mix_act.sem, mix_act.at("aT", n))
                    pe.wait_ge(mix_dve.sem, mix_dve.at("PB1", n))
                    for g, rhs in enumerate((proj_a[:, :, 2], proj_b[:, :, 0])):
                        for tt in range(NT):
                            for st in range(NT):
                                lhs = (aT[:, st, tt * P:(tt + 1) * P] if g == 0 else
                                       att[:, st, int(st != tt)])
                                ins = nc.tensor.matmul(
                                    M[0][:, (2 * g + tt) * P:(2 * g + tt + 1) * P], lhs, rhs[:, st],
                                    start=st == 0, stop=st == NT - 1)
                    mark(ins, "oAB")
                if k == 8:
                    pe.wait_ge(mix_dve.sem, mix_dve.at("on", n))
                    for g in range(4):
                        ins = nc.tensor.transpose(M[3][:, g * P:(g + 1) * P], on[:, g], ident[:])
                    mark(ins, "oT")

            for c in range(2):
                for j in range(4):
                    if c == 0:
                        before_slot(0, j)
                    head_product(c, j, 4 * c + j, 0, 0, 0)
            with pe.Fori(0, HEADS - 1) as i:
                for q in range(16):
                    if q in MIX_AT:
                        hook(MIX_AT[q], i)
                    p = q // 2
                    head_product(p // 4, p % 4, 8 + p, 8, i, i + 1, (q % 2,))
                hook(MIX_AT[16], i)
            for q in range(2 * len(OUT_ORDER)):
                p = q // 2
                cb, j = OUT_ORDER[p]
                if q in LAST_MIX_AT:
                    hook(LAST_MIX_AT[q], HEADS - 1)
                if q == 12:
                    pe.wait_ge(mix_dve.sem, mix_dve.at("lo", HEADS - 1))
                if q == 0:
                    pe.wait_ge(mix_dve.sem, mix_dve.at("lo", HEADS - 2))
                if j == 0 and q % 2 == 0:
                    pe.wait_ge(pair_read[cb % 2], HEADS + cb // 2)
                if q % 2 == 0 and p >= 14:
                    gain_transpose_pe(1, p - 14)
                multiply(pe, OUT_AT + p, 0, 0, yT_hi, yT_lo, 4 * j, pair[cb % 2], j == 0, j == 3,
                         (q % 2,))

            def mlp(at, layer, norm):
                before = [PAIR_L0, PAIR_CONV][layer]

                def up(p, base, step, i, n, first=False):
                    if first:
                        before_slot(norm, p)
                    elif p == 0:
                        pe.wait_ge(up_relu[layer], n * NT)
                    multiply(pe, base, step, i, xT_hi, xT_lo, 4 * p, m23, p == 0, p == 3)

                def hidden_T(n):
                    pe.wait_ge(up_sq[layer], n * NT + NT)
                    for b in range(2):
                        for q in range(2):
                            for tt in range(NT):
                                ins = nc.tensor.transpose(
                                    M[b][:, q * T + tt * P:q * T + (tt + 1) * P],
                                    act[:, tt, (2 * b + q) * P:(2 * b + q + 1) * P], ident[:])
                        ins.then_inc(hT_done[layer], 1)

                def down(cb, base, step, i, n):
                    if cb == 0:
                        pe.wait_ge(hT_lo[layer], n * 2 + 2)
                    pe.wait_ge(pair_read[cb % 2], n * 2 + (before + cb // 2))
                    multiply(pe, base, step, i, yT_hi, yT_lo, 0, pair[cb % 2], True, True)

                for p in range(4):
                    up(p, at + p, 0, 0, 0, first=True)
                blocks_n = FF // 512
                with pe.Fori(0, blocks_n - 1) as i:
                    for p in range(8):
                        if p == 2:
                            hidden_T(i)
                        if p < 4:
                            up(p, at + 4 + p, 8, i, i + 1)
                        else:
                            down(p - 4, at + 4 + p, 8, i, i)
                hidden_T(blocks_n - 1)
                for cb in range(CB):
                    if layer == 0 and cb >= 2:
                        gain_transpose_pe(2, cb - 2)
                    down(cb, at + MLP_SLOTS - 4 + cb, 0, 0, blocks_n - 1)

            mlp(MLP0_AT, 0, 1)

            def conv_in(which, j, base, step, i, n, first=False):
                if first and which == "c":
                    before_slot(2, j)
                if j == 0:
                    if which == "b":
                        if not first:
                            pe.wait_ge(b_read, n)
                    else:
                        pe.wait_ge(pair_read["ch".index(which)],
                                   PAIR_MLP0 if first else n * 3 + (PAIR_MLP0 - 2))
                dst = {"c": pair[0], "h": pair[1], "b": m23}[which]
                multiply(pe, base, step, i, xT_hi, xT_lo, 4 * j, dst, j == 0, j == 3)

            def conv_T(src, done):
                for b in range(2):
                    for q in range(2):
                        for tt in range(NT):
                            ins = nc.tensor.transpose(
                                M[b][:, q * T + tt * P:q * T + (tt + 1) * P],
                                src[:, tt, (2 * b + q) * P:(2 * b + q + 1) * P], ident[:])
                    ins.then_inc(done, 1)

            def u_T(n):
                pe.wait_ge(pair_read[1], n * 3 + (PAIR_MLP0 + 1))
                conv_T(cg, uT_done)

            def b_T(n):
                pe.wait_ge(b_read, n + 1)
                pe.wait_ge(uT_read, n * 2 + 2)
                conv_T(bg, bT_done)

            def conv_out(cb, base, step, i, n):
                if cb == 0:
                    pe.wait_ge(cv_lo, n + 1)
                more = 0 if isinstance(n, int) else 1
                pe.wait_ge(pair_read[cb % 2], n * 3 + (PAIR_MLP0 + 1 + more + cb // 2))
                multiply(pe, base, step, i, yT_hi, yT_lo, 0, pair[cb % 2], True, True)

            for u, which in enumerate("chb"):
                for j in range(4):
                    conv_in(which, j, CONV_AT + 4 * u + j, 0, 0, 0, first=True)
            with pe.Fori(0, CB - 1) as i:
                for p in range(16):
                    if p == 1:
                        u_T(i)
                    if p == 2:
                        b_T(i)
                    at = CONV_AT + 12 + p
                    if p < 4:
                        conv_in("c", p, at, 16, i, i + 1)
                    elif p < 8:
                        conv_in("h", p - 4, at, 16, i, i + 1)
                    elif p < 12:
                        conv_out(p - 8, at, 16, i, i)
                    else:
                        conv_in("b", p - 12, at, 16, i, i + 1)
            u_T(CB - 1)
            b_T(CB - 1)
            for cb in range(CB):
                if cb >= 2:
                    gain_transpose_pe(3, cb - 2)
                conv_out(cb, CONV_AT + CONV_SLOTS - 4 + cb, 0, 0, CB - 1)

            mlp(MLP1_AT, 1, 3)

        @block.scalar
        def _(eng):
            for at, n, src in ((G_MIX, 32, mix_norm_g.rearrange("a (k p) -> (a k) p", p=P)),
                               (G_MLP, 32, mlp_norm_g.rearrange("a (k p) -> (a k) p", p=P)),
                               (G_CONV, 48, conv_w[0].rearrange("a (k p) -> (a k) p", p=P)),
                               (G_HGRN, 8, hgrn_norm_g[0].rearrange("(k p) -> k p", p=P)),
                               (G_SUB, 1, diff_subln_g)):
                eng.dma_start(rows_a[at:at + n, :], src).then_inc(rows_in, 16)
            eng.dma_start(rows_b[:, :], hgrn_lb.rearrange("a b (k p) -> (a b k) p", p=P)
                          ).then_inc(rows_in, 16)
            eng.dma_start(lam4[:].rearrange("p a b -> p (a b)"),
                          diff_lambda[0].rearrange("(o a) b -> o (a b)", o=1).broadcast_to([P, 4 * DA])
                          ).then_inc(lam_in, 16)

            def norm_hi_of(n, cb):
                for b in range(2):
                    eng.wait_ge(norm_T[n], 2 * cb + b + 1)
                    for q in range(2):
                        kt = 4 * cb + 2 * b + q
                        ins = nc.scalar.activation(
                            xT_hi[:, kt], M[b][:, q * T:(q + 1) * T], ACT.Copy,
                            scale=gains[:, GAIN_OF[n] + kt:GAIN_OF[n] + kt + 1])
                    ins.then_inc(norm_hi[n], 1)

            def squares(n, cbs):
                for cb in cbs:
                    for tt in range(NT):
                        if (cb, tt) != (0, 0) or n:
                            eng.wait_ge(sq_done, (n * CB + cb) * NT + tt)
                        ins = nc.scalar.activation(junk, h[:, tt, cb * 512:(cb + 1) * 512],
                                                   ACT.Square, accum_out=sumsq[:, tt, cb:cb + 1])
                        ins.then_inc(sq_done, 1)

            def copy_product(c, n):
                wait_product(eng, PROJ_AT + 4 * c + 3, 8, n)
                for tt in range(NT):
                    ins = nc.scalar.activation([proj_a, proj_b][c][:, tt],
                                               pair[c][:, tt].rearrange("p (g n) -> p g n", g=4),
                                               ACT.Copy, scale=rstd[:, 0, tt:tt + 1])
                ins.then_inc(pair_read[c], 1)

            def hook(k, n):
                def mark(ins, name):
                    assert name in mix_act.names
                    ins.then_inc(mix_act.sem, 1)

                if k == 0:
                    eng.wait_ge(pair_read[1], n + 1)
                    mark(nc.scalar.activation(silu[:], proj_b[:, :, 1], ACT.Sigmoid), "sig_hg")
                if k == 1:
                    eng.wait_ge(mix_pe.sem, mix_pe.at("gateT", n))
                    z = M[1].rearrange("p (a b) -> p a b", a=2)
                    mark(nc.scalar.activation(kin[:], z, ACT.Sigmoid, scale=-1.0), "sig_neg")
                    mark(nc.scalar.activation(gate[:], z, ACT.Sigmoid), "sig_pos")
                    eng.wait_ge(mix_pe.sem, mix_pe.at("qkT", n))
                    mark(nc.scalar.activation(qkT[:], M[0].rearrange("p (a b) -> p a b", a=2),
                                              ACT.Copy), "qkT")
                    eng.wait_ge(mix_pe.sem, mix_pe.at("hqT", n))
                    mark(nc.scalar.activation(hqT[:], M[2][:, 0:T], ACT.Copy), "hqT")
                if k == 2:
                    eng.wait_ge(mix_pool.sem, mix_pool.at("neg_mx", n))
                    for tt in range(NT):
                        for mp in range(2):
                            c = 2 * tt + mp
                            ins = nc.scalar.activation(sm[:, tt, mp], sm[:, tt, mp], ACT.Exp,
                                                       bias=neg_mx[:, c:c + 1],
                                                       accum_out=rowsum[:, c:c + 1])
                    mark(ins, "exp_s")
                if k == 5:
                    eng.wait_ge(mix_pe.sem, mix_pe.at("aT", n))
                    mark(nc.scalar.activation(aT[:], M[0].rearrange("p (a b) -> p a b", a=NT),
                                              ACT.Copy), "aT")
                if k == 7:
                    eng.wait_ge(mix_pe.sem, mix_pe.at("oAB", n))
                    for g in range(4):
                        ins = nc.scalar.activation(on[:, g], M[0][:, g * P:(g + 1) * P], ACT.Square,
                                                   accum_out=osq[:, g:g + 1])
                    mark(ins, "osq")
                if k == 8:
                    eng.wait_ge(mix_pe.sem, mix_pe.at("oT", n))
                    for g, name in enumerate(("hi_a", "hi_b")):
                        mark(nc.scalar.activation(row(yT_hi, n * 2 + g), M[3][:, g * T:(g + 1) * T],
                                                  ACT.Copy, scale=out_gain(g, n)), name)

            eng.wait_ge(rows_T, 1)
            nc.scalar.activation(gains[:, 0:121], M[3][:, 0:121], ACT.Copy)
            nc.scalar.activation(lbt[:].rearrange("p a b c -> p (a b c)"), M[3][:, 128:176], ACT.Copy
                                 ).then_inc(par_act, 1)
            eng.wait_ge(par_act, 1)
            norm_hi_of(0, 0)
            for n in range(2):
                split_hi(eng, n, 0, 0)
                if n == 0:
                    norm_hi_of(0, 1)
            eng.wait_ge(par_dve, 4)
            nc.scalar.activation(lbt[:], lbt[:], ACT.Exp).then_inc(par_act, 1)
            nc.scalar.activation(lam_sum[:], lam_sum[:], ACT.Exp).then_inc(par_act, 1)
            for p in range(8):
                if p in (1, 2):
                    norm_hi_of(0, p + 1)
                    squares(0, (2 * p - 2, 2 * p - 1))
                if p == 5:
                    eng.wait_ge(rstd_step, 2)
                    copy_product(0, 0)
                split_hi(eng, p + 2, 0, 0)
            with eng.Fori(0, HEADS - 1) as i:
                copy_product(1, i)
                hook(0, i)
                for q in range(16):
                    if q in MIX_AT:
                        hook(MIX_AT[q], i)
                    if q == 15:
                        copy_product(0, i + 1)
                    split_hi(eng, 8 + q // 2 + 2, 8, i, (q % 2,))
                hook(MIX_AT[16], i)
            copy_product(1, HEADS - 1)
            hook(0, HEADS - 1)
            for q in range(32):
                if q in LAST_MIX_AT:
                    hook(LAST_MIX_AT[q], HEADS - 1)
                if q in (28, 30):
                    norm_hi_of(1, q // 2 - 14)
                split_hi(eng, OUT_AT + q // 2 + 2, 0, 0, (q % 2,))

            def mlp(at, layer, norm):
                rows = rstd[:, norm]

                def rectify(n, *position):
                    wait_product(eng, *position)
                    for tt in range(NT):
                        nc.scalar.activation(act[:, tt], m23[:, tt], ACT.Relu,
                                             scale=rows[:, tt:tt + 1]).then_inc(up_relu[layer], 1)
                    for tt in range(NT):
                        eng.wait_ge(up_relu[layer], n * NT + (tt + 1))
                        nc.scalar.activation(act[:, tt], act[:, tt], ACT.Square
                                             ).then_inc(up_sq[layer], 1)

                def hidden_hi(n):
                    for b in range(2):
                        eng.wait_ge(hT_done[layer], n * 2 + (b + 1))
                        nc.scalar.activation(yT_hi[:, 2 * b:2 * b + 2],
                                             M[b].rearrange("p (a b) -> p a b", a=2), ACT.Copy
                                             ).then_inc(hT_hi[layer], 1)

                for p in range(4):
                    if p in (1, 2):
                        norm_hi_of(norm, p + 1)
                        squares(norm, (2 * p - 2, 2 * p - 1))
                    split_hi(eng, at + p + 2, 0, 0)
                eng.wait_ge(rstd_step, 2 * norm + 2)
                rectify(0, at + 3, 0, 0)
                with eng.Fori(0, FF // 512 - 1) as i:
                    for p in range(8):
                        if p == 2:
                            hidden_hi(i)
                        if p == 4:
                            rectify(i + 1, at + 7, 8, i)
                        split_hi(eng, at + 4 + p + 2, 8, i)
                hidden_hi(FF // 512 - 1)
                for cb in range(CB):
                    if layer == 0 and cb >= 2:
                        norm_hi_of(2, cb - 2)
                    split_hi(eng, at + MLP_SLOTS - 4 + cb + 2, 0, 0)

            mlp(MLP0_AT, 0, 1)

            def copy_gate(read, dst, src, position):
                wait_product(eng, *position)
                for tt in range(NT):
                    ins = nc.scalar.activation(dst[:, tt], src[:, tt], ACT.Copy,
                                               scale=rstd[:, 2, tt:tt + 1])
                ins.then_inc(read, 1)

            def c_gate(*position):
                copy_gate(pair_read[0], cg, pair[0], position)

            def b_gate(*position):
                copy_gate(b_read, bg, m23, position)

            def copy_uT(n):
                for b in range(2):
                    eng.wait_ge(uT_done, n * 2 + (b + 1))
                    nc.scalar.activation(uT[:, 2 * b:2 * b + 2],
                                         M[b].rearrange("p (a b) -> p a b", a=2), ACT.Copy
                                         ).then_inc(uT_read, 1)

            def conv_hi(n):
                eng.wait_ge(cv_step, n * CONV_STEPS + CONV_STEPS)
                nc.scalar.activation(yT_hi[:, 0:4], cT, ACT.Copy).then_inc(cv_hi, 1)

            for p in range(12):
                if p in (1, 2):
                    norm_hi_of(2, p + 1)
                    squares(2, (2 * p - 2, 2 * p - 1))
                if p == 5:
                    eng.wait_ge(rstd_step, 6)
                    c_gate(CONV_AT + 3, 0, 0)
                split_hi(eng, CONV_AT + p + 2, 0, 0)
            b_gate(CONV_AT + 11, 0, 0)
            with eng.Fori(0, CB - 1) as i:
                for p in range(16):
                    if p == 2:
                        copy_uT(i)
                    if p == 4:
                        c_gate(CONV_AT + 15, 16, i)
                    if p == 6:
                        conv_hi(i)
                    split_hi(eng, CONV_AT + 12 + p + 2, 16, i)
                b_gate(CONV_AT + 27, 16, i)
            copy_uT(CB - 1)
            conv_hi(CB - 1)
            for cb in range(CB):
                if cb >= 2:
                    norm_hi_of(3, cb - 2)
                split_hi(eng, CONV_AT + CONV_SLOTS - 4 + cb + 2, 0, 0)

            mlp(MLP1_AT, 1, 3)
            for cb in range(CB):
                eng.wait_ge(pair_read[cb % 2], PAIR_MLP1 - 1 + cb // 2)
                squares(4, (cb,))

        @block.vector
        def _(dve):
            def norm_lo_of(n, cb):
                for b in range(2):
                    dve.wait_ge(norm_hi[n], 2 * cb + b + 1)
                    for q in range(2):
                        kt = 4 * cb + 2 * b + q
                        ins = nc.vector.scalar_tensor_tensor(
                            out=xT_lo[:, kt], in0=M[b][:, q * T:(q + 1) * T],
                            scalar=gains[:, GAIN_OF[n] + kt:GAIN_OF[n] + kt + 1],
                            in1=xT_hi[:, kt].bitcast(F32), op0=ALU.mult, op1=ALU.subtract)
                    ins.then_inc(norm_lo[n], 1)

            def sum_squares(n):
                dve.wait_ge(sq_done, (n + 1) * NT * CB)
                if n:
                    dve.wait_ge(rstd_step, 2 * n)
                nc.vector.tensor_reduce(meansq[:], sumsq[:], AX_X, ALU.add).then_inc(sq_sum, 1)

            def add_block(cb, *position):
                wait_product(dve, *position)
                cols = slice(cb * 512, (cb + 1) * 512)
                for tt in range(NT):
                    ins = nc.vector.tensor_tensor(h[:, tt, cols], pair[cb % 2][:, tt], h[:, tt, cols],
                                                  ALU.add)
                ins.then_inc(pair_read[cb % 2], 1)

            def hook(k, n):
                def mark(ins, name):
                    assert name in mix_dve.names
                    order.append(name)
                    ins.then_inc(mix_dve.sem, 1)

                def own(name):
                    dve.wait_ge(mix_dve.sem, mix_dve.at(name, n))

                def q_level(d, lv):
                    if lv == 0:
                        mark(nc.vector.tensor_tensor(lq[:, 0], hqT[:], gate[:, d], ALU.mult),
                             f"Q{'FB'[d]}1")
                        return
                    m = LEVELS[lv - 1]
                    own(f"Q{'FB'[d]}{m}")
                    factor = flat(even if d == 0 else odd, d, lv - 1)
                    mark(nc.vector.tensor_tensor(
                        lq[:, lv].rearrange("p (a b) -> p a b", b=m),
                        lq[:, lv - 1].rearrange("p (a b) -> p a b", b=m),
                        factor.unsqueeze(2).broadcast_to([P, T // m, m]), ALU.mult),
                        f"Q{'FB'[d]}{2 * m}")

                def pick(d, group):
                    bank = M[3] if group == 0 else M[2]
                    for g in range(4):
                        lv = 4 * group + g
                        m = LEVELS[lv]
                        if m == 128:
                            ins = nc.vector.tensor_copy(att[:, d, 1], bank[:, g * P:(g + 1) * P])
                            continue
                        stand_alone(dve, n)
                        dst = att[:, :, 0].rearrange("p t (a b c) -> p t a b c", b=2, c=m)[
                            :, :, :, 1 - d]
                        ins = nc.vector.copy_predicated(
                            dst, mask[:, d, lv].bitcast(U32).rearrange("p (a c) -> p a c", c=m)
                            .unsqueeze(1).broadcast_to([P, NT, 64 // m, m]),
                            bank[:, g * P:(g + 1) * P].rearrange("p (t a c) -> p t a c", t=NT, c=m))
                        if g < 3:
                            ins.then_inc(picked, 1)
                            dve.wait_ge(picked, n * 12 + ((2 * d + group) * 3 + g + 1))
                    mark(ins, f"P{'FB'[d]}{group}")

                if k == 1:
                    dve.wait_ge(mix_act.sem, mix_act.at("sig_neg", n))
                    for d in range(2):
                        ins = nc.vector.tensor_scalar(kin[:, d], kin[:, d], lb_col(one_lb, n, d),
                                                      None, ALU.mult)
                    mark(ins, "kin")
                    dve.wait_ge(mix_act.sem, mix_act.at("sig_pos", n))
                    for d in range(2):
                        ins = nc.vector.tensor_scalar(gate[:, d], gate[:, d], lb_col(one_lb, n, d),
                                                      lb_col(lb, n, d), ALU.mult, ALU.add)
                    mark(ins, "f")
                    own("f")
                    f_pairs = gate[:, :, :].rearrange("p d (a b) -> p d a b", b=2)
                    nc.vector.tensor_copy(both(even, 0)[:, :, :, 1], f_pairs[:, :, :, 0])
                    mark(nc.vector.tensor_copy(both(odd, 0)[:, :, :, 0], f_pairs[:, :, :, 1]),
                         "tree1")
                if k == 2:
                    for mp in range(2):
                        dve.wait_ge(mix_pe.sem, mix_pe.at(f"S{mp}", n))
                        if mp == 0:
                            dve.wait_ge(mix_pool.sem, mix_pool.at("kin_sum", n))
                        ins = nc.vector.scalar_tensor_tensor(
                            out=sm[:, :, mp], in0=M[mp].rearrange("p (a b) -> p a b", a=2),
                            scalar=DA ** -0.5, in1=bias[:], op0=ALU.mult, op1=ALU.add)
                    mark(ins, "s")
                    own("s")
                    mark(nc.vector.tensor_reduce(mx[:], sm[:].rearrange("p a b c -> p (a b) c"),
                                                 AX_X, ALU.max), "max")
                    dve.wait_ge(mix_act.sem, mix_act.at("hqT", n))
                    for lv in range(4):
                        if lv == 1:
                            dve.wait_ge(mix_pool.sem, mix_pool.at("tree4", n))
                        q_level(0, lv)
                if k == 3:
                    dve.wait_ge(const_pool, CONST_ALL)
                    dve.wait_ge(mix_pe.sem, mix_pe.at("diag", n))
                    mark(nc.vector.tensor_copy(att[:, :, 0], M[2][:, 0:T].rearrange(
                        "p (a b) -> p a b", a=NT)), "diag")
                    dve.wait_ge(mix_act.sem, mix_act.at("exp_s", n))
                    mark(nc.vector.reciprocal(rinv[:], rowsum[:]), "r_inv")
                    own("r_inv")
                    mark(nc.vector.tensor_scalar(neg_lr[:], rinv[:].rearrange(
                        "p (a b) -> p a b", b=2)[:, :, 1], neg_lam[:, 0:1], None, ALU.mult), "neg_lr")
                    own("neg_lr")
                    for tt in range(NT):
                        ins = nc.vector.tensor_scalar(sm[:, tt, 1], sm[:, tt, 1], neg_lr[:, tt:tt + 1],
                                                      None, ALU.mult)
                    mark(ins, "a1")
                    own("a1")
                    for tt in range(NT):
                        ins = nc.vector.scalar_tensor_tensor(
                            out=sm[:, tt, 0], in0=sm[:, tt, 0], scalar=rinv[:, 2 * tt:2 * tt + 1],
                            in1=sm[:, tt, 1], op0=ALU.mult, op1=ALU.add)
                    mark(ins, "a")
                    dve.wait_ge(mix_pe.sem, mix_pe.at("F0", n))
                    own("diag")
                    pick(0, 0)
                    dve.wait_ge(mix_pool.sem, mix_pool.at("tree64", n))
                    for lv in range(4, 8):
                        q_level(0, lv)
                if k == 4:
                    dve.wait_ge(mix_pe.sem, mix_pe.at("F1", n))
                    own("PF0")
                    pick(0, 1)
                    for lv in range(4):
                        q_level(1, lv)
                if k == 5:
                    dve.wait_ge(mix_pe.sem, mix_pe.at("B0", n))
                    own("PF1")
                    pick(1, 0)
                    for lv in range(4, 8):
                        q_level(1, lv)
                if k == 6:
                    dve.wait_ge(mix_pe.sem, mix_pe.at("B1", n))
                    own("PB0")
                    pick(1, 1)
                if k == 7:
                    dve.wait_ge(mix_pool.sem, mix_pool.at("o_rstd", n))
                    for tt in range(NT):
                        nc.vector.tensor_scalar(on[:, tt], M[0][:, tt * P:(tt + 1) * P],
                                                orstd[:, tt:tt + 1], None, ALU.mult)
                    for tt in range(NT):
                        ins = nc.vector.scalar_tensor_tensor(
                            out=on[:, 2 + tt], in0=M[0][:, (2 + tt) * P:(3 + tt) * P],
                            scalar=orstd[:, 2 + tt:3 + tt], in1=silu[:, tt], op0=ALU.mult,
                            op1=ALU.mult)
                    mark(ins, "on")
                if k == 8:
                    dve.wait_ge(mix_act.sem, mix_act.at("hi_b", n))
                    for g in range(2):
                        ins = nc.vector.scalar_tensor_tensor(
                            out=row(yT_lo, n * 2 + g), in0=M[3][:, g * T:(g + 1) * T],
                            scalar=out_gain(g, n), in1=row(yT_hi, n * 2 + g).bitcast(F32),
                            op0=ALU.mult, op1=ALU.subtract)
                    mark(ins, "lo")
                    assert order == mix_dve.names, (order, mix_dve.names)
                    order.clear()

            order = []
            step = [0]

            def par(ins):
                step[0] += 1
                ins.then_inc(par_dve, 1)
                dve.wait_ge(par_dve, step[0])

            dve.wait_ge(lam_in, 16)
            par(nc.vector.tensor_tensor(lam4[:, 0::2], lam4[:, 0::2], lam4[:, 1::2], ALU.mult))
            par(nc.vector.tensor_reduce(lam_sum[:], lam4[:, 0::2], AX_X, ALU.add))
            dve.wait_ge(par_act, 1)
            par(nc.vector.tensor_reduce(lbm[:], lbt[:].rearrange("p a b c -> p a c b"), AX_X, ALU.max))
            par(nc.vector.tensor_tensor(lbt[:], lbt[:], lbm[:].unsqueeze(2).broadcast_to(
                [P, 2, 3, HEADS]), ALU.subtract))
            norm_lo_of(0, 0)
            for n in range(2):
                split_lo(dve, n, 0, 0)
                if n == 0:
                    norm_lo_of(0, 1)
            dve.wait_ge(par_act, 3)
            par(nc.vector.tensor_tensor(neg_lam[:], lam_sum[:, 1:2], lam_sum[:, 0:1], ALU.subtract))
            par(nc.vector.tensor_scalar(neg_lam[:], neg_lam[:], -LAM_INIT, None, ALU.add))
            par(nc.vector.tensor_reduce(lbs[:], lbt[:].rearrange("p a b c -> p a c b"), AX_X, ALU.add))
            par(nc.vector.reciprocal(lbs[:], lbs[:]))
            lb_v = lb[:].rearrange("p h d -> p d h")
            one_v = one_lb[:].rearrange("p h d -> p d h")
            par(nc.vector.tensor_tensor(lb_v, lbt[:, :, 0], lbs[:], ALU.mult))
            par(nc.vector.tensor_scalar(one_v, lb_v, -1.0, 1.0, ALU.mult, ALU.add))
            par(nc.vector.tensor_scalar(gains[:, G_SUB:G_SUB + 1], gains[:, G_SUB:G_SUB + 1],
                                        1.0 - LAM_INIT, None, ALU.mult))
            assert step[0] == PAR_LB
            for p in range(8):
                if p in (1, 2):
                    norm_lo_of(0, p + 1)
                if p == 3:
                    sum_squares(0)
                split_lo(dve, p + 2, 0, 0)
            with dve.Fori(0, HEADS - 1) as i:
                for q in range(16):
                    if q in MIX_AT:
                        hook(MIX_AT[q], i)
                    split_lo(dve, 8 + q // 2 + 2, 8, i, (q % 2,))
                hook(MIX_AT[16], i)
            for q in range(32):
                if q in LAST_MIX_AT:
                    hook(LAST_MIX_AT[q], HEADS - 1)
                if q in (28, 30):
                    norm_lo_of(1, q // 2 - 14)
                split_lo(dve, OUT_AT + q // 2 + 2, 0, 0, (q % 2,))
                cb, j = OUT_ORDER[q // 2]
                if j == 3 and q % 2:
                    add_block(cb, OUT_AT + q // 2, 0, 0)

            def mlp(at, layer, norm):
                def hidden_lo(n):
                    for b in range(2):
                        dve.wait_ge(hT_hi[layer], n * 2 + (b + 1))
                        nc.vector.tensor_tensor(yT_lo[:, 2 * b:2 * b + 2],
                                                M[b].rearrange("p (a b) -> p a b", a=2),
                                                yT_hi[:, 2 * b:2 * b + 2].bitcast(F32), ALU.subtract
                                                ).then_inc(hT_lo[layer], 1)

                for p in range(4):
                    if p in (1, 2):
                        norm_lo_of(norm, p + 1)
                    if p == 3:
                        sum_squares(norm)
                    split_lo(dve, at + p + 2, 0, 0)
                with dve.Fori(0, FF // 512 - 1) as i:
                    for p in range(8):
                        if p == 2:
                            hidden_lo(i)
                        split_lo(dve, at + 4 + p + 2, 8, i)
                        if p >= 4:
                            add_block(p - 4, at + 4 + p, 8, i)
                hidden_lo(FF // 512 - 1)
                for cb in range(CB):
                    if layer == 0 and cb >= 2:
                        norm_lo_of(2, cb - 2)
                    split_lo(dve, at + MLP_SLOTS - 4 + cb + 2, 0, 0)
                    add_block(cb, at + MLP_SLOTS - 4 + cb, 0, 0)

            mlp(MLP0_AT, 0, 1)

            def make_u(n, *position):
                wait_product(dve, *position)
                dve.wait_ge(pair_read[0], PAIR_MLP0 + 1 if isinstance(n, int) else
                            n * 3 + (PAIR_MLP0 - 1))
                for tt in range(NT):
                    ins = nc.vector.scalar_tensor_tensor(
                        out=cg[:, tt], in0=pair[1][:, tt], scalar=rstd[:, 2, tt:tt + 1],
                        in1=cg[:, tt], op0=ALU.mult, op1=ALU.mult)
                ins.then_inc(pair_read[1], 1)

            def convolve(n):
                def tap(w, q):
                    at = G_CONV + w * KT + q
                    if isinstance(n, int):
                        return gains[:, at + 4 * n:at + 4 * n + 1]
                    return gains[:, bass.ds(n * 4 + at, 1)]

                dve.wait_ge(uT_read, n * 2 + 2)
                for q in range(4):
                    ins = nc.vector.tensor_scalar(cT[:, q], uT[:, q], tap(1, q), None, ALU.mult)
                ins.then_inc(cv_step, 1)
                dve.wait_ge(cv_step, n * CONV_STEPS + 1)
                for q in range(4):
                    ins = nc.vector.scalar_tensor_tensor(
                        out=cT[:, q, 1:T], in0=uT[:, q, 0:T - 1], scalar=tap(0, q),
                        in1=cT[:, q, 1:T], op0=ALU.mult, op1=ALU.add)
                ins.then_inc(cv_step, 1)
                dve.wait_ge(cv_step, n * CONV_STEPS + 2)
                for q in range(4):
                    ins = nc.vector.scalar_tensor_tensor(
                        out=cT[:, q, 0:T - 1], in0=uT[:, q, 1:T], scalar=tap(2, q),
                        in1=cT[:, q, 0:T - 1], op0=ALU.mult, op1=ALU.add)
                ins.then_inc(cv_step, 1)
                dve.wait_ge(cv_step, n * CONV_STEPS + 3)
                for b in range(2):
                    dve.wait_ge(bT_done, n * 2 + (b + 1))
                    ins = nc.vector.tensor_tensor(cT[:, 2 * b:2 * b + 2],
                                                  M[b].rearrange("p (a b) -> p a b", a=2),
                                                  cT[:, 2 * b:2 * b + 2], ALU.mult)
                ins.then_inc(cv_step, 1)

            def conv_lo(n):
                dve.wait_ge(cv_hi, n + 1)
                nc.vector.tensor_tensor(yT_lo[:, 0:4], cT, yT_hi[:, 0:4].bitcast(F32), ALU.subtract
                                        ).then_inc(cv_lo, 1)

            for p in range(12):
                if p in (1, 2):
                    norm_lo_of(2, p + 1)
                if p == 3:
                    sum_squares(2)
                if p == 9:
                    dve.wait_ge(rstd_step, 6)
                    make_u(0, CONV_AT + 7, 0, 0)
                split_lo(dve, CONV_AT + p + 2, 0, 0)
            with dve.Fori(0, CB - 1) as i:
                for p in range(16):
                    if p == 4:
                        convolve(i)
                    if p == 7:
                        conv_lo(i)
                    if p == 8:
                        make_u(i + 1, CONV_AT + 19, 16, i)
                    split_lo(dve, CONV_AT + 12 + p + 2, 16, i)
                    if 8 <= p < 12:
                        add_block(p - 8, CONV_AT + 12 + p, 16, i)
            convolve(CB - 1)
            conv_lo(CB - 1)
            for cb in range(CB):
                if cb >= 2:
                    norm_lo_of(3, cb - 2)
                split_lo(dve, CONV_AT + CONV_SLOTS - 4 + cb + 2, 0, 0)
                add_block(cb, CONV_AT + CONV_SLOTS - 4 + cb, 0, 0)

            mlp(MLP1_AT, 1, 3)

            sum_squares(4)
            dve.wait_ge(rstd_step, 10)
            dve.wait_ge(fin_rows, 16)
            for cb in range(CB):
                cols = slice(cb * 512, (cb + 1) * 512)
                for tt in range(NT):
                    nc.vector.scalar_tensor_tensor(
                        out=h[:, tt, cols], in0=h[:, tt, cols], scalar=rstd[:, 4, tt:tt + 1],
                        in1=raw[:, 0, cb], op0=ALU.mult, op1=ALU.mult).then_inc(fin_ready, 1)


_INS = ["x", "mix_norm_g", "mlp_norm_g", "final_norm_g", "ab_w_in", "ab_w_out", "diff_lambda",
        "diff_subln_g", "hgrn_lb", "hgrn_norm_g", "conv_w_in", "conv_w", "conv_w_out", "mlp_w_up",
        "mlp_w_down"]


def kernel(**inputs):
    import concourse.bacc as _bacc
    from concourse.bass_utils import run_bass_kernel_spmd as _run

    nc = _bacc.Bacc("TRN2", target_bir_lowering=False, num_devices=1)
    arrays, args = {}, []
    for name in _INS:
        a = np.ascontiguousarray(inputs[name])
        arrays[f"in_{name}"] = a
        args.append(nc.dram_tensor(f"in_{name}", a.shape, mybir.dt.from_np(a.dtype),
                                   kind="ExternalInput").ap())
    out = nc.dram_tensor("out_dram", (1, T, D), F32, kind="ExternalOutput").ap()
    build(nc, *args, out)
    r = _run(nc, [arrays], core_ids=[0])
    return r.results[0]["out_dram"]
```

```python
from contextlib import ExitStack

import concourse.bass as bass
import numpy as np
from concourse import mybir

F32 = mybir.dt.float32
F32R = mybir.dt.float32r
U32 = mybir.dt.uint32
ALU = mybir.AluOpType
ACT = mybir.ActivationFunctionType
AX_X = mybir.AxisListType.X

P = 128
T = 256
NT = T // P
D = 2048
KT = D // P
CB = D // 512
FF = 4 * D
HEADS = 8
DA = 64
EPS = 1e-6
LAM_INIT = 0.8 - 0.6 * 1.0
RAW = 4
HALVES = 4
LEVELS = [1, 2, 4, 8, 16, 32, 64, 128]

PROJ_AT = 0
OUT_AT = PROJ_AT + HEADS * 8
FF_BLOCKS = FF // 512
MLP_SLOTS = FF_BLOCKS * 8
MLP0_AT = OUT_AT + 16
CONV_AT = MLP0_AT + MLP_SLOTS
CONV_SLOTS = CB * 16
MLP1_AT = CONV_AT + CONV_SLOTS
TOTAL = MLP1_AT + MLP_SLOTS

PAIR_L0 = HEADS + CB // 2
PAIR_MLP0 = PAIR_L0 + FF_BLOCKS * CB // 2
PAIR_CONV = PAIR_MLP0 + CB * (1 + CB // 2)
PAIR_MLP1 = PAIR_CONV + FF_BLOCKS * CB // 2

CONV_STEPS = 4
CONST_ALL = 11 + 2 * 2 * 7
PAR_LB = 11
ROWS_DMAS = 5

G_MIX, G_MLP, G_CONV, G_HGRN, G_SUB = 0, 32, 64, 112, 120
GAIN_OF = [G_MIX, G_MLP, G_MIX + KT, G_MLP + KT]

OUT_HALVES = [(0, hd) for hd in range(6)] + [(1, hd) for hd in range(6)] + [
    (0, 6), (1, 6), (0, 7), (1, 7)] + [(cb, hd) for cb in (2, 3) for hd in range(HEADS)]

MIX_AT = {1: 1, 3: 2, 7: 3, 11: 4, 14: 5, 16: 6}
LAST_MIX_AT = {1: 1, 3: 2, 6: 3, 10: 4, 11: 5, 13: 6}
COPY_AT = 14


class Steps:

    def __init__(self, sem, names):
        self.sem, self.names = sem, names

    def at(self, name, n):
        return n * len(self.names) + (self.names.index(name) + 1)


def build(nc, x, mix_norm_g, mlp_norm_g, final_norm_g, ab_w_in, ab_w_out, diff_lambda, diff_subln_g,
          hgrn_lb, hgrn_norm_g, conv_w_in, conv_w, conv_w_out, mlp_w_up, mlp_w_down, out):
    with ExitStack() as ctx:
        def sb(name, shape, dt=F32):
            return ctx.enter_context(nc.sbuf_tensor(name, shape, dt))

        def pb(name, shape, dt=F32):
            return ctx.enter_context(nc.psum_tensor(name, shape, dt))

        def sem(name):
            return ctx.enter_context(nc.semaphore(name))

        raw = sb("raw", [P, RAW, 4, 512])
        w_hi = sb("w_hi", [P, HALVES, 2, 512], F32R)
        w_lo = sb("w_lo", [P, HALVES, 2, 512], F32R)
        h = sb("h", [P, NT, D])
        xT_hi = sb("xT_hi", [P, KT, T], F32R)
        xT_lo = sb("xT_lo", [P, KT, T], F32R)
        yT_hi = sb("yT_hi", [P, KT, T], F32R)
        yT_lo = sb("yT_lo", [P, KT, T], F32R)
        ident = sb("ident", [P, P])
        rows_a = sb("rows_a", [P, P])
        rows_b = sb("rows_b", [48, P])
        gains = sb("gains", [P, P])
        lbt = sb("lbt", [P, 2, 3, HEADS])
        lbm = sb("lbm", [P, 2, HEADS])
        lbs = sb("lbs", [P, 2, HEADS])
        lb = sb("lb", [P, HEADS, 2])
        one_lb = sb("one_lb", [P, HEADS, 2])
        lam4 = sb("lam4", [P, 4, DA])
        lam_sum = sb("lam_sum", [P, 2])
        neg_lam = sb("neg_lam", [P, 1])
        sumsq = sb("sumsq", [P, NT, CB])
        meansq = sb("meansq", [P, NT])
        rstd = sb("rstd", [P, 5, NT])
        rstd2 = sb("rstd2", [P, 5, NT])
        minus_half = sb("minus_half", [P, 4])
        minus_one = sb("minus_one", [P, NT])
        mask = sb("mask", [P, 7, P])
        bias = sb("bias", [P, NT, T])
        proj_a = sb("proj_a", [P, NT, 4, P])
        proj_b = sb("proj_b", [P, NT, 4, P])
        qkT = sb("qkT", [P, 2, T])
        hqT = sb("hqT", [P, T])
        gate = sb("gate", [P, 2, T])
        kin = sb("kin", [P, 2, T])
        kin_sum = sb("kin_sum", [P, T])
        silu = sb("silu", [P, NT, P])
        even = sb("even", [P, 2, 512])
        odd = sb("odd", [P, 2, 512])
        lq = sb("lq", [P, 2, 4, T])
        lk = sb("lk", [P, 7, T])
        sm = sb("sm", [P, NT, 2, T])
        aT = sb("aT", [P, NT, T])
        att = sb("att", [P, NT, 2, P])
        on = sb("on", [P, 4, P])
        mx = sb("mx", [P, 4])
        neg_mx = sb("neg_mx", [P, 4])
        rowsum = sb("rowsum", [P, 4])
        rinv = sb("rinv", [P, 4])
        neg_lr = sb("neg_lr", [P, NT])
        osq = sb("osq", [P, 4])
        orstd = sb("orstd", [P, 4])
        act = sm[:, :, :, :].rearrange("p a b c -> p (a b) c")
        junk = lq[:, 0, 0:2].rearrange("p a b -> p (a b)")
        cg = proj_a[:, :, :, :].rearrange("p a b c -> p (a b c)").rearrange(
            "p (a b) -> p a b", b=T)
        cT = lq[:, 1]
        rows2 = bias[:, 0]
        rstd2_wide = bias[:, 1]

        pair = [pb(f"pair{i}", [P, NT, 512]) for i in range(2)]
        m01 = pb("m01", [P, 2, 512])
        m23 = pb("m23", [P, 2, 512])
        M = [m01[:, 0], m01[:, 1], m23[:, 0], m23[:, 1]]

        def chunks(banks):
            return banks[:].rearrange("p a (b t) -> p (a b) t", t=T)

        landed = [sem(f"landed{i}") for i in range(RAW)]
        hi_ready = sem("hi_ready")
        lo_ready = sem("lo_ready")
        w_used = sem("w_used")
        x_in = [sem(f"x_in{i}") for i in range(CB)]
        mix_rows_in, rows_in = sem("mix_rows_in"), sem("rows_in")
        lam_in = sem("lam_in")
        const_pool = sem("const_pool")
        rows_T = sem("rows_T")
        par_dve = sem("par_dve")
        par_act = sem("par_act")
        pair_read = [sem(f"pair_read{i}") for i in range(2)]
        norm_T = [sem(f"norm_T{i}") for i in range(4)]
        norm_hi = [sem(f"norm_hi{i}") for i in range(4)]
        norm_lo = [sem(f"norm_lo{i}") for i in range(4)]
        sq_done = sem("sq_done")
        sq_sum = sem("sq_sum")
        rstd_step = sem("rstd_step")
        up_relu = [sem(f"up_relu{i}") for i in range(2)]
        up_sq = [sem(f"up_sq{i}") for i in range(2)]
        up_hi = [sem(f"up_hi{i}") for i in range(2)]
        up_lo = [sem(f"up_lo{i}") for i in range(2)]
        waited = sem("waited")
        picked = sem("picked")
        r2_wide, r2_T, r2_row = sem("r2_wide"), sem("r2_T"), sem("r2_row")
        u_ready = sem("u_ready")
        cv_step = sem("cv_step")
        cv_hi, cv_lo = sem("cv_hi"), sem("cv_lo")
        fin_added = sem("fin_added")
        fin_rows = sem("fin_rows")
        fin_ready = sem("fin_ready")
        stored = sem("stored")

        mix_pe = Steps(sem("mix_pe"), ["gateT", "qkT", "hqT", "S0", "S1", "diag", "G0", "aT", "G1",
                                       "oAB", "oT"])
        mix_act = Steps(sem("mix_act"), ["sig_hg", "sig_neg", "sig_pos", "qkT", "hqT", "exp_s",
                                         "aT", "osq", "hi_a", "hi_b"])
        mix_dve = Steps(sem("mix_dve"), ["kin", "f", "tree1", "s", "max", "neg_mx"]
                        + [f"Q{d}{m}" for m in LEVELS[:4] for d in "FB"]
                        + ["diag", "r_inv", "neg_lr", "a1", "a", "P0"]
                        + [f"Q{d}{m}" for m in LEVELS[4:] for d in "FB"]
                        + ["P1", "on", "lo"])
        k_steps = [[f"KF{2 * m}", f"C{m}", f"KB{2 * m}"] for m in LEVELS[:7]]
        mix_pool = Steps(sem("mix_pool"), ["silu", "kin_sum", "tree2", "tree4"]
                         + k_steps[0] + k_steps[1] + k_steps[2] + ["tree8"]
                         + k_steps[3][:2] + ["tree16", "tree32", "tree64"] + k_steps[3][2:]
                         + k_steps[4] + k_steps[5] + k_steps[6] + ["bias", "o_ms", "o_rstd"])

        def flat(tile, d, lv):
            at = 512 - (512 >> lv)
            return tile[:, d, at:at + (256 >> lv)]

        def both(tile, lv):
            at = 512 - (512 >> lv)
            return tile[:, :, at:at + (256 >> lv)].rearrange("p d (a b) -> p d a b", b=2)

        def hidden_at(n):
            return 4 if isinstance(n, int) and n == FF_BLOCKS - 1 else 0

        def h_read(n):
            return PAIR_MLP0 + 1 if isinstance(n, int) and n == 0 else n * 3 + (PAIR_MLP0 - 1)

        def conv_at(n):
            return 4 if isinstance(n, int) and n == CB - 1 else 0

        def row(tile, at):
            return tile[:, at] if isinstance(at, int) else tile[:, bass.ds(at, 1), :].rearrange(
                "p a b -> p (a b)")

        def out_gain(g, n):
            if g == 0:
                return gains[:, G_SUB:G_SUB + 1]
            return gains[:, G_HGRN + n:G_HGRN + n + 1] if isinstance(n, int) else \
                gains[:, bass.ds(n + G_HGRN, 1)]

        def lb_col(tile, n, d):
            return tile[:, n, d:d + 1] if isinstance(n, int) else \
                tile[:, bass.ds(n, 1), d:d + 1].rearrange("p a b -> p (a b)")

        ab_in = ab_w_in[0].rearrange("(kt p) (g h n) -> p kt g h n", p=P, g=8, h=HEADS)
        ab_out = ab_w_out[0].rearrange("(g h p) n -> p h g n", g=2, p=P)
        up_src = [mlp_w_up[i].rearrange("(kt p) n -> p kt n", p=P) for i in range(2)]
        down_src = [mlp_w_down[i].rearrange("(kt p) n -> p kt n", p=P) for i in range(2)]
        cin = conv_w_in[0].rearrange("(kt p) n -> p kt n", p=P)
        cout = conv_w_out[0].rearrange("(kt p) n -> p kt n", p=P)

        def count(scale, const, base, step, i):
            if isinstance(i, int):
                return scale * (base + step * i) + const
            return i * (scale * step) + (scale * base + const)

        def stand_alone(eng, n):
            if not isinstance(n, int):
                eng.sem_inc(waited, 1)

        def load(sp, base, step, i, src, pieces=1):
            slot = base % RAW
            if base >= RAW:
                sp.wait_ge(lo_ready, count(2, 2 - 2 * RAW, base, step, i))
            if pieces == 1:
                sp.dma_start(raw[:, slot], src).then_inc(landed[slot], 16)
                return
            for q in range(pieces):
                sp.dma_start(raw[:, slot, q], src(q)).then_inc(landed[slot], 16)

        def landed_at(base, step, i):
            each, before = (64, 0) if base < MLP0_AT else (16, 48 * (MLP0_AT // RAW))
            uses = base // RAW + 1
            return i * (each * step // RAW) + (each * uses + before)

        def split_hi(eng, base, step, i, ks=(0, 1)):
            if base >= TOTAL:
                return
            slot = base % RAW
            if 0 in ks:
                eng.wait_ge(landed[slot], landed_at(base, step, i))
            for k in ks:
                ring = (2 * base + k) % HALVES
                if 2 * base + k >= HALVES:
                    eng.wait_ge(w_used, count(2, k + 1 - HALVES, base, step, i))
                nc.scalar.activation(w_hi[:, ring], raw[:, slot, 2 * k:2 * k + 2], ACT.Copy
                                     ).then_inc(hi_ready, 1)

        def split_lo(eng, base, step, i, ks=(0, 1)):
            if base >= TOTAL:
                return
            slot = base % RAW
            for k in ks:
                ring = (2 * base + k) % HALVES
                eng.wait_ge(hi_ready, count(2, k + 1, base, step, i))
                nc.vector.tensor_tensor(w_lo[:, ring], raw[:, slot, 2 * k:2 * k + 2],
                                        w_hi[:, ring].bitcast(F32), ALU.subtract
                                        ).then_inc(lo_ready, 1)

        def multiply(eng, base, step, i, hi, lo, kt0, dst, first, last, ks=(0, 1)):
            for k in ks:
                ring = (2 * base + k) % HALVES
                eng.wait_ge(lo_ready, count(2, k + 1, base, step, i))
                for q in range(2):
                    kt = kt0 + 2 * k + q
                    begin = first and k == ks[0] and q == 0
                    end = last and k == ks[-1] and q == 1
                    for tt in range(NT):
                        cols = slice(tt * P, (tt + 1) * P)
                        nc.tensor.matmul(dst[:, tt], hi[:, kt, cols], w_hi[:, ring, q],
                                         start=begin, stop=False)
                        nc.tensor.matmul(dst[:, tt], hi[:, kt, cols], w_lo[:, ring, q],
                                         start=False, stop=False)
                        mm = nc.tensor.matmul(dst[:, tt], lo[:, kt, cols], w_hi[:, ring, q],
                                              start=False, stop=end)
                mm.then_inc(w_used, 1)

        def multiply_T(eng, base, step, i, kt0, dst, first, last):
            for k in range(2):
                ring = (2 * base + k) % HALVES
                eng.wait_ge(lo_ready, count(2, k + 1, base, step, i))
                for q in range(2):
                    kt = kt0 + 2 * k + q
                    end = last and k == 1 and q == 1
                    for c in range(4):
                        cols = slice(c * P, (c + 1) * P)
                        begin = first and k == 0 and q == 0 and c % 2 == 0
                        nc.tensor.matmul(dst[:, c], w_hi[:, ring, q, cols], xT_hi[:, kt],
                                         start=begin, stop=False)
                        nc.tensor.matmul(dst[:, c], w_hi[:, ring, q, cols], xT_lo[:, kt],
                                         start=False, stop=False)
                        mm = nc.tensor.matmul(dst[:, c], w_lo[:, ring, q, cols], xT_hi[:, kt],
                                              start=False, stop=end and c % 2 == 1)
                mm.then_inc(w_used, 1)

        def wait_product(eng, base, step, i, k=1):
            eng.wait_ge(w_used, count(2, k + 1, base, step, i))

        block = ctx.enter_context(nc.Block())

        @block.sync
        def _(sp):
            def head_columns(c, j, at):
                return lambda q: ab_in[:, 4 * j + q, 4 * c:4 * c + 4, at, :]

            def parameter_loads():
                for at, n, src in ((G_MLP, 32, mlp_norm_g.rearrange("a (k p) -> (a k) p", p=P)),
                                   (G_CONV, 48, conv_w[0].rearrange("a (k p) -> (a k) p", p=P)),
                                   (G_HGRN, 8, hgrn_norm_g[0].rearrange("(k p) -> k p", p=P)),
                                   (G_SUB, 1, diff_subln_g)):
                    sp.dma_start(rows_a[at:at + n, :], src).then_inc(rows_in, 16)
                sp.dma_start(rows_b[:, :], hgrn_lb.rearrange("a b (k p) -> (a b k) p", p=P)
                             ).then_inc(rows_in, 16)
                sp.dma_start(lam4[:].rearrange("p a b -> p (a b)"),
                             diff_lambda[0].rearrange("(o a) b -> o (a b)", o=1)
                             .broadcast_to([P, 4 * DA])).then_inc(lam_in, 16)

            for p in range(8):
                if p < CB:
                    sp.dma_start(h[:, :, p * 512:(p + 1) * 512],
                                 x[0].rearrange("(t p) n -> p t n", p=P)[:, :, p * 512:(p + 1) * 512]
                                 ).then_inc(x_in[p], 16)
                load(sp, p, 0, 0, head_columns(p // 4, p % 4, 0), 4)
                if p == 1:
                    parameter_loads()
            with sp.Fori(0, HEADS - 1) as i:
                for p in range(8):
                    load(sp, 8 + p, 8, i,
                         lambda q: head_columns(p // 4, p % 4, bass.ds(i + 1, 1))(q)
                         .rearrange("p a b n -> p (a b) n"), 4)
            def out_tile(p, q):
                cb, hd = OUT_HALVES[2 * p + q // 2]
                return ab_out[:, hd, q % 2, cb * 512:(cb + 1) * 512]

            for p in range(len(OUT_HALVES) // 2):
                load(sp, OUT_AT + p, 0, 0, lambda q: out_tile(p, q), 4)

            def mlp(at, layer):
                for j in range(4):
                    load(sp, at + j, 0, 0, up_src[layer][:, 4 * j:4 * j + 4, 0:512])
                with sp.Fori(0, FF_BLOCKS - 1) as i:
                    for j in range(4):
                        load(sp, at + 4 + j, 8, i,
                             up_src[layer][:, 4 * j:4 * j + 4, bass.ds(i * 512 + 512, 512)])
                    for cb in range(CB):
                        load(sp, at + 8 + cb, 8, i,
                             down_src[layer][:, bass.ds(i * 4, 4), cb * 512:(cb + 1) * 512])
                for cb in range(CB):
                    load(sp, at + MLP_SLOTS - 4 + cb, 0, 0,
                         down_src[layer][:, FF // P - 4:FF // P, cb * 512:(cb + 1) * 512])

            mlp(MLP0_AT, 0)
            for u, g in enumerate((1, 2, 0)):
                for j in range(4):
                    load(sp, CONV_AT + 4 * u + j, 0, 0,
                         cin[:, 4 * j:4 * j + 4, g * D:g * D + 512])
            with sp.Fori(0, CB - 2) as i:
                for u, g in ((0, 1), (1, 2)):
                    for j in range(4):
                        load(sp, CONV_AT + 12 + 4 * u + j, 16, i,
                             cin[:, 4 * j:4 * j + 4, bass.ds(i * 512 + (g * D + 512), 512)])
                for cb in range(CB):
                    load(sp, CONV_AT + 20 + cb, 16, i,
                         cout[:, bass.ds(i * 4, 4), cb * 512:(cb + 1) * 512])
                for j in range(4):
                    load(sp, CONV_AT + 24 + j, 16, i,
                         cin[:, 4 * j:4 * j + 4, bass.ds(i * 512 + 512, 512)])
            for u, g in enumerate((1, 2, 0)):
                for j in range(4):
                    load(sp, CONV_AT + CONV_SLOTS - 20 + 4 * u + j, 0, 0,
                         cin[:, 4 * j:4 * j + 4, (g + 1) * D - 512:(g + 1) * D])
            for n in (CB - 2, CB - 1):
                for cb in range(CB):
                    load(sp, CONV_AT + CONV_SLOTS - 4 * (CB - n) + cb, 0, 0,
                         cout[:, 4 * n:4 * n + 4, cb * 512:(cb + 1) * 512])
            mlp(MLP1_AT, 1)
            sp.wait_ge(lo_ready, 2 * (TOTAL - 4) + 2)
            sp.dma_start(raw[:, 0], final_norm_g.rearrange("(a c n) -> a c n", a=1, n=512)
                         .broadcast_to([P, 4, 512])).then_inc(fin_rows, 16)
            for cb in range(CB):
                for tt in range(NT):
                    sp.wait_ge(fin_ready, cb * NT + tt + 1)
                    sp.dma_start(out[0, tt * P:(tt + 1) * P, cb * 512:(cb + 1) * 512],
                                 h[:, tt, cb * 512:(cb + 1) * 512]).then_inc(stored, 16)
            sp.wait_ge(stored, 16 * CB * NT)

        @block.gpsimd
        def _(pool):
            nc.gpsimd.memset(ident[:], 1.0).then_inc(const_pool, 1)
            pool.wait_ge(const_pool, 1)
            nc.gpsimd.affine_select(out=ident[:], in_=ident[:], compare_op=ALU.is_equal, fill=0.0,
                                    base=0, pattern=[[-1, P]], channel_multiplier=1
                                    ).then_inc(const_pool, 1)
            nc.gpsimd.memset(minus_one[:], -1.0)
            nc.gpsimd.memset(minus_half[:], -0.5).then_inc(const_pool, 1)
            nc.gpsimd.iota(sm[:, :, 0, :], pattern=[[P, NT], [-1, T]], base=0, channel_multiplier=1,
                           allow_small_or_imprecise_dtypes=True).then_inc(const_pool, 1)
            pool.wait_ge(const_pool, 4)
            nc.gpsimd.tensor_scalar(sm[:, :, 1, :], sm[:, :, 0, :], 0.0, None, ALU.max
                                    ).then_inc(const_pool, 1)
            nc.gpsimd.tensor_scalar(bias[:], sm[:, :, 0, :], 0.0, None, ALU.min
                                    ).then_inc(const_pool, 1)
            pool.wait_ge(const_pool, 6)
            nc.gpsimd.tensor_tensor(bias[:], bias[:], sm[:, :, 1, :], ALU.subtract
                                    ).then_inc(const_pool, 1)
            pool.wait_ge(const_pool, 7)
            nc.gpsimd.tensor_scalar(bias[:], bias[:], 0.5, None, ALU.mult).then_inc(const_pool, 1)
            nc.gpsimd.memset(even[:], 1.0).then_inc(const_pool, 1)
            nc.gpsimd.memset(odd[:], 1.0).then_inc(const_pool, 1)
            nc.gpsimd.memset(mask[:], 1.0).then_inc(const_pool, 1)
            done = 11
            pool.wait_ge(const_pool, done)

            def rstd_of(n):
                pool.wait_ge(sq_sum, n + 1)
                nc.gpsimd.tensor_scalar(meansq[:], meansq[:], 1.0 / D, EPS, ALU.mult, ALU.add
                                        ).then_inc(rstd_step, 1)
                pool.wait_ge(rstd_step, 2 * n + 1)
                nc.gpsimd.tensor_tensor(rstd[:, n], meansq[:], minus_half[:, 0:NT], ALU.pow)
                nc.gpsimd.tensor_tensor(rstd2[:, n], meansq[:], minus_one[:], ALU.pow
                                        ).then_inc(rstd_step, 1)

            rstd_of(0)
            for d in range(2):
                for lv in range(7):
                    m = LEVELS[lv]
                    part = mask[:, lv].rearrange("p (a b c) -> p a b c", b=2, c=m)[:, :, 1 - d]
                    lo = m * d
                    nc.gpsimd.affine_select(out=part, in_=part, compare_op=ALU.is_ge, fill=0.0,
                                            base=-lo, pattern=[[-2 * m, 64 // m], [0, m]],
                                            channel_multiplier=1).then_inc(const_pool, 1)
                    done += 1
                    pool.wait_ge(const_pool, done)
                    nc.gpsimd.affine_select(out=part, in_=part, compare_op=ALU.is_ge, fill=0.0,
                                            base=lo + m - 1, pattern=[[2 * m, 64 // m], [0, m]],
                                            channel_multiplier=-1).then_inc(const_pool, 1)
                    done += 1

            assert done == CONST_ALL

            def mix(n):
                def mark(ins, name):
                    assert mix_pool.names[marks[0]] == name
                    marks[0] += 1
                    ins.then_inc(mix_pool.sem, 1)

                marks = [0]

                def own(name):
                    pool.wait_ge(mix_pool.sem, mix_pool.at(name, n))

                pool.wait_ge(mix_act.sem, mix_act.at("sig_hg", n))
                mark(nc.gpsimd.tensor_tensor(silu[:], silu[:], proj_b[:, :, 1], ALU.mult), "silu")
                pool.wait_ge(mix_dve.sem, mix_dve.at("kin", n))
                mark(nc.gpsimd.tensor_tensor(kin_sum[:], kin[:, 0], kin[:, 1], ALU.add), "kin_sum")

                def tree(lv):
                    first, second = both(even, lv - 1)[:, :, :, 1], both(odd, lv - 1)[:, :, :, 0]
                    nc.gpsimd.tensor_tensor(both(even, lv)[:, :, :, 1], first[:, :, 0::2],
                                            second[:, :, 0::2], ALU.mult)
                    mark(nc.gpsimd.tensor_tensor(both(odd, lv)[:, :, :, 0], first[:, :, 1::2],
                                                 second[:, :, 1::2], ALU.mult), f"tree{LEVELS[lv]}")

                def k_level(d, lv):
                    m = LEVELS[lv - 1]
                    if d == 1:
                        src = dst = kin[:, 1]
                    else:
                        src, dst = kin[:, 0] if lv == 1 else lk[:, lv - 2], lk[:, lv - 1]
                    factor = flat(odd if d == 0 else even, d, lv - 1)
                    mark(nc.gpsimd.tensor_tensor(
                        dst.rearrange("p (a b) -> p a b", b=m),
                        src.rearrange("p (a b) -> p a b", b=m),
                        factor.unsqueeze(2).broadcast_to([P, T // m, m]), ALU.mult),
                        f"K{'FB'[d]}{LEVELS[lv]}")

                def combine(lv):
                    m = LEVELS[lv]
                    dst = kin[:, 0] if lv == 0 else lk[:, lv - 1]
                    stand_alone(pool, n)
                    mark(nc.gpsimd.tensor_copy(
                        dst.rearrange("p (a b c) -> p a b c", b=2, c=m)[:, :, 1],
                        kin[:, 1].rearrange("p (a b c) -> p a b c", b=2, c=m)[:, :, 1]), f"C{m}")

                pool.wait_ge(mix_dve.sem, mix_dve.at("tree1", n))
                tree(1)
                own("tree2")
                tree(2)
                own("tree4")
                for lv in range(1, 8):
                    m = LEVELS[lv - 1]
                    if lv == 4:
                        tree(3)
                        own("tree8")
                    k_level(0, lv)
                    own(f"KF{2 * m}")
                    combine(lv - 1)
                    if lv == 4:
                        for up in (4, 5, 6):
                            tree(up)
                            own(f"tree{LEVELS[up]}")
                    own(f"C{m}")
                    k_level(1, lv)
                    own(f"KB{2 * m}")
                pool.wait_ge(mix_dve.sem, mix_dve.at("s", n))
                stand_alone(pool, n)
                mark(nc.gpsimd.tensor_scalar(bias[:], bias[:], 0.5, None, ALU.mult), "bias")
                pool.wait_ge(mix_act.sem, mix_act.at("osq", n))
                stand_alone(pool, n)
                mark(nc.gpsimd.tensor_scalar(osq[:], osq[:], 1.0 / P, EPS, ALU.mult, ALU.add),
                     "o_ms")
                own("o_ms")
                mark(nc.gpsimd.tensor_tensor(orstd[:], osq[:], minus_half[:], ALU.pow), "o_rstd")
                assert marks[0] == len(mix_pool.names)

            pool.wait_ge(const_pool, CONST_ALL)
            pool.wait_ge(par_dve, PAR_LB)
            with pool.Fori(0, HEADS - 1) as i:
                mix(i)
            mix(HEADS - 1)
            for n in range(1, 5):
                rstd_of(n)
                if n == 2:
                    pool.wait_ge(r2_row, 1)
                    for b in range(CB):
                        pool.wait_ge(pair_read[1], h_read(b))
                        nc.gpsimd.tensor_tensor(cg, cg, rows2.unsqueeze(1).broadcast_to([P, 4, T]),
                                                ALU.mult).then_inc(u_ready, 1)

        def gain_transpose_pe(n, cb):
            if n == 0:
                nc.tensor.wait_ge(x_in[cb], 16)
            else:
                last = {1: PAIR_L0, 2: PAIR_MLP0, 3: PAIR_CONV}[n]
                nc.tensor.wait_ge(pair_read[cb % 2], last - 1 + cb // 2)
            for b in range(2):
                if cb:
                    nc.tensor.wait_ge(norm_lo[n], 2 * (cb - 1) + b + 1)
                for q in range(2):
                    kt = 4 * cb + 2 * b + q
                    for tt in range(NT):
                        ins = nc.tensor.transpose(M[b][:, q * T + tt * P:q * T + (tt + 1) * P],
                                                  h[:, tt, kt * P:(kt + 1) * P], ident[:])
                ins.then_inc(norm_T[n], 1)

        def before_slot(n, j):
            if n == 0 and j == 0:
                gain_transpose_pe(0, 0)
                gain_transpose_pe(0, 1)
            if j:
                if j < 3:
                    gain_transpose_pe(n, j + 1)
            nc.tensor.wait_ge(norm_lo[n], 2 * j + 2)

        @block.tensor
        def _(pe):
            pe.wait_ge(const_pool, 2)
            pe.wait_ge(mix_rows_in, 16)
            nc.tensor.transpose(M[3][:, 256:288], rows_a[G_MIX:G_MIX + 32, :], ident[0:32, 0:32]
                                ).then_inc(rows_T, 1)

            def transpose_parameters():
                pe.wait_ge(mix_rows_in, 16)
                pe.wait_ge(rows_in, 16 * ROWS_DMAS)
                pe.wait_ge(par_act, 1)
                nc.tensor.transpose(M[3][:, 0:121], rows_a[0:121, :], ident[0:121, 0:121])
                nc.tensor.transpose(M[3][:, 128:176], rows_b[:, :], ident[0:48, 0:48]
                                    ).then_inc(rows_T, 1)

            def head_product(c, j, base, step, i, n, ks=(0, 1)):
                if j == 0 and 0 in ks and not isinstance(n, int):
                    pe.wait_ge(pair_read[c], n)
                multiply(pe, base, step, i, xT_hi, xT_lo, 4 * j, pair[c], j == 0 and 0 in ks,
                         j == 3 and 1 in ks, ks)

            def hook(k, n):
                def mark(ins, name):
                    assert name in mix_pe.names
                    ins.then_inc(mix_pe.sem, 1)

                def levels(group):
                    banks = m23[:].rearrange("p a b -> p (a b)")
                    for g in range(4):
                        lv = 4 * group + g
                        m = LEVELS[lv]
                        if m == 128:
                            for d, keys in enumerate((lk[:, lv - 1], kin[:, 1])):
                                s_at, t_at = (0, P) if d == 0 else (P, 0)
                                ins = nc.tensor.matmul(
                                    banks[:, g * T + d * P:g * T + (d + 1) * P],
                                    keys[:, s_at:s_at + P], lq[:, d, g, t_at:t_at + P],
                                    start=True, stop=True)
                            continue
                        keys = kin[:, 0] if lv == 0 else lk[:, lv - 1]
                        for tile in range(NT):
                            back = lq[:, 1, g, tile * P:(tile + 1) * P]
                            q_both = bass.AP(tensor=back.tensor, offset=back.offset, ap=[
                                back.ap[0], [2 * m, P // (2 * m)], [m - 4 * T, 2], [1, m]])
                            at = g * T + tile * P
                            ins = nc.tensor.matmul(
                                banks[:, at:at + P].rearrange("p (a b c) -> p a b c", b=2, c=m),
                                keys[:, tile * P:(tile + 1) * P], q_both, start=True, stop=True)
                    return ins

                if k == 1:
                    pe.wait_ge(pair_read[0], n + 1)
                    pe.wait_ge(pair_read[1], n + 1)
                    for bank, src, gs, name in ((M[1], proj_b, (2, 3), "gateT"),
                                                (M[0], proj_a, (0, 1), "qkT"),
                                                (M[2], proj_a, (3,), "hqT")):
                        for at, g in enumerate(gs):
                            for tt in range(NT):
                                ins = nc.tensor.transpose(
                                    bank[:, at * T + tt * P:at * T + (tt + 1) * P], src[:, tt, g],
                                    ident[:])
                        mark(ins, name)
                if k == 2:
                    pe.wait_ge(mix_act.sem, mix_act.at("qkT", n))
                    for mp in range(2):
                        part = slice(mp * DA, (mp + 1) * DA)
                        for tt in range(NT):
                            ins = nc.tensor.matmul(M[mp][:, tt * T:(tt + 1) * T],
                                                   qkT[part, 0, tt * P:(tt + 1) * P], qkT[part, 1],
                                                   start=True, stop=True)
                        mark(ins, f"S{mp}")
                if k == 3:
                    pe.wait_ge(mix_dve.sem, mix_dve.at("s", n))
                    pe.wait_ge(mix_act.sem, mix_act.at("hqT", n))
                    pe.wait_ge(mix_pool.sem, mix_pool.at("kin_sum", n))
                    for tile in range(NT):
                        cols = slice(tile * P, (tile + 1) * P)
                        ins = nc.tensor.matmul(M[1][:, cols], kin_sum[:, cols], hqT[:, cols],
                                               start=True, stop=True)
                    mark(ins, "diag")
                    pe.wait_ge(mix_pool.sem, mix_pool.at("C8", n))
                    pe.wait_ge(mix_dve.sem, mix_dve.at("QB8", n))
                    mark(levels(0), "G0")
                if k == 4:
                    pe.wait_ge(mix_dve.sem, mix_dve.at("a", n))
                    for st in range(NT):
                        for tt in range(NT):
                            ins = nc.tensor.transpose(M[0][:, st * T + tt * P:st * T + (tt + 1) * P],
                                                      sm[:, tt, 0, st * P:(st + 1) * P], ident[:])
                    mark(ins, "aT")
                    pe.wait_ge(mix_pool.sem, mix_pool.at("KB128", n))
                    pe.wait_ge(mix_dve.sem, mix_dve.at("QB128", n))
                    mark(levels(1), "G1")
                if k == 5:
                    pe.wait_ge(mix_act.sem, mix_act.at("aT", n))
                    pe.wait_ge(mix_dve.sem, mix_dve.at("P1", n))
                    for g, rhs in enumerate((proj_a[:, :, 2], proj_b[:, :, 0])):
                        for tt in range(NT):
                            for st in range(NT):
                                lhs = (aT[:, st, tt * P:(tt + 1) * P] if g == 0 else
                                       att[:, st, int(st != tt)])
                                ins = nc.tensor.matmul(
                                    M[0][:, (2 * g + tt) * P:(2 * g + tt + 1) * P], lhs, rhs[:, st],
                                    start=st == 0, stop=st == NT - 1)
                    mark(ins, "oAB")
                if k == 6:
                    pe.wait_ge(mix_dve.sem, mix_dve.at("on", n))
                    for g in range(4):
                        ins = nc.tensor.transpose(M[3][:, g * P:(g + 1) * P], on[:, g], ident[:])
                    mark(ins, "oT")

            for c in range(2):
                for j in range(4):
                    if c == 0:
                        before_slot(0, j)
                    if (c, j) == (0, 3):
                        transpose_parameters()
                    head_product(c, j, 4 * c + j, 0, 0, 0)
            pe.wait_ge(par_act, 2)
            with pe.Fori(0, HEADS - 1) as i:
                for q in range(16):
                    if q in MIX_AT:
                        hook(MIX_AT[q], i)
                    p = q // 2
                    head_product(p // 4, p % 4, 8 + p, 8, i, i + 1, (q % 2,))
                hook(MIX_AT[16], i)
            for q, (cb, hd) in enumerate(OUT_HALVES):
                if q in LAST_MIX_AT:
                    hook(LAST_MIX_AT[q], HEADS - 1)
                if q == 0 or hd >= 6 and cb == 0:
                    pe.wait_ge(mix_dve.sem, mix_dve.at("lo", max(hd, 5)))
                if hd == 0:
                    pe.wait_ge(pair_read[cb % 2], HEADS + cb // 2)
                if q in (28, 30):
                    gain_transpose_pe(1, q // 2 - 14)
                multiply(pe, OUT_AT + q // 2, 0, 0, yT_hi, yT_lo, 2 * hd - 2 * (q % 2),
                         pair[cb % 2], hd == 0, hd == HEADS - 1, (q % 2,))

            def mlp(at, layer, norm):
                before = [PAIR_L0, PAIR_CONV][layer]

                def up(p, base, step, i, n):
                    if p == 0 and not (isinstance(n, int) and n == 1):
                        pe.wait_ge(up_relu[layer], n * NT)
                    multiply_T(pe, base, step, i, 4 * p, chunks(m23), p == 0, p == 3)

                def down(cb, base, step, i, n):
                    if cb == 0:
                        pe.wait_ge(up_lo[layer], n * 2 + 2)
                    pe.wait_ge(pair_read[cb % 2], n * 2 + (before + cb // 2))
                    multiply(pe, base, step, i, yT_hi, yT_lo, hidden_at(n), pair[cb % 2], True, True)

                def both_products(i):
                    for p in range(8):
                        if p < 4:
                            up(p, at + 4 + p, 8, i, i + 1)
                        else:
                            down(p - 4, at + 4 + p, 8, i, i)

                pe.wait_ge(pair_read[0], before)
                for p in range(4):
                    before_slot(norm, p)
                    multiply_T(pe, at + p, 0, 0, 4 * p, chunks(pair[0]), p == 0, p == 3)
                both_products(0)
                with pe.Fori(1, FF_BLOCKS - 2) as i:
                    both_products(i)
                both_products(FF_BLOCKS - 2)
                for cb in range(CB):
                    if layer == 0 and cb >= 2:
                        gain_transpose_pe(2, cb - 2)
                    down(cb, at + MLP_SLOTS - 4 + cb, 0, 0, FF_BLOCKS - 1)

            mlp(MLP0_AT, 0, 1)

            def conv_in(which, j, base, step, i, n, first=False):
                if first and which == "c":
                    before_slot(2, j)
                if j == 0:
                    if which == "b":
                        if not first:
                            pe.wait_ge(cv_step, n * CONV_STEPS)
                    else:
                        pe.wait_ge(pair_read["ch".index(which)],
                                   PAIR_MLP0 if first else n * 3 + (PAIR_MLP0 - 2))
                dst = {"c": pair[0], "h": pair[1], "b": m23}[which]
                multiply_T(pe, base, step, i, 4 * j, chunks(dst), j == 0, j == 3)

            def conv_out(cb, base, step, i, n):
                if cb == 0:
                    pe.wait_ge(cv_lo, n + 1)
                more = 0 if isinstance(n, int) and n == CB - 1 else 1
                pe.wait_ge(pair_read[cb % 2], n * 3 + (PAIR_MLP0 + 1 + more + cb // 2))
                multiply(pe, base, step, i, yT_hi, yT_lo, conv_at(n), pair[cb % 2], True, True)

            for u, which in enumerate("chb"):
                for j in range(4):
                    if (which, j) == ("h", 1):
                        pe.wait_ge(r2_wide, 1)
                        pe.wait_ge(norm_lo[2], 8)
                        for tt in range(NT):
                            ins = nc.tensor.transpose(M[0][:, tt * P:(tt + 1) * P],
                                                      rstd2_wide[:, tt * P:(tt + 1) * P], ident[:])
                        ins.then_inc(r2_T, 1)
                    conv_in(which, j, CONV_AT + 4 * u + j, 0, 0, 0, first=True)
            with pe.Fori(0, CB - 2) as i:
                for p in range(16):
                    at = CONV_AT + 12 + p
                    if p < 4:
                        conv_in("c", p, at, 16, i, i + 1)
                    elif p < 8:
                        conv_in("h", p - 4, at, 16, i, i + 1)
                    elif p < 12:
                        conv_out(p - 8, at, 16, i, i)
                    else:
                        conv_in("b", p - 12, at, 16, i, i + 1)
            for p in range(16):
                at = CONV_AT + CONV_SLOTS - 20 + p
                if p < 12:
                    conv_in("chb"[p // 4], p % 4, at, 0, 0, CB - 1)
                else:
                    conv_out(p - 12, at, 0, 0, CB - 2)
            for cb in range(CB):
                if cb >= 2:
                    gain_transpose_pe(3, cb - 2)
                conv_out(cb, CONV_AT + CONV_SLOTS - 4 + cb, 0, 0, CB - 1)

            mlp(MLP1_AT, 1, 3)

        @block.scalar
        def _(eng):
            eng.dma_start(rows_a[G_MIX:G_MIX + 32, :], mix_norm_g.rearrange("a (k p) -> (a k) p", p=P)
                          ).then_inc(mix_rows_in, 16)

            def norm_hi_of(n, cb):
                for b in range(2):
                    eng.wait_ge(norm_T[n], 2 * cb + b + 1)
                    for q in range(2):
                        kt = 4 * cb + 2 * b + q
                        ins = nc.scalar.activation(
                            xT_hi[:, kt], M[b][:, q * T:(q + 1) * T], ACT.Copy,
                            scale=gains[:, GAIN_OF[n] + kt:GAIN_OF[n] + kt + 1])
                    ins.then_inc(norm_hi[n], 1)

            def squares(n, cbs, added=None):
                for cb in cbs:
                    for tt in range(NT):
                        if (cb, tt) != (0, 0) or n:
                            eng.wait_ge(sq_done, (n * CB + cb) * NT + tt)
                        if added is not None:
                            eng.wait_ge(added, tt + 1)
                        ins = nc.scalar.activation(junk, h[:, tt, cb * 512:(cb + 1) * 512],
                                                   ACT.Square, accum_out=sumsq[:, tt, cb:cb + 1])
                        ins.then_inc(sq_done, 1)

            def copy_product(c, n):
                wait_product(eng, PROJ_AT + 4 * c + 3, 8, n)
                for tt in range(NT):
                    ins = nc.scalar.activation([proj_a, proj_b][c][:, tt],
                                               pair[c][:, tt].rearrange("p (g n) -> p g n", g=4),
                                               ACT.Copy, scale=rstd[:, 0, tt:tt + 1])
                ins.then_inc(pair_read[c], 1)

            def hook(k, n):
                def mark(ins, name):
                    assert name in mix_act.names
                    ins.then_inc(mix_act.sem, 1)

                if k == 0:
                    eng.wait_ge(pair_read[1], n + 1)
                    mark(nc.scalar.activation(silu[:], proj_b[:, :, 1], ACT.Sigmoid), "sig_hg")
                if k == 1:
                    eng.wait_ge(mix_pe.sem, mix_pe.at("gateT", n))
                    z = M[1].rearrange("p (a b) -> p a b", a=2)
                    mark(nc.scalar.activation(kin[:], z, ACT.Sigmoid, scale=-1.0), "sig_neg")
                    mark(nc.scalar.activation(gate[:], z, ACT.Sigmoid), "sig_pos")
                    eng.wait_ge(mix_pe.sem, mix_pe.at("qkT", n))
                    mark(nc.scalar.activation(qkT[:], M[0].rearrange("p (a b) -> p a b", a=2),
                                              ACT.Copy), "qkT")
                    eng.wait_ge(mix_pe.sem, mix_pe.at("hqT", n))
                    mark(nc.scalar.activation(hqT[:], M[2][:, 0:T], ACT.Copy), "hqT")
                if k == 2:
                    eng.wait_ge(mix_dve.sem, mix_dve.at("neg_mx", n))
                    for tt in range(NT):
                        for mp in range(2):
                            c = 2 * tt + mp
                            ins = nc.scalar.activation(sm[:, tt, mp], sm[:, tt, mp], ACT.Exp,
                                                       bias=neg_mx[:, c:c + 1],
                                                       accum_out=rowsum[:, c:c + 1])
                    mark(ins, "exp_s")
                if k == 4:
                    eng.wait_ge(mix_pe.sem, mix_pe.at("aT", n))
                    mark(nc.scalar.activation(aT[:], M[0].rearrange("p (a b) -> p a b", a=NT),
                                              ACT.Copy), "aT")
                if k == 5:
                    eng.wait_ge(mix_pe.sem, mix_pe.at("oAB", n))
                    for g in range(4):
                        ins = nc.scalar.activation(on[:, g], M[0][:, g * P:(g + 1) * P], ACT.Square,
                                                   accum_out=osq[:, g:g + 1])
                    mark(ins, "osq")
                if k == 6:
                    eng.wait_ge(mix_pe.sem, mix_pe.at("oT", n))
                    for g, name in enumerate(("hi_a", "hi_b")):
                        mark(nc.scalar.activation(row(yT_hi, n * 2 + g), M[3][:, g * T:(g + 1) * T],
                                                  ACT.Copy, scale=out_gain(g, n)), name)

            eng.wait_ge(rows_T, 1)
            nc.scalar.activation(gains[:, G_MIX:G_MIX + 32], M[3][:, 256:288], ACT.Copy
                                 ).then_inc(par_act, 1)
            eng.wait_ge(par_act, 1)
            norm_hi_of(0, 0)
            for n in range(2):
                split_hi(eng, n, 0, 0)
                if n == 0:
                    norm_hi_of(0, 1)
            for p in range(8):
                if p == 3:
                    eng.wait_ge(rows_T, 2)
                    nc.scalar.activation(gains[:, 32:121], M[3][:, 32:121], ACT.Copy)
                    nc.scalar.activation(lbt[:].rearrange("p a b c -> p (a b c)"),
                                         M[3][:, 128:176], ACT.Copy).then_inc(par_act, 1)
                if p == 4:
                    eng.wait_ge(par_dve, 4)
                    nc.scalar.activation(lbt[:], lbt[:], ACT.Exp).then_inc(par_act, 1)
                    nc.scalar.activation(lam_sum[:], lam_sum[:], ACT.Exp).then_inc(par_act, 1)
                if p in (1, 2):
                    norm_hi_of(0, p + 1)
                    squares(0, (2 * p - 2, 2 * p - 1))
                if p == 5:
                    eng.wait_ge(rstd_step, 2)
                    copy_product(0, 0)
                split_hi(eng, p + 2, 0, 0)
            with eng.Fori(0, HEADS - 1) as i:
                copy_product(1, i)
                hook(0, i)
                for q in range(16):
                    if q in MIX_AT:
                        hook(MIX_AT[q], i)
                    if q == COPY_AT:
                        copy_product(0, i + 1)
                    split_hi(eng, 8 + q // 2 + 2, 8, i, (q % 2,))
                hook(MIX_AT[16], i)
            copy_product(1, HEADS - 1)
            hook(0, HEADS - 1)
            for q in range(len(OUT_HALVES)):
                if q in LAST_MIX_AT:
                    hook(LAST_MIX_AT[q], HEADS - 1)
                if q in (28, 30):
                    norm_hi_of(1, q // 2 - 14)
                split_hi(eng, OUT_AT + q // 2 + 2, 0, 0, (q % 2,))

            def mlp(at, layer, norm):
                def rectify(n, src, *position):
                    wait_product(eng, *position)
                    if not (isinstance(n, int) and n == 0):
                        eng.wait_ge(up_lo[layer], n * 2)
                    for b in range(2):
                        part = slice(2 * b, 2 * b + 2)
                        nc.scalar.activation(act[:, part], chunks(src)[:, part], ACT.Relu
                                             ).then_inc(up_relu[layer], 1)
                    for b in range(2):
                        part = slice(2 * b, 2 * b + 2)
                        eng.wait_ge(up_relu[layer], n * 2 + (b + 1))
                        nc.scalar.activation(act[:, part], act[:, part], ACT.Square
                                             ).then_inc(up_sq[layer], 1)

                def hidden_hi(n):
                    kt = hidden_at(n)
                    if kt == 0:
                        wait_product(eng, at + 3, 8, n)
                    for b in range(2):
                        eng.wait_ge(up_sq[layer], n * 2 + (b + 1))
                        nc.scalar.activation(yT_hi[:, kt + 2 * b:kt + 2 * b + 2],
                                             act[:, 2 * b:2 * b + 2], ACT.Copy
                                             ).then_inc(up_hi[layer], 1)

                def both_products(i):
                    for p in range(8):
                        if p == 1:
                            hidden_hi(i)
                        if p == 4:
                            rectify(i + 1, m23, at + 7, 8, i)
                        if p == 5 and isinstance(i, int) and i == FF_BLOCKS - 2:
                            hidden_hi(i + 1)
                        split_hi(eng, at + 4 + p + 2, 8, i)

                for p in range(4):
                    if p in (1, 2):
                        norm_hi_of(norm, p + 1)
                        squares(norm, (2 * p - 2, 2 * p - 1))
                    split_hi(eng, at + p + 2, 0, 0)
                rectify(0, pair[0], at + 3, 0, 0)
                both_products(0)
                with eng.Fori(1, FF_BLOCKS - 2) as i:
                    both_products(i)
                both_products(FF_BLOCKS - 2)
                for cb in range(CB):
                    if layer == 0 and cb >= 2:
                        norm_hi_of(2, cb - 2)
                    split_hi(eng, at + MLP_SLOTS - 4 + cb + 2, 0, 0)

            mlp(MLP0_AT, 0, 1)

            def copy_c(*position):
                wait_product(eng, *position)
                nc.scalar.activation(cg, chunks(pair[0]), ACT.Copy).then_inc(pair_read[0], 1)

            def conv_hi(n):
                eng.wait_ge(cv_step, n * CONV_STEPS + CONV_STEPS)
                kt = conv_at(n)
                nc.scalar.activation(yT_hi[:, kt:kt + 4], cT, ACT.Copy).then_inc(cv_hi, 1)

            for p in range(12):
                if p in (1, 2):
                    norm_hi_of(2, p + 1)
                    squares(2, (2 * p - 2, 2 * p - 1))
                if p == 4:
                    copy_c(CONV_AT + 3, 0, 0)
                if p == 6:
                    eng.wait_ge(r2_T, 1)
                    nc.scalar.activation(rows2, M[0][:, 0:T], ACT.Copy).then_inc(r2_row, 1)
                split_hi(eng, CONV_AT + p + 2, 0, 0)
            with eng.Fori(0, CB - 2) as i:
                for p in range(16):
                    if p == 1:
                        conv_hi(i)
                    if p == 4:
                        eng.wait_ge(cv_step, i * CONV_STEPS + 3)
                        copy_c(CONV_AT + 15, 16, i)
                    split_hi(eng, CONV_AT + 12 + p + 2, 16, i)
            at = CONV_AT + CONV_SLOTS - 20
            for p in range(16):
                if p == 1:
                    conv_hi(CB - 2)
                if p == 4:
                    eng.wait_ge(cv_step, (CB - 2) * CONV_STEPS + 3)
                    copy_c(at + 3, 0, 0)
                if p == 13:
                    conv_hi(CB - 1)
                split_hi(eng, at + p + 2, 0, 0)
            for cb in range(CB):
                if cb >= 2:
                    norm_hi_of(3, cb - 2)
                split_hi(eng, CONV_AT + CONV_SLOTS - 4 + cb + 2, 0, 0)

            mlp(MLP1_AT, 1, 3)
            for cb in range(CB - 1):
                eng.wait_ge(pair_read[cb % 2], PAIR_MLP1 - 1 + cb // 2)
                squares(4, (cb,))
            squares(4, (CB - 1,), fin_added)

        @block.vector
        def _(dve):
            def norm_lo_of(n, cb):
                for b in range(2):
                    dve.wait_ge(norm_hi[n], 2 * cb + b + 1)
                    for q in range(2):
                        kt = 4 * cb + 2 * b + q
                        ins = nc.vector.scalar_tensor_tensor(
                            out=xT_lo[:, kt], in0=M[b][:, q * T:(q + 1) * T],
                            scalar=gains[:, GAIN_OF[n] + kt:GAIN_OF[n] + kt + 1],
                            in1=xT_hi[:, kt].bitcast(F32), op0=ALU.mult, op1=ALU.subtract)
                    ins.then_inc(norm_lo[n], 1)

            def sum_squares(n):
                dve.wait_ge(sq_done, (n + 1) * NT * CB)
                if n:
                    dve.wait_ge(rstd_step, 2 * n)
                nc.vector.tensor_reduce(meansq[:], sumsq[:], AX_X, ALU.add).then_inc(sq_sum, 1)

            def add_scaled(cb, factor, *position):
                wait_product(dve, *position)
                cols = slice(cb * 512, (cb + 1) * 512)
                for tt in range(NT):
                    ins = nc.vector.scalar_tensor_tensor(
                        out=h[:, tt, cols], in0=pair[cb % 2][:, tt], scalar=factor[:, tt:tt + 1],
                        in1=h[:, tt, cols], op0=ALU.mult, op1=ALU.add)
                    if position[0] == TOTAL - 1:
                        ins.then_inc(fin_added, 1)
                if position[0] < TOTAL - 1:
                    ins.then_inc(pair_read[cb % 2], 1)

            def add_block(cb, *position):
                wait_product(dve, *position)
                cols = slice(cb * 512, (cb + 1) * 512)
                for tt in range(NT):
                    ins = nc.vector.tensor_tensor(h[:, tt, cols], pair[cb % 2][:, tt], h[:, tt, cols],
                                                  ALU.add)
                ins.then_inc(pair_read[cb % 2], 1)

            def hook(k, n):
                def mark(ins, name):
                    assert name in mix_dve.names
                    order.append(name)
                    ins.then_inc(mix_dve.sem, 1)

                def own(name):
                    dve.wait_ge(mix_dve.sem, mix_dve.at(name, n))

                def q_level(d, lv):
                    if lv == 0:
                        mark(nc.vector.tensor_tensor(lq[:, d, 0], hqT[:], gate[:, d], ALU.mult),
                             f"Q{'FB'[d]}1")
                        return
                    m = LEVELS[lv - 1]
                    own(f"Q{'FB'[d]}{m}")
                    factor = flat(even if d == 0 else odd, d, lv - 1)
                    mark(nc.vector.tensor_tensor(
                        lq[:, d, lv % 4].rearrange("p (a b) -> p a b", b=m),
                        lq[:, d, (lv - 1) % 4].rearrange("p (a b) -> p a b", b=m),
                        factor.unsqueeze(2).broadcast_to([P, T // m, m]), ALU.mult),
                        f"Q{'FB'[d]}{2 * m}")

                def pick(group):
                    banks = m23[:].rearrange("p a (t c) -> p (a t) c", c=P)
                    for g in range(4):
                        lv = 4 * group + g
                        part = banks[:, 2 * g:2 * g + 2]
                        if LEVELS[lv] == 128:
                            ins = nc.vector.tensor_copy(att[:, :, 1], part)
                            continue
                        stand_alone(dve, n)
                        ins = nc.vector.copy_predicated(
                            att[:, :, 0], mask[:, lv].bitcast(U32).unsqueeze(1).broadcast_to(
                                [P, NT, P]), part)
                        if lv != 3:
                            ins.then_inc(picked, 1)
                            dve.wait_ge(picked, n * 6 + (3 * group + g + 1))
                    mark(ins, f"P{group}")

                if k == 1:
                    dve.wait_ge(mix_act.sem, mix_act.at("sig_neg", n))
                    for d in range(2):
                        ins = nc.vector.tensor_scalar(kin[:, d], kin[:, d], lb_col(one_lb, n, d),
                                                      None, ALU.mult)
                    mark(ins, "kin")
                    dve.wait_ge(mix_act.sem, mix_act.at("sig_pos", n))
                    for d in range(2):
                        ins = nc.vector.tensor_scalar(gate[:, d], gate[:, d], lb_col(one_lb, n, d),
                                                      lb_col(lb, n, d), ALU.mult, ALU.add)
                    mark(ins, "f")
                    own("f")
                    f_pairs = gate[:, :, :].rearrange("p d (a b) -> p d a b", b=2)
                    nc.vector.tensor_copy(both(even, 0)[:, :, :, 1], f_pairs[:, :, :, 0])
                    mark(nc.vector.tensor_copy(both(odd, 0)[:, :, :, 0], f_pairs[:, :, :, 1]),
                         "tree1")
                if k == 2:
                    for mp in range(2):
                        dve.wait_ge(mix_pe.sem, mix_pe.at(f"S{mp}", n))
                        if mp == 0:
                            dve.wait_ge(mix_pool.sem, mix_pool.at("kin_sum", n))
                        ins = nc.vector.scalar_tensor_tensor(
                            out=sm[:, :, mp], in0=M[mp].rearrange("p (a b) -> p a b", a=2),
                            scalar=DA ** -0.5, in1=bias[:], op0=ALU.mult, op1=ALU.add)
                    mark(ins, "s")
                    own("s")
                    mark(nc.vector.tensor_reduce(mx[:], sm[:].rearrange("p a b c -> p (a b) c"),
                                                 AX_X, ALU.max), "max")
                    own("max")
                    mark(nc.vector.tensor_scalar(neg_mx[:], mx[:], -1.0, None, ALU.mult), "neg_mx")
                    dve.wait_ge(mix_act.sem, mix_act.at("hqT", n))
                    for lv in range(4):
                        if lv > 1:
                            dve.wait_ge(mix_pool.sem, mix_pool.at(f"tree{LEVELS[lv - 1]}", n))
                        for d in range(2):
                            q_level(d, lv)
                if k == 3:
                    dve.wait_ge(const_pool, CONST_ALL)
                    dve.wait_ge(mix_pe.sem, mix_pe.at("diag", n))
                    mark(nc.vector.tensor_copy(att[:, :, 0], M[1][:, 0:T].rearrange(
                        "p (a b) -> p a b", a=NT)), "diag")
                    dve.wait_ge(mix_act.sem, mix_act.at("exp_s", n))
                    mark(nc.vector.reciprocal(rinv[:], rowsum[:]), "r_inv")
                    own("r_inv")
                    mark(nc.vector.tensor_scalar(neg_lr[:], rinv[:].rearrange(
                        "p (a b) -> p a b", b=2)[:, :, 1], neg_lam[:, 0:1], None, ALU.mult), "neg_lr")
                    own("neg_lr")
                    for tt in range(NT):
                        ins = nc.vector.tensor_scalar(sm[:, tt, 1], sm[:, tt, 1], neg_lr[:, tt:tt + 1],
                                                      None, ALU.mult)
                    mark(ins, "a1")
                    own("a1")
                    for tt in range(NT):
                        ins = nc.vector.scalar_tensor_tensor(
                            out=sm[:, tt, 0], in0=sm[:, tt, 0], scalar=rinv[:, 2 * tt:2 * tt + 1],
                            in1=sm[:, tt, 1], op0=ALU.mult, op1=ALU.add)
                    mark(ins, "a")
                    dve.wait_ge(mix_pe.sem, mix_pe.at("G0", n))
                    own("diag")
                    pick(0)
                    for lv in range(4, 8):
                        dve.wait_ge(mix_pool.sem, mix_pool.at(f"tree{LEVELS[lv - 1]}", n))
                        for d in range(2):
                            q_level(d, lv)
                if k == 4:
                    dve.wait_ge(mix_pe.sem, mix_pe.at("G1", n))
                    own("P0")
                    pick(1)
                if k == 5:
                    dve.wait_ge(mix_pool.sem, mix_pool.at("o_rstd", n))
                    for tt in range(NT):
                        nc.vector.tensor_scalar(on[:, tt], M[0][:, tt * P:(tt + 1) * P],
                                                orstd[:, tt:tt + 1], None, ALU.mult)
                    for tt in range(NT):
                        ins = nc.vector.scalar_tensor_tensor(
                            out=on[:, 2 + tt], in0=M[0][:, (2 + tt) * P:(3 + tt) * P],
                            scalar=orstd[:, 2 + tt:3 + tt], in1=silu[:, tt], op0=ALU.mult,
                            op1=ALU.mult)
                    mark(ins, "on")
                if k == 6:
                    dve.wait_ge(mix_act.sem, mix_act.at("hi_b", n))
                    for g in range(2):
                        ins = nc.vector.scalar_tensor_tensor(
                            out=row(yT_lo, n * 2 + g), in0=M[3][:, g * T:(g + 1) * T],
                            scalar=out_gain(g, n), in1=row(yT_hi, n * 2 + g).bitcast(F32),
                            op0=ALU.mult, op1=ALU.subtract)
                    mark(ins, "lo")
                    assert order == mix_dve.names, (order, mix_dve.names)
                    order.clear()

            order = []
            step = [0]

            def par(ins):
                step[0] += 1
                ins.then_inc(par_dve, 1)
                dve.wait_ge(par_dve, step[0])

            def parameters_before_exp():
                dve.wait_ge(lam_in, 16)
                par(nc.vector.tensor_tensor(lam4[:, 0::2], lam4[:, 0::2], lam4[:, 1::2], ALU.mult))
                par(nc.vector.tensor_reduce(lam_sum[:], lam4[:, 0::2], AX_X, ALU.add))
                dve.wait_ge(par_act, 2)
                par(nc.vector.tensor_reduce(lbm[:], lbt[:].rearrange("p a b c -> p a c b"), AX_X, ALU.max))
                par(nc.vector.tensor_tensor(lbt[:], lbt[:], lbm[:].unsqueeze(2).broadcast_to(
                    [P, 2, 3, HEADS]), ALU.subtract))

            def parameters_after_exp():
                dve.wait_ge(par_act, 4)
                par(nc.vector.tensor_tensor(neg_lam[:], lam_sum[:, 1:2], lam_sum[:, 0:1], ALU.subtract))
                par(nc.vector.tensor_scalar(neg_lam[:], neg_lam[:], -LAM_INIT, None, ALU.add))
                par(nc.vector.tensor_reduce(lbs[:], lbt[:].rearrange("p a b c -> p a c b"), AX_X, ALU.add))
                par(nc.vector.reciprocal(lbs[:], lbs[:]))
                lb_v = lb[:].rearrange("p h d -> p d h")
                one_v = one_lb[:].rearrange("p h d -> p d h")
                par(nc.vector.tensor_tensor(lb_v, lbt[:, :, 0], lbs[:], ALU.mult))
                par(nc.vector.tensor_scalar(one_v, lb_v, -1.0, 1.0, ALU.mult, ALU.add))
                par(nc.vector.tensor_scalar(gains[:, G_SUB:G_SUB + 1], gains[:, G_SUB:G_SUB + 1],
                                            1.0 - LAM_INIT, None, ALU.mult))
                assert step[0] == PAR_LB

            norm_lo_of(0, 0)
            for n in range(2):
                split_lo(dve, n, 0, 0)
                if n == 0:
                    norm_lo_of(0, 1)
            for p in range(8):
                if p in (1, 2):
                    norm_lo_of(0, p + 1)
                if p == 3:
                    sum_squares(0)
                    parameters_before_exp()
                if p == 5:
                    parameters_after_exp()
                split_lo(dve, p + 2, 0, 0)
            with dve.Fori(0, HEADS - 1) as i:
                for q in range(16):
                    if q in MIX_AT:
                        hook(MIX_AT[q], i)
                    split_lo(dve, 8 + q // 2 + 2, 8, i, (q % 2,))
                hook(MIX_AT[16], i)
            for q, (cb, hd) in enumerate(OUT_HALVES):
                if q in LAST_MIX_AT:
                    hook(LAST_MIX_AT[q], HEADS - 1)
                if q in (28, 30):
                    norm_lo_of(1, q // 2 - 14)
                split_lo(dve, OUT_AT + q // 2 + 2, 0, 0, (q % 2,))
                if hd == HEADS - 1:
                    add_block(cb, OUT_AT + q // 2, 0, 0, q % 2)

            def mlp(at, layer, norm):
                def hidden_lo(n):
                    kt = hidden_at(n)
                    for b in range(2):
                        dve.wait_ge(up_hi[layer], n * 2 + (b + 1))
                        nc.vector.tensor_tensor(yT_lo[:, kt + 2 * b:kt + 2 * b + 2],
                                                act[:, 2 * b:2 * b + 2],
                                                yT_hi[:, kt + 2 * b:kt + 2 * b + 2].bitcast(F32),
                                                ALU.subtract).then_inc(up_lo[layer], 1)

                def both_products(i):
                    for p in range(8):
                        if p == 2:
                            hidden_lo(i)
                        if p == 6 and isinstance(i, int) and i == FF_BLOCKS - 2:
                            hidden_lo(i + 1)
                        split_lo(dve, at + 4 + p + 2, 8, i)
                        if p >= 4:
                            add_scaled(p - 4, rstd2[:, norm], at + 4 + p, 8, i)

                for p in range(4):
                    if p in (1, 2):
                        norm_lo_of(norm, p + 1)
                    if p == 3:
                        sum_squares(norm)
                    split_lo(dve, at + p + 2, 0, 0)
                dve.wait_ge(rstd_step, 2 * norm + 2)
                both_products(0)
                with dve.Fori(1, FF_BLOCKS - 2) as i:
                    both_products(i)
                both_products(FF_BLOCKS - 2)
                for cb in range(CB):
                    if layer == 0 and cb >= 2:
                        norm_lo_of(2, cb - 2)
                    split_lo(dve, at + MLP_SLOTS - 4 + cb + 2, 0, 0)
                    add_scaled(cb, rstd2[:, norm], at + MLP_SLOTS - 4 + cb, 0, 0)

            mlp(MLP0_AT, 0, 1)

            def make_u(n, *position):
                wait_product(dve, *position)
                dve.wait_ge(pair_read[0], h_read(n))
                nc.vector.tensor_tensor(cg, chunks(pair[1]), cg, ALU.mult
                                        ).then_inc(pair_read[1], 1)

            def convolve(n):
                def tap(w, q):
                    at = G_CONV + w * KT + q
                    if isinstance(n, int):
                        return gains[:, at + 4 * n:at + 4 * n + 1]
                    return gains[:, bass.ds(n * 4 + at, 1)]

                dve.wait_ge(u_ready, n + 1)
                for q in range(4):
                    ins = nc.vector.tensor_scalar(cT[:, q], cg[:, q], tap(1, q), None, ALU.mult)
                ins.then_inc(cv_step, 1)
                dve.wait_ge(cv_step, n * CONV_STEPS + 1)
                for q in range(4):
                    ins = nc.vector.scalar_tensor_tensor(
                        out=cT[:, q, 1:T], in0=cg[:, q, 0:T - 1], scalar=tap(0, q),
                        in1=cT[:, q, 1:T], op0=ALU.mult, op1=ALU.add)
                ins.then_inc(cv_step, 1)
                dve.wait_ge(cv_step, n * CONV_STEPS + 2)
                for q in range(4):
                    ins = nc.vector.scalar_tensor_tensor(
                        out=cT[:, q, 0:T - 1], in0=cg[:, q, 1:T], scalar=tap(2, q),
                        in1=cT[:, q, 0:T - 1], op0=ALU.mult, op1=ALU.add)
                ins.then_inc(cv_step, 1)

            def conv_gate(n, *position):
                wait_product(dve, *position)
                dve.wait_ge(cv_step, n * CONV_STEPS + 3)
                nc.vector.tensor_tensor(cT, chunks(m23), cT, ALU.mult).then_inc(cv_step, 1)

            def conv_lo(n):
                dve.wait_ge(cv_hi, n + 1)
                kt = conv_at(n)
                nc.vector.tensor_tensor(yT_lo[:, kt:kt + 4], cT, yT_hi[:, kt:kt + 4].bitcast(F32),
                                        ALU.subtract).then_inc(cv_lo, 1)

            for p in range(12):
                if p in (1, 2):
                    norm_lo_of(2, p + 1)
                if p == 3:
                    sum_squares(2)
                if p == 4:
                    dve.wait_ge(rstd_step, 6)
                    for tt in range(NT):
                        ins = nc.vector.tensor_copy(rstd2_wide[:, tt * P:(tt + 1) * P],
                                                    rstd2[:, 2, tt:tt + 1].broadcast_to([P, P]))
                    ins.then_inc(r2_wide, 1)
                if p == 8:
                    make_u(0, CONV_AT + 7, 0, 0)
                if p == 11:
                    convolve(0)
                split_lo(dve, CONV_AT + p + 2, 0, 0)
            with dve.Fori(0, CB - 2) as i:
                for p in range(16):
                    if p == 0:
                        conv_gate(i, CONV_AT + 11, 16, i)
                    if p == 2:
                        conv_lo(i)
                    if p == 8:
                        make_u(i + 1, CONV_AT + 19, 16, i)
                    if p == 12:
                        convolve(i + 1)
                    split_lo(dve, CONV_AT + 12 + p + 2, 16, i)
                    if 8 <= p < 12:
                        add_scaled(p - 8, rstd[:, 2], CONV_AT + 12 + p, 16, i)
            at = CONV_AT + CONV_SLOTS - 20
            for p in range(16):
                if p == 0:
                    conv_gate(CB - 2, at - 1, 0, 0)
                if p == 2:
                    conv_lo(CB - 2)
                if p == 8:
                    make_u(CB - 1, at + 7, 0, 0)
                if p == 11:
                    convolve(CB - 1)
                if p == 12:
                    conv_gate(CB - 1, at + 11, 0, 0)
                if p == 14:
                    conv_lo(CB - 1)
                split_lo(dve, at + p + 2, 0, 0)
                if p >= 12:
                    add_scaled(p - 12, rstd[:, 2], at + p, 0, 0)
            for cb in range(CB):
                if cb >= 2:
                    norm_lo_of(3, cb - 2)
                split_lo(dve, CONV_AT + CONV_SLOTS - 4 + cb + 2, 0, 0)
                add_scaled(cb, rstd[:, 2], CONV_AT + CONV_SLOTS - 4 + cb, 0, 0)

            mlp(MLP1_AT, 1, 3)

            sum_squares(4)
            dve.wait_ge(rstd_step, 10)
            dve.wait_ge(fin_rows, 16)
            for cb in range(CB):
                cols = slice(cb * 512, (cb + 1) * 512)
                for tt in range(NT):
                    nc.vector.scalar_tensor_tensor(
                        out=h[:, tt, cols], in0=h[:, tt, cols], scalar=rstd[:, 4, tt:tt + 1],
                        in1=raw[:, 0, cb], op0=ALU.mult, op1=ALU.mult).then_inc(fin_ready, 1)


_INS = ["x", "mix_norm_g", "mlp_norm_g", "final_norm_g", "ab_w_in", "ab_w_out", "diff_lambda",
        "diff_subln_g", "hgrn_lb", "hgrn_norm_g", "conv_w_in", "conv_w", "conv_w_out", "mlp_w_up",
        "mlp_w_down"]


def kernel(**inputs):
    import concourse.bacc as _bacc
    from concourse.bass_utils import run_bass_kernel_spmd as _run

    nc = _bacc.Bacc("TRN2", target_bir_lowering=False, num_devices=1)
    arrays, args = {}, []
    for name in _INS:
        a = np.ascontiguousarray(inputs[name])
        arrays[f"in_{name}"] = a
        args.append(nc.dram_tensor(f"in_{name}", a.shape, mybir.dt.from_np(a.dtype),
                                   kind="ExternalInput").ap())
    out = nc.dram_tensor("out_dram", (1, T, D), F32, kind="ExternalOutput").ap()
    build(nc, *args, out)
    r = _run(nc, [arrays], core_ids=[0])
    return r.results[0]["out_dram"]
```
